# Optimizing a Trainium2 kernel written in Bass

```python
import math
import jax, jax.numpy as jnp
from jax import lax
import numpy as np
import jax
import jax.numpy as jnp

D_MODEL = 1024
BATCH = 1
SEQ = 256
DEPTH = 2

HEAD_DIM = 64
N_SB_HEADS = 8
N_MOBA_HEADS = 8
N_ATT_HEADS = N_SB_HEADS + N_MOBA_HEADS
ATT_W = N_ATT_HEADS * HEAD_DIM
SB_QBLOCK = 128
MOBA_BLOCK = 256
MOBA_TOPK = 3
MOBA_QBLOCK = 32
N_RET_HEADS = 4
RET_DK = D_MODEL // N_RET_HEADS
RET_DV = 2 * RET_DK
RET_QK_W = N_RET_HEADS * RET_DK
RET_V_W = N_RET_HEADS * RET_DV
RET_CHUNK = 128
D_FF = -(-8 * D_MODEL // 768) * 256
ROPE_THETA = 10000.0
NORM_EPS = 1e-6
GN_EPS = 1e-5
NEG = -1e30
N_EVEN = (DEPTH + 1) // 2
N_ODD = DEPTH // 2


def rms_norm(x, g):
    xf = x.astype(jnp.float32)
    y = xf * lax.rsqrt(jnp.mean(xf * xf, axis=-1, keepdims=True) + NORM_EPS)
    return (y * g.astype(jnp.float32)).astype(x.dtype)

def rotary(x, pos):
    d = x.shape[-1]
    inv = ROPE_THETA ** (-jnp.arange(0, d, 2, dtype=jnp.float32) / d)
    ang = pos.astype(jnp.float32)[:, None] * inv[None, :]
    cos, sin = jnp.cos(ang), jnp.sin(ang)
    xf = x.astype(jnp.float32)
    x1, x2 = xf[..., : d // 2], xf[..., d // 2:]
    out = jnp.concatenate([x1 * cos - x2 * sin, x2 * cos + x1 * sin], axis=-1)
    return out.astype(x.dtype)

def ada_mod(c, w, b):
    m = jax.nn.silu(c) @ w + b
    return jnp.split(m[:, None, :], 6, axis=-1)

def modulate(h, shift, scale):
    return h * (1 + scale) + shift

def stick_breaking_attention(q, k, v):
    B, H, S, D = q.shape
    nblk = S // SB_QBLOCK
    kpos = jnp.arange(S)
    scale = D ** -0.5

    def block(i):
        start = i * SB_QBLOCK
        qb = lax.dynamic_slice_in_dim(q, start, SB_QBLOCK, axis=2)
        z = jnp.einsum('bhqd,bhkd->bhqk', qb, k).astype(jnp.float32) * scale
        qpos = start + jnp.arange(SB_QBLOCK)
        strict = kpos[None, :] < qpos[:, None]
        log_1mb = jnp.where(strict, jax.nn.log_sigmoid(-z), 0.0)
        after = lax.cumsum(log_1mb, axis=3, reverse=True) - log_1mb
        a = jnp.where(strict, jnp.exp(jax.nn.log_sigmoid(z) + after), 0.0)
        return jnp.einsum('bhqk,bhkd->bhqd', a.astype(v.dtype), v)

    out = lax.map(block, jnp.arange(nblk))
    return jnp.moveaxis(out, 0, 2).reshape(B, H, S, D)

def moba_attention(q, k, v):
    B, H, S, D = q.shape
    nb = -(-S // MOBA_BLOCK)
    spad = nb * MOBA_BLOCK
    pad = ((0, 0), (0, 0), (0, spad - S), (0, 0))
    kp = jnp.pad(k, pad)
    vp = jnp.pad(v, pad)
    kb = kp.reshape(B, H, nb, MOBA_BLOCK, D)
    vb = vp.reshape(B, H, nb, MOBA_BLOCK, D)
    kmean = jnp.mean(kb.astype(jnp.float32), axis=3).astype(k.dtype)
    kk = min(MOBA_TOPK, nb)
    scale = D ** -0.5
    nqb = S // MOBA_QBLOCK
    bi = jnp.arange(B)[:, None, None, None]
    hi = jnp.arange(H)[None, :, None, None]
    blk_ids = jnp.arange(nb)
    kpos_in = jnp.arange(MOBA_BLOCK)

    def block(i):
        start = i * MOBA_QBLOCK
        qb = lax.dynamic_slice_in_dim(q, start, MOBA_QBLOCK, axis=2)
        qpos = start + jnp.arange(MOBA_QBLOCK)
        own = start // MOBA_BLOCK
        gate = jnp.einsum('bhqd,bhnd->bhqn', qb, kmean).astype(jnp.float32)
        gate = jnp.where(blk_ids < own, gate, NEG)
        _, idx = lax.top_k(gate, kk)
        sel_valid = idx < own
        ksel = kb[bi, hi, idx]
        vsel = vb[bi, hi, idx]
        s_past = jnp.einsum('bhqd,bhqnkd->bhqnk', qb, ksel).astype(jnp.float32) * scale
        s_past = jnp.where(sel_valid[..., None], s_past, NEG)
        s_past = s_past.reshape(B, H, MOBA_QBLOCK, kk * MOBA_BLOCK)
        k_own = lax.dynamic_slice_in_dim(kp, own * MOBA_BLOCK, MOBA_BLOCK, axis=2)
        v_own = lax.dynamic_slice_in_dim(vp, own * MOBA_BLOCK, MOBA_BLOCK, axis=2)
        s_own = jnp.einsum('bhqd,bhkd->bhqk', qb, k_own).astype(jnp.float32) * scale
        kpos_own = own * MOBA_BLOCK + kpos_in
        s_own = jnp.where(kpos_own[None, :] <= qpos[:, None], s_own, NEG)
        p = jax.nn.softmax(jnp.concatenate([s_past, s_own], axis=-1), axis=-1).astype(v.dtype)
        p_past = p[..., : kk * MOBA_BLOCK].reshape(B, H, MOBA_QBLOCK, kk, MOBA_BLOCK)
        p_own = p[..., kk * MOBA_BLOCK:]
        return (jnp.einsum('bhqnk,bhqnkd->bhqd', p_past, vsel)
                + jnp.einsum('bhqk,bhkd->bhqd', p_own, v_own))

    out = lax.map(block, jnp.arange(nqb))
    return jnp.moveaxis(out, 0, 2).reshape(B, H, S, D)

def retention_chunkwise(q, k, v):
    B, H, S, dk = q.shape
    dv = v.shape[-1]
    C = RET_CHUNK
    nc = S // C
    log_g = jnp.log(1.0 - 2.0 ** (-5.0 - jnp.arange(H, dtype=jnp.float32)))
    n = jnp.arange(C, dtype=jnp.float32)
    diff = n[:, None] - n[None, :]
    decay = jnp.where(diff >= 0, jnp.exp(log_g[:, None, None] * jnp.maximum(diff, 0.0)), 0.0)
    xi = jnp.exp(log_g[:, None] * (n + 1.0))
    zeta = jnp.exp(log_g[:, None] * (C - 1.0 - n))
    chunk_decay = jnp.exp(log_g * C)

    def chunks(t):
        return jnp.moveaxis(t.reshape(B, H, nc, C, t.shape[-1]), 2, 0)

    def step(state, inp):
        qi, ki, vi = inp
        inner = jnp.einsum('bhqd,bhkd->bhqk', qi, ki).astype(jnp.float32) * decay
        o = (jnp.einsum('bhqk,bhkv->bhqv', inner, vi.astype(jnp.float32))
             + jnp.einsum('bhqd,bhdv->bhqv', qi.astype(jnp.float32), state) * xi[..., None])
        state = state * chunk_decay[:, None, None] + jnp.einsum(
            'bhkd,bhkv->bhdv', ki.astype(jnp.float32) * zeta[..., None], vi.astype(jnp.float32))
        return state, o

    init = jnp.zeros((B, H, dk, dv), jnp.float32)
    _, out = lax.scan(step, init, (chunks(q), chunks(k), chunks(v)))
    return jnp.moveaxis(out, 0, 2).reshape(B, H, S, dv)

def attn_hybrid_mixer(h, w_qkv, w_o, pos):
    B, S, _ = h.shape
    qkv = (h @ w_qkv).reshape(B, S, 3, N_ATT_HEADS, HEAD_DIM).transpose(2, 0, 3, 1, 4)
    q, k, v = qkv[0], qkv[1], qkv[2]
    sb = stick_breaking_attention(q[:, :N_SB_HEADS], k[:, :N_SB_HEADS], v[:, :N_SB_HEADS])
    qm = rotary(q[:, N_SB_HEADS:], pos)
    km = rotary(k[:, N_SB_HEADS:], pos)
    mb = moba_attention(qm, km, v[:, N_SB_HEADS:])
    o = jnp.concatenate([sb, mb], axis=1).transpose(0, 2, 1, 3).reshape(B, S, ATT_W)
    return o @ w_o

def retention_mixer(h, w_in, gn_gain, w_o, pos):
    B, S, _ = h.shape
    proj = h @ w_in
    q, k, v, g = jnp.split(proj, [RET_QK_W, 2 * RET_QK_W, 2 * RET_QK_W + RET_V_W], axis=-1)

    def heads(t, d):
        return t.reshape(B, S, N_RET_HEADS, d).transpose(0, 2, 1, 3)

    q = rotary(heads(q, RET_DK), pos)
    k = rotary(heads(k, RET_DK), pos) * (RET_DK ** -0.5)
    v = heads(v, RET_DV)
    o = retention_chunkwise(q, k, v)
    mu = jnp.mean(o, axis=-1, keepdims=True)
    var = jnp.mean(jnp.square(o - mu), axis=-1, keepdims=True)
    o = (o - mu) * lax.rsqrt(var + GN_EPS)
    o = o.transpose(0, 2, 1, 3).reshape(B, S, RET_V_W) * gn_gain.astype(jnp.float32)
    return (jax.nn.silu(g) * o.astype(h.dtype)) @ w_o

def swiglu(h, w_gate_up, w_down):
    gt, up = jnp.split(h @ w_gate_up, 2, axis=-1)
    return (jax.nn.silu(gt) * up) @ w_down

def first_inputs(seed: int = 0) -> dict:
    key = jax.random.key(seed)
    ks = jax.random.split(key, 14)
    f32 = jnp.float32

    def nrm(k, shape, fan_in):
        return jax.random.normal(k, shape, f32) * (fan_in ** -0.5)

    return {
        "x": jax.random.normal(ks[0], (BATCH, SEQ, D_MODEL), f32),
        "c": jax.random.normal(ks[1], (BATCH, D_MODEL), f32),
        "ada_w": nrm(ks[2], (DEPTH, D_MODEL, 6 * D_MODEL), D_MODEL),
        "ada_b": 0.02 * jax.random.normal(ks[3], (DEPTH, 6 * D_MODEL), f32),
        "norm_gains": 1.0 + 0.05 * jax.random.normal(ks[4], (DEPTH, 2, D_MODEL), f32),
        "att_w_qkv": nrm(ks[5], (N_EVEN, D_MODEL, 3 * ATT_W), D_MODEL),
        "att_w_o": nrm(ks[6], (N_EVEN, ATT_W, D_MODEL), ATT_W),
        "ret_w_in": nrm(ks[7], (N_ODD, D_MODEL, 2 * RET_QK_W + 2 * RET_V_W), D_MODEL),
        "ret_gn": 1.0 + 0.05 * jax.random.normal(ks[8], (N_ODD, RET_V_W), f32),
        "ret_w_o": nrm(ks[9], (N_ODD, RET_V_W, D_MODEL), RET_V_W),
        "ffn_w_gate_up": nrm(ks[10], (DEPTH, D_MODEL, 2 * D_FF), D_MODEL),
        "ffn_w_down": nrm(ks[11], (DEPTH, D_FF, D_MODEL), D_FF),
        "final_norm": 1.0 + 0.05 * jax.random.normal(ks[12], (D_MODEL,), f32),
    }

def first_block(x, c, ada_w, ada_b, norm_gains, att_w_qkv, att_w_o, ret_w_in, ret_gn,
              ret_w_o, ffn_w_gate_up, ffn_w_down, final_norm):
    S = x.shape[1]
    pos = jnp.arange(S, dtype=jnp.int32)
    for layer in range(DEPTH):
        shift_m, scale_m, gate_m, shift_f, scale_f, gate_f = ada_mod(c, ada_w[layer], ada_b[layer])
        h = modulate(rms_norm(x, norm_gains[layer, 0]), shift_m, scale_m)
        j = layer // 2
        if layer % 2 == 0:
            y = attn_hybrid_mixer(h, att_w_qkv[j], att_w_o[j], pos)
        else:
            y = retention_mixer(h, ret_w_in[j], ret_gn[j], ret_w_o[j], pos)
        x = x + gate_m * y
        h = modulate(rms_norm(x, norm_gains[layer, 1]), shift_f, scale_f)
        x = x + gate_f * swiglu(h, ffn_w_gate_up[layer], ffn_w_down[layer])
    return rms_norm(x, final_norm)


CONV_WIDTH = 512
CONV_GROUPS = 8
CONV_K = 3
MLA_HEADS = 8
MLA_Q_LORA = 256
MLA_KV_LORA = 128
MLA_NOPE = 64
MLA_ROPE = 32
MLA_V = 64
MLA_QK = MLA_NOPE + MLA_ROPE
DIL_PATTERNS = ((128, 1), (512, 4), (2048, 16))
DIL_GROUPS = len(DIL_PATTERNS)
DIL_HEADS = 8
DIL_HEAD_DIM = 64
DIL_WIDTH = DIL_HEADS * DIL_HEAD_DIM
N_BRANCH = 3
Q_BLOCK = 128
EPS = 1e-6

SPLIT_SIZES = ((CONV_WIDTH,) * 4
               + (MLA_Q_LORA, MLA_KV_LORA, MLA_ROPE, MLA_HEADS * MLA_V)
               + (DIL_GROUPS * DIL_WIDTH,) * 3 + (DIL_WIDTH,)
               + (N_BRANCH * D_MODEL,))
SPLIT_POINTS = tuple(int(v) for v in np.cumsum(SPLIT_SIZES)[:-1])
N_IN = int(sum(SPLIT_SIZES))


def rmsnorm(x, g):
    xf = x.astype(jnp.float32)
    y = xf * lax.rsqrt(jnp.mean(xf * xf, axis=-1, keepdims=True) + EPS)
    return (y * g.astype(jnp.float32)).astype(x.dtype)

def rope_tables(S):
    inv = ROPE_THETA ** (-jnp.arange(0, MLA_ROPE, 2, dtype=jnp.float32) / MLA_ROPE)
    ang = jnp.arange(S, dtype=jnp.float32)[:, None] * inv[None, :]
    return jnp.cos(ang), jnp.sin(ang)

def apply_rope(t, cos, sin):
    tf = t.astype(jnp.float32)
    t1, t2 = jnp.split(tf, 2, axis=-1)
    c = cos[None, :, None, :]
    s = sin[None, :, None, :]
    return jnp.concatenate([t1 * c - t2 * s, t2 * c + t1 * s], axis=-1).astype(t.dtype)

def alibi_slopes():
    n = DIL_GROUPS * DIL_HEADS
    m = 2.0 ** (-8.0 * jnp.arange(1, n + 1, dtype=jnp.float32) / n)
    return m.reshape(DIL_GROUPS, DIL_HEADS)

def causal_block_attention(q, k, v, scale):
    B, H, S, Dk = q.shape
    Dv = v.shape[-1]
    nqb = S // Q_BLOCK
    qb = q.reshape(B, H, nqb, Q_BLOCK, Dk).transpose(2, 0, 1, 3, 4)
    kf = k.astype(jnp.float32)
    vf = v.astype(jnp.float32)
    kpos = jnp.arange(S)

    def one_block(args):
        qblk, i = args
        s = jnp.einsum('bhqc,bhkc->bhqk', qblk.astype(jnp.float32), kf) * scale
        qpos = i * Q_BLOCK + jnp.arange(Q_BLOCK)
        s = jnp.where(kpos[None, :] <= qpos[:, None], s, -jnp.inf)
        p = jax.nn.softmax(s, axis=-1)
        return jnp.einsum('bhqk,bhkc->bhqc', p, vf)

    o = lax.map(one_block, (qb, jnp.arange(nqb)))
    return o.transpose(1, 2, 0, 3, 4).reshape(B, H, S, Dv)

def dilated_group_attention(q, k, v, slopes, dilation, n_back):
    B, S, H, hd = q.shape
    L = S // dilation
    nb = -(-L // Q_BLOCK)
    Lp = nb * Q_BLOCK

    def to_sub(t):
        return t.reshape(B, L, dilation, H, hd).transpose(0, 2, 3, 1, 4)

    qs = jnp.pad(to_sub(q).astype(jnp.float32), ((0, 0), (0, 0), (0, 0), (0, Lp - L), (0, 0)))
    qs = qs.reshape(B, dilation, H, nb, Q_BLOCK, hd)

    def windows(t):
        tp = jnp.pad(to_sub(t).astype(jnp.float32), ((0, 0), (0, 0), (0, 0), (Q_BLOCK, Lp - L), (0, 0)))
        tb = tp.reshape(B, dilation, H, nb + 1, Q_BLOCK, hd)
        return jnp.concatenate([tb[:, :, :, :-1], tb[:, :, :, 1:]], axis=4)

    kw = windows(k)
    vw = windows(v)
    qq = jnp.arange(Q_BLOCK)[:, None]
    kk = jnp.arange(2 * Q_BLOCK)[None, :]
    j = Q_BLOCK + qq - kk
    key_idx = (jnp.arange(nb)[:, None, None] - 1) * Q_BLOCK + kk[None]
    valid = (j >= 0) & (j <= n_back) & (key_idx >= 0)
    dist = (dilation * j).astype(jnp.float32)
    bias = -slopes.reshape(1, 1, H, 1, 1, 1) * dist
    scale = DIL_HEAD_DIM ** -0.5
    s = jnp.einsum('bdhnqc,bdhnkc->bdhnqk', qs, kw) * scale + bias
    s = jnp.where(valid, s, -jnp.inf)
    lse = jax.nn.logsumexp(s, axis=-1)
    p = jnp.exp(s - lse[..., None])
    o = jnp.einsum('bdhnqk,bdhnkc->bdhnqc', p, vw)
    o = o.reshape(B, dilation, H, Lp, hd)[:, :, :, :L]
    lse = lse.reshape(B, dilation, H, Lp)[:, :, :, :L]
    o = o.transpose(0, 3, 1, 2, 4).reshape(B, S, H, hd)
    lse = lse.transpose(0, 3, 1, 2).reshape(B, S, H)
    return o, lse

def hybrid_layer(x, norm_g, w_in, b_gate, conv_w, conv_b, q_a_norm_g, w_uq, kv_a_norm_g, w_ukv,
                 mla_q_norm_g, mla_k_norm_g, dil_q_norm_g, dil_k_norm_g,
                 w_out_a, w_out_b, w_out_c, w_o, cos, sin, slopes):
    B, S, _ = x.shape
    h = rmsnorm(x, norm_g)
    proj = h @ w_in
    (a_b, a_c, a_x, a_z, c_q, c_kv, k_pe, b_z, dq, dk, dv, c_z, gate_pre) = jnp.split(proj, SPLIT_POINTS, axis=-1)

    u = a_c * a_x
    up = jnp.pad(u, ((0, 0), (CONV_K - 1, 0), (0, 0)))
    conv = conv_b
    for tap in range(CONV_K):
        conv = conv + up[:, tap:tap + S] * conv_w[tap]
    y_a = a_b * conv * jax.nn.silu(a_z)

    q = (rmsnorm(c_q, q_a_norm_g) @ w_uq).reshape(B, S, MLA_HEADS, MLA_QK)
    kv = (rmsnorm(c_kv, kv_a_norm_g) @ w_ukv).reshape(B, S, MLA_HEADS, MLA_NOPE + MLA_V)
    k_nope, v = jnp.split(kv, [MLA_NOPE], axis=-1)
    k = jnp.concatenate([k_nope, jnp.broadcast_to(k_pe[:, :, None, :], (B, S, MLA_HEADS, MLA_ROPE))], axis=-1)
    q = rmsnorm(q, mla_q_norm_g)
    k = rmsnorm(k, mla_k_norm_g)
    q = jnp.concatenate([q[..., :MLA_NOPE], apply_rope(q[..., MLA_NOPE:], cos, sin)], axis=-1)
    k = jnp.concatenate([k[..., :MLA_NOPE], apply_rope(k[..., MLA_NOPE:], cos, sin)], axis=-1)
    o_b = causal_block_attention(q.transpose(0, 2, 1, 3), k.transpose(0, 2, 1, 3), v.transpose(0, 2, 1, 3),
                                 MLA_QK ** -0.5)
    o_b = o_b.transpose(0, 2, 1, 3).reshape(B, S, MLA_HEADS * MLA_V).astype(x.dtype)
    y_b = o_b * jax.nn.silu(b_z)

    dq = rmsnorm(dq.reshape(B, S, DIL_GROUPS, DIL_HEADS, DIL_HEAD_DIM), dil_q_norm_g[:, None, :])
    dk = rmsnorm(dk.reshape(B, S, DIL_GROUPS, DIL_HEADS, DIL_HEAD_DIM), dil_k_norm_g[:, None, :])
    dv = dv.reshape(B, S, DIL_GROUPS, DIL_HEADS, DIL_HEAD_DIM)
    outs = []
    lses = []
    for gi, (window, dilation) in enumerate(DIL_PATTERNS):
        o_g, lse_g = dilated_group_attention(dq[:, :, gi], dk[:, :, gi], dv[:, :, gi], slopes[gi],
                                             dilation, window // dilation)
        outs.append(o_g)
        lses.append(lse_g)
    alpha = jax.nn.softmax(jnp.stack(lses, axis=0), axis=0)
    o_c = jnp.sum(alpha[..., None] * jnp.stack(outs, axis=0), axis=0)
    o_c = o_c.reshape(B, S, DIL_WIDTH).astype(x.dtype)
    y_c = o_c * jax.nn.silu(c_z)

    g_a, g_b, g_c = jnp.split(jax.nn.sigmoid(gate_pre + b_gate), N_BRANCH, axis=-1)
    merged = g_a * (y_a @ w_out_a) + g_b * (y_b @ w_out_b) + g_c * (y_c @ w_out_c)
    return x + merged @ w_o

def second_inputs(seed: int = 0) -> dict:
    key = jax.random.key(seed)
    ks = jax.random.split(key, 18)
    f32 = jnp.float32

    def nrm(k, shape, scale):
        return jax.random.normal(k, shape, f32) * scale

    def gain(k, shape):
        return 1.0 + 0.02 * jax.random.normal(k, shape, f32)

    Ld = DEPTH
    return {
        'x': jax.random.normal(ks[0], (BATCH, SEQ, D_MODEL), f32),
        'norm_g': gain(ks[1], (Ld, D_MODEL)),
        'w_in': nrm(ks[2], (Ld, D_MODEL, N_IN), D_MODEL ** -0.5),
        'b_gate': nrm(ks[3], (Ld, N_BRANCH * D_MODEL), 0.1),
        'conv_w': nrm(ks[4], (Ld, CONV_K, CONV_WIDTH), CONV_K ** -0.5),
        'conv_b': nrm(ks[5], (Ld, CONV_WIDTH), 0.02),
        'q_a_norm_g': gain(ks[6], (Ld, MLA_Q_LORA)),
        'w_uq': nrm(ks[7], (Ld, MLA_Q_LORA, MLA_HEADS * MLA_QK), MLA_Q_LORA ** -0.5),
        'kv_a_norm_g': gain(ks[8], (Ld, MLA_KV_LORA)),
        'w_ukv': nrm(ks[9], (Ld, MLA_KV_LORA, MLA_HEADS * (MLA_NOPE + MLA_V)), MLA_KV_LORA ** -0.5),
        'mla_q_norm_g': gain(ks[10], (Ld, MLA_QK)),
        'mla_k_norm_g': gain(ks[11], (Ld, MLA_QK)),
        'dil_q_norm_g': gain(ks[12], (Ld, DIL_GROUPS, DIL_HEAD_DIM)),
        'dil_k_norm_g': gain(ks[13], (Ld, DIL_GROUPS, DIL_HEAD_DIM)),
        'w_out_a': nrm(ks[14], (Ld, CONV_WIDTH, D_MODEL), CONV_WIDTH ** -0.5),
        'w_out_b': nrm(ks[15], (Ld, MLA_HEADS * MLA_V, D_MODEL), (MLA_HEADS * MLA_V) ** -0.5),
        'w_out_c': nrm(ks[16], (Ld, DIL_WIDTH, D_MODEL), DIL_WIDTH ** -0.5),
        'w_o': nrm(ks[17], (Ld, D_MODEL, D_MODEL), D_MODEL ** -0.5),
    }

def second_block(x, norm_g, w_in, b_gate, conv_w, conv_b, q_a_norm_g, w_uq, kv_a_norm_g, w_ukv,
              mla_q_norm_g, mla_k_norm_g, dil_q_norm_g, dil_k_norm_g, w_out_a, w_out_b, w_out_c, w_o):
    cos, sin = rope_tables(x.shape[1])
    slopes = alibi_slopes()
    for l in range(DEPTH):
        x = hybrid_layer(x, norm_g[l], w_in[l], b_gate[l], conv_w[l], conv_b[l], q_a_norm_g[l], w_uq[l],
                         kv_a_norm_g[l], w_ukv[l], mla_q_norm_g[l], mla_k_norm_g[l], dil_q_norm_g[l],
                         dil_k_norm_g[l], w_out_a[l], w_out_b[l], w_out_c[l], w_o[l], cos, sin, slopes)
    return x


def setup_inputs(seed=0):
    out = dict(first_inputs(seed))
    for name, value in second_inputs(seed + 1).items():
        if name != "x":
            out[name + "_2"] = value
    return out


def reference(
    x, c, ada_w, ada_b, norm_gains, att_w_qkv, att_w_o, ret_w_in, ret_gn, ret_w_o,
    ffn_w_gate_up, ffn_w_down, final_norm, norm_g_2, w_in_2, b_gate_2, conv_w_2, conv_b_2,
    q_a_norm_g_2, w_uq_2, kv_a_norm_g_2, w_ukv_2, mla_q_norm_g_2, mla_k_norm_g_2,
    dil_q_norm_g_2, dil_k_norm_g_2, w_out_a_2, w_out_b_2, w_out_c_2, w_o_2,
):
    x = first_block(
        x, c, ada_w, ada_b, norm_gains, att_w_qkv, att_w_o, ret_w_in, ret_gn, ret_w_o,
        ffn_w_gate_up, ffn_w_down, final_norm,
    )
    return second_block(
        x, norm_g_2, w_in_2, b_gate_2, conv_w_2, conv_b_2, q_a_norm_g_2, w_uq_2, kv_a_norm_g_2,
        w_ukv_2, mla_q_norm_g_2, mla_k_norm_g_2, dil_q_norm_g_2, dil_k_norm_g_2, w_out_a_2,
        w_out_b_2, w_out_c_2, w_o_2,
    )


_drawn_inputs = setup_inputs


def setup_inputs(seed=0):
    import zlib

    import numpy as np

    out = dict(_drawn_inputs(seed))
    spreads = {}
    factors = {'norm_g_2': 2.719,
     'b_gate_2': 2.784,
     'conv_b_2': 6.39,
     'q_a_norm_g_2': 8.0,
     'kv_a_norm_g_2': 8.0,
     'mla_q_norm_g_2': 8.0,
     'mla_k_norm_g_2': 8.0,
     'dil_q_norm_g_2': 8.0,
     'dil_k_norm_g_2': 8.0}
    for name, (base, spread) in spreads.items():
        noise = np.random.default_rng([zlib.crc32(name.encode()), seed]).standard_normal(out[name].shape)
        drawn = base * np.exp(spread * noise) if base else spread * noise
        out[name] = jnp.asarray(drawn.astype(out[name].dtype))
    for name, factor in factors.items():
        out[name] = (out[name] * factor).astype(out[name].dtype)
    return out
```

```python
from contextlib import ExitStack

import numpy as np

import concourse.bass as bass
from concourse import mybir

D = 1024
T = 256
P = 128
KT = D // P
HD = 64
D_FF = 2816
FT = D_FF // P
EPS = 1e-6
GN_EPS = 1e-5
MASKED = 1e30
LAYERS2 = 2

B_QKV = 0
B_ATT_O = B_QKV + 24
B_FFN0 = B_ATT_O + 8
B_DOWN0 = B_FFN0 + 2 * FT
B_RET = B_DOWN0 + FT
B_RET_O = B_RET + 48
B_FFN1 = B_RET_O + 16
B_DOWN1 = B_FFN1 + 2 * FT
B_HYB = B_DOWN1 + FT
HYB_BLOCKS = 88 + 12 + 8
N_BLOCKS = B_HYB + LAYERS2 * HYB_BLOCKS
G_QKV = 0
G_ATT_O = 24
G_FFN0 = G_ATT_O + 8
G_DOWN0 = G_FFN0 + 2 * FT
G_RET = G_DOWN0 + 8
G_RET_O = G_RET + 48
G_FFN1 = G_RET_O + 8
G_DOWN1 = G_FFN1 + 2 * FT
G_HYB = G_DOWN1 + 8
HYB_TILES = 88 + 24 + 8
assert B_HYB % 4 == 0 and HYB_BLOCKS % 4 == 0 and G_HYB % 4 == 0 and HYB_TILES % 4 == 0

C_G0 = 0
C_FINAL = C_G0 + 32
C_RETGN = C_FINAL + 8
C_ADAB = C_RETGN + 16
C_HYB = C_ADAB + 96
L_NORM = 0
L_BGATE = 8
L_CONVW = L_BGATE + 24
L_CONVB = L_CONVW + 12
L_QA = L_CONVB + 4
L_KVA = L_QA + 2
L_DQ = L_KVA + 1
L_DK = L_DQ + 3
LC = L_DK + 3
N_COLS = C_HYB + LAYERS2 * LC

H_CQ, H_KPE, H_BZ, H_DQ, H_DK, H_DV, H_CZ, H_A = 0, 3, 4, 8, 20, 32, 44, 48
H_MERGE = 64
H_WO = 100
DIL = (1, 4, 16)
N_BACK = (128, 128, 128)
SLOPES = [2.0 ** (-8.0 * (n + 1) / 24) for n in range(24)]
HYB_S = 4 + 4 + 8 + 24
HYB_T = 2 + 1 + 24 + 12 + 8 + 8 + 24
HYB_O = 8
ATT_S = ["m0", "m1", "m2", "z0", "z1", "m3", "m4", "z2", "z3", "m5", "m6", "z4", "z5", "m7", "z6", "z7", "a",
         "c0", "c1", "c2", "c3", "c4", "c5", "c6", "c7"]
L1_S = len(ATT_S)
L1_T = 8 + 8 + 16 + 8
L1_O = 8


BESIDE = [[] for _ in range(18)]
for _n in range(H_MERGE - H_CZ):
    BESIDE[0 if _n < 2 else _n - 1 if _n < 17 else 16].append(H_CZ + _n)


class Ring:

    def __init__(self, slots, base=0):
        self.slots, self.base, self.n = slots, base, 0

    def next(self):
        n = self.n
        self.n += 1
        freed = self.base + (n - self.slots + 1 if n >= self.slots else 0)
        return n % self.slots, freed, self.base + n + 1


class Chain:

    def __init__(self, eng, sem):
        self.eng, self.sem, self.n = eng, sem, 0

    def add(self, ins):
        ins.then_inc(self.sem, 1)
        self.n += 1
        return self.n

    def wait(self, n=None):
        self.eng.wait_ge(self.sem, self.n if n is None else n)

    def link(self, ins):
        self.add(ins)
        self.wait()

    def restart(self):
        self.eng.sem_clear(self.sem)
        self.n = 0


def build(nc, a, out):
    fp32 = mybir.dt.float32
    f32r = mybir.dt.float32r
    ALU = mybir.AluOpType
    ACT = mybir.ActivationFunctionType
    AX = mybir.AxisListType.X
    LNEXP = "natural_log_exp_and_others"

    ctx = ExitStack()
    with ctx:
        def sb(name, shape, dt=fp32, stack=ctx):
            return stack.enter_context(nc.sbuf_tensor(name, shape, dt))

        def sem(name):
            return ctx.enter_context(nc.semaphore(name))

        x = sb("x", [P, KT, T])
        sq = sb("sq", [P, KT, T])
        h = sb("h", [P, KT, 2 * T], f32r)
        raw = sb("raw", [P, 4, 1024])
        whi = sb("whi", [P, 4, 1024], f32r)
        wlo = sb("wlo", [P, 4, 1024], f32r)
        rstd = sb("rstd", [P, T])
        cols = sb("cols", [P, N_COLS])
        lcol = sb("lcol", [P, LC])
        hb = sb("hb", [P, 24])
        nq = sb("nq", [P, 3])
        mod = sb("mod", [P, 96])
        modA = sb("modA", [P, 8])
        silc = sb("silc", [P, 3 * 8])
        ident = sb("ident", [P, P])
        ones = sb("ones", [P, P])
        slopes = sb("slopes", [P, 24])
        mark = sb("mark", [P, HYB_S])
        cmask = sb("cmask", [P, 384])

        G = ctx.enter_context(nc.psum_tensor("G", [P, 2, 512], fp32))
        S = ctx.enter_context(nc.psum_tensor("S", [P, 3, 512], fp32))
        Tp = ctx.enter_context(nc.psum_tensor("Tp", [P, 2, 512], fp32))
        O = ctx.enter_context(nc.psum_tensor("O", [P, 512], fp32))

        first = ExitStack()
        araw = sb("araw", [P, 4, 1024], stack=first)
        acc = sb("acc", [P, 2, 1024], stack=first)
        att = ExitStack()
        sqk = sb("sqk", [P, 8, T], stack=att)
        mqk = sb("mqk", [P, 8, T], stack=att)
        mro = sb("mro", [P, 8, T], stack=att)
        rtmp = sb("rtmp", [P, 2, T], stack=att)
        vT = sb("vT", [P, 4, T], stack=att)
        vtok = sb("vtok", [P, 2, 1024], stack=att)
        zs = sb("zs", [P, 8, 384], stack=att)
        sp = sb("sp", [P, 8, 384], stack=att)
        pr = sb("pr", [P, 2, 384], stack=att)
        pt = sb("pt", [P, 2, 384], stack=att)
        mn = sb("mn", [P, 2, 2], stack=att)
        rs = sb("rs", [P, 2, 2], stack=att)
        ri = sb("ri", [P, 2, 2], stack=att)
        usum = sb("usum", [P, P], stack=att)
        sbm = sb("sbm", [P, 384], stack=att)
        mcos = sb("mcos", [P, T], stack=att)
        msin = sb("msin", [P, T], stack=att)
        oh = sb("oh", [P, KT, 2 * T], f32r, stack=att)
        att.close()
        start = ExitStack()
        adaw = sb("adaw", [P, 16, 1024], stack=start)
        start.close()
        ffn = ExitStack()
        ah = sb("ah", [P, FT, 2 * T], f32r, stack=ffn)
        sg = sb("sg", [P, 2, T], stack=ffn)
        af = sb("af", [P, 2, T], stack=ffn)
        ffn.close()
        ret = ExitStack()
        rqk = sb("rqk", [P, 16, T], stack=ret)
        rv = sb("rv", [P, 2, 2048], stack=ret)
        rvT = sb("rvT", [P, 2, T], stack=ret)
        rg = sb("rg", [P, 16, T], stack=ret)
        rp = sb("rp", [P, 2, 384], stack=ret)
        rcos = sb("rcos", [P, T], stack=ret)
        rsin = sb("rsin", [P, T], stack=ret)
        dec = sb("dec", [P, 4, T], stack=ret)
        rmu = sb("rmu", [P, T], stack=ret)
        yr = sb("yr", [P, 16, 2 * T], f32r, stack=ret)
        ret.close()
        first.close()
        second = ExitStack()
        dist = sb("dist", [P, 3, 384], stack=second)
        bones = sb("bones", [P, P], stack=second)
        lcs = sb("lcs", [P, 2, 2, 16], stack=second)
        rows = sb("rows", [P, LAYERS2, 2, 96], stack=second)
        dqk = sb("dqk", [P, 24, T], stack=second)
        dv = sb("dv", [P, 2, 1536], stack=second)
        qkT = sb("qkT", [96, 8, 2 * T], stack=second)
        vm = sb("vm", [P, 2, 512], stack=second)
        bz = sb("bz", [P, 4, T], stack=second)
        cz = sb("cz", [P, 4, T], stack=second)
        sn = sb("sn", [P, 2, 3, 384], stack=second)
        bias = sb("bias", [P, 2, 384], stack=second)
        pt2 = sb("pt2", [P, 3, 384], stack=second)
        mn2 = sb("mn2", [P, 2, 2, 3], stack=second)
        mj = sb("mj", [P, 2, 2], stack=second)
        rs2 = sb("rs2", [P, 2, 2, 3], stack=second)
        rj = sb("rj", [P, 2, 2], stack=second)
        s32 = sb("s32", [P, 32], stack=second)
        ua = sb("ua", [P, 2 + T], stack=second)
        at = sb("at", [P, 5, T], stack=second)
        over = ExitStack()
        cF = sb("cF", [P, 3, T], stack=over)
        csq = sb("csq", [P, 3, T], stack=over)
        cr = sb("cr", [P, 2, T], stack=over)
        kpT = sb("kpT", [32, T], stack=over)
        kpe = sb("kpe", [P, 2, 32], stack=over)
        qk = sb("qk", [P, 2, 2, 8 * 96], stack=over)
        over.close()
        yh = sb("yh", [P, 12, 2 * T], f32r, stack=second)
        second.close()
        wuq = sn[:, :, :, :].rearrange("p a b c -> p (a b c)")[:, 0:1536].rearrange("p (k n) -> p k n", k=2)
        wkv = pt2[:, :, :].rearrange("p a b -> p (a b)")[:, 0:1024]
        mh_stack = ExitStack()
        _d = [sb("o_dist", [P, 3, 384], stack=mh_stack), sb("o_bones", [P, P], stack=mh_stack),
              sb("o_lcs", [P, 2, 2, 16], stack=mh_stack), sb("o_rows", [P, LAYERS2, 2, 96], stack=mh_stack)]
        mh = sb("mh", [P, KT, 2 * T], f32r, stack=mh_stack)
        th = sb("th", [P, 6, T], stack=mh_stack)
        mg = sb("mg", [P, 2, T], stack=mh_stack)
        mh_stack.close()
        sq2 = ExitStack()
        for n, t in (("o2_dist", [P, 3, 384]), ("o2_bones", [P, P]), ("o2_lcs", [P, 2, 2, 16]),
                     ("o2_rows", [P, LAYERS2, 2, 96]), ("o2_dqk", [P, 24, T]), ("o2_dv", [P, 2, 1536])):
            sb(n, t, stack=sq2)
        qks = sb("qks", [P, 2, 2, 8 * 96], stack=sq2)
        sq2.close()

        w_raw = [sem(f"w_raw{i}") for i in range(4)]
        w_hi, w_lo = sem("w_hi"), sem("w_lo")
        blk_done = sem("blk_done")
        slot_free = [sem(f"slot_free{i}") for i in range(4)]
        sq_ready = sem("sq_ready")
        ss_done = sem("ss_done")
        ln_done = sem("ln_done")
        rstd_ready = sem("rstd_ready")
        t_ready = sem("t_ready")
        hi_ready = sem("hi_ready")
        h_ready = sem("h_ready")
        s_done, s_free = sem("s_done"), sem("s_free")
        t_done, t_free = sem("t_done"), sem("t_free")
        o_done, o_free = sem("o_done"), sem("o_free")
        o_hi = sem("o_hi")
        in_x, in_cols, in_const, in_att = sem("in_x"), sem("in_cols"), sem("in_const"), sem("in_att")
        in_ret, in_hyb, in_small = sem("in_ret"), sem("in_hyb"), sem("in_small")
        ada_raw = [sem(f"ada_raw{i}") for i in range(4)]
        ada_first = [sem(f"ada_first{i}") for i in range(4)]
        ada_acc = sem("ada_acc")
        ada_used = sem("ada_used")
        mod_ready = sem("mod_ready")
        exp_c, silu_c = sem("exp_c"), sem("silu_c")
        rope_ready = sem("rope_ready")
        sb_ln, sb_sp, sb_a = sem("sb_ln"), sem("sb_sp"), sem("sb_a")
        p_ready, pn_ready = sem("p_ready"), sem("pn_ready")
        ah_hi, ah_ready = sem("ah_hi"), sem("ah_ready")
        r_sc, r_pt, r_o, r_of = sem("r_sc"), sem("r_pt"), sem("r_o"), sem("r_of")
        r_c, r_sq, r_norm, r_y, r_hi, r_lo = (sem(n) for n in ("r_c", "r_sq", "r_norm", "r_y", "r_hi", "r_lo"))
        c_ready, cn_ready = sem("c_ready"), sem("cn_ready")
        qk_in, qk_sq, qk_ss, qk_rs, qk_ready = (sem(n) for n in ("qk_in", "qk_sq", "qk_ss", "qk_rs", "qk_ready"))
        d_sq, d_rs, d_norm = sem("d_sq"), sem("d_rs"), sem("d_norm")
        mj_ready = sem("mj_ready")
        bias_ready = sem("bias_ready")
        tanh_ready = sem("tanh_ready")
        a_ready = sem("a_ready")
        y_hi, y_lo = sem("y_hi"), sem("y_lo")
        half_done = sem("half_done")
        m_ready, m_hi, m_lo = sem("m_ready"), sem("m_hi"), sem("m_lo")
        lcol_ready = sem("lcol_ready")
        dve_own, act_own, pool_own = sem("dve_own"), sem("act_own"), sem("pool_own")
        stored = sem("stored")

        def gslot(g):
            return G[:, g % 2, 0:T]

        def taken(g, r4=0):
            return g // 4 + 1 + r4

        block = ctx.enter_context(nc.Block())

        @block.sync
        def _(sp_):
            sp_.dma_start(x[:, :, :], a["x"]).then_inc(in_x, 16)
            for q in range(4):
                sp_.dma_start(adaw[:, 4 * q:4 * q + 4, :],
                              a["ada"][4 * q:4 * q + 4].rearrange("n p c -> p n c")).then_inc(ada_first[q], 16)
            for s in range(4):
                sp_.dma_start(raw[:, s, :], a["w"][s]).then_inc(w_raw[s], 16)
            with sp_.Fori(1, N_BLOCKS // 4) as t:
                for s in range(4):
                    sp_.wait_ge(w_lo, t * 4 - 3 + s)
                    sp_.dma_start(raw[:, s, :], a["w"][t * 4 + s]).then_inc(w_raw[s], 16)
            for s in range(4):
                sp_.wait_ge(slot_free[s], G_HYB // 4 + LAYERS2 * HYB_TILES // 4)
            sp_.dma_start(out, x[:, :, :]).then_inc(stored, 16)
            sp_.wait_ge(stored, 16)

        @block.gpsimd
        def _(pool):
            chain = Chain(pool, pool_own)
            pool.wait_ge(ada_acc, 2)
            for s in range(4):
                pool.dma_start(araw[:, s, :], a["ada"][16 + s]).then_inc(ada_raw[s], 16)

            def times_c(dst, w, k):
                return pool.tensor_tensor(dst, w, silc[:, 16 + k:17 + k].broadcast_to([P, 1024]), ALU.mult)

            def pair(v2, last):
                chain.restart()
                for half in range(2):
                    for k in range(8):
                        n = 8 * half + k
                        s = n % 4
                        pool.wait_ge(ada_raw[s], v2 * 64 - 48 + 16 * (n // 4))
                        if k == 0:
                            pool.wait_ge(mod_ready, v2 * 2 + half - 1)
                            ins = times_c(acc[:, half, :], araw[:, s, :], 0)
                        else:
                            chain.link(times_c(araw[:, s, :], araw[:, s, :], k))
                            ins = pool.tensor_tensor(acc[:, half, :], acc[:, half, :], araw[:, s, :], ALU.add)
                        if k < 7:
                            chain.link(ins)
                        else:
                            ins.then_inc(ada_acc, 1)
                            pool.wait_ge(ada_acc, v2 * 2 + half + 1)
                        if not (last and n >= 12):
                            pool.dma_start(araw[:, s, :], a["ada"][v2 * 16 + (n + 4)]).then_inc(ada_raw[s], 16)

            with pool.Fori(1, 5) as v2:
                pair(v2, False)
            pair(5, True)
            pool.wait_ge(in_hyb, 64)
            with pool.Fori(0, LAYERS2) as l:
                for j in range(24):
                    head, grp = j // 3, j % 3
                    pool.wait_ge(s_free, L1_S + l * HYB_S + (16 + j - 1 if j >= 2 else 0))
                    c = 8 * grp + head
                    pool.tensor_tensor(bias[:, j % 2, :], dist[:, grp, :], slopes[:, c:c + 1].broadcast_to([P, 384]),
                                       ALU.mult).then_inc(bias_ready, 1)

        @block.tensor
        def _(pe):
            def run(b, g, n_out, k_of, moving, b4=0, g4=0, each_k=None, each_out=None, half=None):
                t = 0
                for m in range(n_out):
                    if g + m >= 2:
                        pe.wait_ge(slot_free[(g + m - 2) % 4], taken(g + m - 2) + g4)
                    o = gslot(g + m)
                    for k in range(k_of):
                        c = t % 8
                        slot = (b + t // 8) % 4
                        if c == 0:
                            pe.wait_ge(w_lo, b + t // 8 + 1 + 4 * b4)
                        if each_k is not None and m == 0:
                            each_k(k)
                        mv = moving(m, k)
                        wh, wl = whi[:, slot, c * P:(c + 1) * P], wlo[:, slot, c * P:(c + 1) * P]
                        pe.matmul(o, wh, mv[:, 0:T], start=(k == 0), stop=False)
                        pe.matmul(o, wh, mv[:, T:2 * T], start=False, stop=False)
                        ins = pe.matmul(o, wl, mv[:, 0:T], start=False, stop=(k == k_of - 1))
                        t += 1
                        if t % 8 == 0:
                            ins.then_inc(blk_done, 1)
                        elif half is not None and k == k_of - 1:
                            ins.then_inc(half, 1)
                    if each_out is not None:
                        each_out(m)
                assert t % 8 == 0

            def sum_squares(base, k):
                pe.wait_ge(sq_ready, base + k + 1)
                ins = pe.matmul(S[:, 2, 0:T], ones[:, :], sq[:, k, :], start=(k == 0), stop=(k == KT - 1))
                if k == KT - 1:
                    ins.then_inc(ss_done, 1)

            def summed(n, vectors=()):
                def hook(m):
                    for k in ([m - 2] if 2 <= m < KT - 1 else range(KT - 3, KT) if m == KT - 1 else []):
                        sum_squares(8 * n, k)
                    if vectors and m in (5, 6):
                        ada(vectors[m - 5])
                return hook

            def ada(v, slot=None):
                pe.wait_ge(ada_acc, v + 1)
                if slot is None and v:
                    pe.wait_ge(mod_ready, v)
                for m in range(8):
                    ins = pe.matmul(S[:, slot or 0, m:m + 1], acc[:, v % 2, m * P:(m + 1) * P], ones[:, 0:1],
                                    start=True, stop=True)
                ins.then_inc(ada_used if slot is None else s_done, 1)

            def h_of(base):
                return lambda k: pe.wait_ge(h_ready, base + k + 1)

            def of_h(m, k):
                return h[:, k, :]

            s_ring, t_ring, o_ring = Ring(3), Ring(2), Ring(1)

            def use_s():
                slot, freed, _ = s_ring.next()
                if not (isinstance(freed, int) and freed == 0):
                    pe.wait_ge(s_free, freed)
                return slot

            def use_t():
                slot, freed, _ = t_ring.next()
                if not (isinstance(freed, int) and freed == 0):
                    pe.wait_ge(t_free, freed)
                return slot

            def pv_head(odd, parts, ready):
                if not odd:
                    _, freed, _ = o_ring.next()
                    if not (isinstance(freed, int) and freed == 0):
                        pe.wait_ge(o_free, freed)
                pe.wait_ge(*ready)
                o = 64 * odd
                for n, (v0, v1, p_) in enumerate(parts):
                    pe.matmul(O[o:o + 64, 0:T], v0, p_[:, 0:T], start=(n == 0), stop=False)
                    ins = pe.matmul(O[o:o + 64, P:T], v1, p_[:, T:384], start=False,
                                    stop=(n == len(parts) - 1))
                if odd:
                    ins.then_inc(o_done, 1)

            def transposes_v(src):
                slot = use_t()
                for j in range(2):
                    ins = pe.transpose(Tp[:, slot, j * P:(j + 1) * P], src[:, j * P:(j + 1) * P], ident[:, :])
                ins.then_inc(t_done, 1)

            def transposes_p(src):
                slot = use_t()
                for j in range(3):
                    ins = pe.transpose(Tp[:, slot, j * P:(j + 1) * P], src[:, j * P:(j + 1) * P], ident[:, :])
                ins.then_inc(t_done, 1)

            pe.wait_ge(in_const, 64)
            for k in range(KT):
                sum_squares(0, k)
            ada(0)
            ada(1)

            def sb_scores(hh):
                g = 13 + 2 * (hh // 2)
                pe.wait_ge(slot_free[g % 4], taken(g))
                slot = use_s()
                t, o = hh // 2, 64 * (hh % 2)
                kk, qq = sqk[o:o + 64, 4 + t, :], sqk[o:o + 64, t, :]
                pe.matmul(S[:, slot, 0:T], kk[:, 0:P], qq, start=True, stop=True)
                pe.matmul(S[:, slot, T:384], kk[:, P:T], qq[:, P:T], start=True, stop=True).then_inc(s_done, 1)

            def sb_sums(hh):
                slot = use_s()
                pe.wait_ge(sb_sp, hh // 4 + 1)
                pe.matmul(S[:, slot, T:384], usum[:, :], sp[:, hh, T:384], start=True, stop=True)
                pe.matmul(S[:, slot, 0:T], usum[:, :], sp[:, hh, 0:T], start=True, stop=False)
                pe.matmul(S[:, slot, P:T], ones[:, :], sp[:, hh, T:384], start=False, stop=True).then_inc(s_done, 1)

            def v_of_att(t):
                g = 8 + t if t < 4 else 16 + t
                pe.wait_ge(slot_free[g % 4], taken(g))
                transposes_v(vT[:, t % 4, :])

            def sb_pair(p):
                pe.wait_ge(t_free, 12 + p + 1)
                for hh in (2 * p, 2 * p + 1):
                    c = 64 * hh
                    pv_head(hh % 2, [(vtok[:, 0, c:c + 64], vtok[:, 1, c:c + 64], zs[:, hh, :])], (sb_a, hh + 1))

            def moba_scores(i):
                slot = use_s()
                g, o = i // 4, 32 * (i % 4)
                q = [mro[o:o + 32, 2 * half + g, :] for half in range(2)]
                kk = [mro[o:o + 32, 4 + 2 * half + g, :] for half in range(2)]
                for half in range(2):
                    pe.matmul(S[:, slot, 0:P], q[half][:, 0:P], kk[half][:, 0:P], start=(half == 0), stop=(half == 1))
                for half in range(2):
                    ins = pe.matmul(S[:, slot, P:384], q[half][:, P:T], kk[half], start=(half == 0), stop=(half == 1))
                ins.then_inc(s_done, 1)

            for b in range(24):
                i = b - 12
                if i == 0:
                    pe.wait_ge(rope_ready, 2)
                if 0 <= i < 8:
                    moba_scores(i)
                if 1 <= i <= 8:
                    pe.wait_ge(pn_ready, i)
                    transposes_p(pr[:, (i - 1) % 2, :])
                run(B_QKV + b, G_QKV + b, 1, 8, of_h, each_k=h_of(0) if b == 0 else None)
                if 1 <= i <= 8:
                    j, col = i - 1, 512 + 64 * (i - 1)
                    pv_head(j % 2, [(vtok[:, 0, col:col + 64], vtok[:, 1, col:col + 64], pt[:, j % 2, :])],
                            (t_free, 4 + j + 1))
                if 9 <= b <= 12:
                    v_of_att(b - 9)
                if 21 <= b:
                    v_of_att(b - 17)
                if b in (14, 16, 18, 20):
                    sb_scores(b - 14)
                    sb_scores(b - 13)
                if b == 14:
                    pe.wait_ge(in_att, 64)
                if b == 20:
                    ada(2, use_s())
                if b == 23:
                    sb_pair(0)
                if b in (21, 23):
                    for hh in range(2 * b - 42, 2 * b - 38):
                        sb_sums(hh)
            v_of_att(7)
            for p in range(1, 4):
                sb_pair(p)

            pe.wait_ge(o_free, 8)
            run(B_ATT_O, G_ATT_O, 8, 8, lambda m, k: oh[:, k, :], each_out=summed(1, (3, 4)))

            def ffn(b, g, n):
                with pe.Fori(0, FT // 2) as i:
                    run(b, g, 4, 8, of_h, b4=i, g4=i, each_k=h_of(8 * n))

            def down(b, g, f, n, vectors=()):
                pe.wait_ge(ah_ready, FT * (f + 1))
                run(b, g, 8, FT, lambda m, k: ah[:, k, :], each_out=summed(n, vectors))

            ffn(B_FFN0, G_FFN0, 1)
            ada(5)
            down(B_DOWN0, G_DOWN0, 0, 2, (6, 7))

            def ret_scores(hh):
                if hh == 0:
                    pe.wait_ge(rope_ready, 4)
                else:
                    pe.wait_ge(r_pt, hh)
                for o, r in ((0, slice(0, T)), (T, slice(P, T))):
                    for half in range(2):
                        kk = rqk[:, 8 + 2 * hh + half, P if o else 0:T if o else P]
                        q = rqk[:, 2 * hh + half, r]
                        ins = pe.matmul(S[:, 0, o:o + r.stop - r.start], kk, q, start=(half == 0), stop=(half == 1))
                ins.then_inc(r_sc, 1)

            def ret_out(hh):
                pe.wait_ge(r_pt, hh + 1)
                if hh == 0:
                    pe.wait_ge(t_free, 32)
                else:
                    pe.wait_ge(r_of, hh)
                for m in range(4):
                    o = S[:, 1 + m // 2, (m % 2) * T:(m % 2 + 1) * T]
                    c = 512 * hh + P * m
                    pe.matmul(o, rv[:, 0, c:c + P], rp[:, hh % 2, 0:T], start=True, stop=False)
                    ins = pe.matmul(o[:, P:T], rv[:, 1, c:c + P], rp[:, hh % 2, T:384], start=False, stop=True)
                ins.then_inc(r_o, 1)

            def ret_sum(src, sem_, n):
                slot = use_t()
                pe.wait_ge(sem_, n)
                for m in range(4):
                    ins = pe.matmul(Tp[:, slot, 0:T], ones[:, :], sq[:, src + m, :], start=(m == 0), stop=(m == 3))
                ins.then_inc(t_done, 1)

            for b in range(48):
                run(B_RET + b, G_RET + b, 1, 8, of_h, each_k=h_of(16) if b == 0 else None)
                if 17 <= b < 33:
                    g = G_RET + b - 1
                    pe.wait_ge(slot_free[g % 4], taken(g))
                    transposes_v(rvT[:, (b - 17) % 2, :])
                if b >= 33:
                    hh, part = (b - 33) // 4, (b - 33) % 4
                    if part == 0:
                        ret_scores(hh)
                    elif part == 1:
                        ret_out(hh)
                    elif part == 2:
                        ret_sum(0, r_of, hh + 1)
                    else:
                        ret_sum(4, r_sq, hh + 1)
            ret_sum(4, r_sq, 4)
            ada(8)
            run(B_RET_O, G_RET_O, 8, 16, lambda m, k: yr[:, k, :],
                each_k=lambda k: pe.wait_ge(r_lo, k // 4 + 1), each_out=summed(3, (9, 10)))
            ffn(B_FFN1, G_FFN1, 3)
            ada(11)
            down(B_DOWN1, G_DOWN1, 1, 4)

            pe.wait_ge(in_hyb, 64)
            with pe.Fori(0, LAYERS2) as l:
                b4, g4 = l * (HYB_BLOCKS // 4), l * (HYB_TILES // 4)
                s_ring = Ring(3, L1_S + l * HYB_S)
                t_ring = Ring(2, L1_T + l * HYB_T)
                o_ring = Ring(1, L1_O + l * HYB_O)
                t_base = L1_T + l * HYB_T

                def use_s():
                    slot, freed, _ = s_ring.next()
                    pe.wait_ge(s_free, freed)
                    return slot

                def use_t():
                    slot, freed, _ = t_ring.next()
                    pe.wait_ge(t_free, freed)
                    return slot

                def pv_head2(odd, parts, ready):
                    if not odd:
                        _, freed, _ = o_ring.next()
                        pe.wait_ge(o_free, freed)
                    pe.wait_ge(*ready)
                    o = 64 * odd
                    for n, (v0, v1, p_) in enumerate(parts):
                        pe.matmul(O[o:o + 64, 0:T], v0, p_[:, 0:T], start=(n == 0), stop=False)
                        ins = pe.matmul(O[o:o + 64, P:T], v1, p_[:, T:384], start=False,
                                        stop=(n == len(parts) - 1))
                    if odd:
                        ins.then_inc(o_done, 1)

                def transposes2(src, n):
                    slot = use_t()
                    for j in range(n):
                        ins = pe.transpose(Tp[:, slot, j * P:(j + 1) * P], src[:, j * P:(j + 1) * P], ident[:, :])
                    ins.then_inc(t_done, 1)

                def block1(j, each_k=None):
                    run(B_HYB + j, G_HYB + j, 1, 8, of_h, b4=b4, g4=g4, each_k=each_k)

                for k in range(KT):
                    sum_squares(40 + l * 8, k)
                for j in range(4):
                    block1(j, h_of(32 + l * 8) if j == 0 else None)
                for tiles in ((0, 1), (2,)):
                    slot = use_t()
                    j = tiles[-1]
                    pe.wait_ge(slot_free[(G_HYB + j) % 4], taken(G_HYB + j) + g4)
                    for k in tiles:
                        ins = pe.matmul(Tp[:, slot, 0:T], ones[:, :], csq[:, k, :], start=(k == tiles[0]),
                                        stop=(k == tiles[-1]))
                    ins.then_inc(t_done, 1)
                slot = use_t()
                pe.wait_ge(slot_free[(G_HYB + 3) % 4], taken(G_HYB + 3) + g4)
                for j in range(2):
                    ins = pe.matmul(Tp[:, slot, 32 * j:32 * j + 32], kpT[:, j * P:(j + 1) * P], ident[0:32, 0:32],
                                    start=True, stop=True)
                ins.then_inc(t_done, 1)
                for j in range(4, 8):
                    block1(j)

                def mla_projections():
                    pe.wait_ge(cn_ready, l + 1)
                    pe.wait_ge(in_small, l * 32 + 32)
                    for tt in range(2):
                        for half in range(2):
                            slot = use_s()
                            for k in range(2):
                                ins = pe.matmul(S[:, slot, 0:384], cF[:, k, tt * P:(tt + 1) * P],
                                                wuq[:, k, 384 * half:384 * half + 384], start=(k == 0), stop=(k == 1))
                            ins.then_inc(s_done, 1)
                    for half in range(2):
                        for tt in range(2):
                            slot = use_s()
                            pe.matmul(S[:, slot, :], cF[:, 2, tt * P:(tt + 1) * P], wkv[:, 512 * half:512 * half + 512],
                                      start=True, stop=True).then_inc(s_done, 1)

                def mla_transposes(hh):
                    slot = use_t()
                    pe.wait_ge(qk_ready, l + 1)
                    for n in range(2):
                        for tt in range(2):
                            ins = pe.transpose(Tp[0:96, slot, (2 * n + tt) * P:(2 * n + tt + 1) * P],
                                               qk[:, n, tt, 96 * hh:96 * hh + 96], ident[:, :])
                    ins.then_inc(t_done, 1)

                def d_sums(j):
                    slot = use_t()
                    pe.wait_ge(d_sq, l * 24 + j + 1)
                    pe.matmul(Tp[:, slot, 0:T], bones[:, :], sq[:, j % 8, :], start=True, stop=True).then_inc(t_done, 1)

                for j in range(24):
                    block1(H_DQ + j)
                    if j >= 1:
                        d_sums(j - 1)
                    if j == 2:
                        mla_projections()
                    if j >= 20:
                        mla_transposes(2 * (j - 20))
                        mla_transposes(2 * (j - 20) + 1)
                for j in range(12):
                    block1(H_DV + j)
                    if j == 0:
                        d_sums(23)
                    else:
                        g = G_HYB + H_DV + j - 1
                        pe.wait_ge(slot_free[g % 4], taken(g) + g4)
                        transposes2(at[:, (j - 1) % 4, :], 2)

                def scores2(i):
                    if i < 8:
                        slot = use_s()
                        q, kk = qkT[:, i, 0:T], qkT[:, i, T:2 * T]
                        pe.matmul(S[:, slot, 0:P], q[:, 0:P], kk[:, 0:P], start=True, stop=True)
                        pe.matmul(S[:, slot, P:384], q[:, P:T], kk, start=True, stop=True).then_inc(s_done, 1)
                        return
                    hh = i - 8
                    o = 64 * (hh % 2)
                    for grp in range(3):
                        slot = use_s()
                        q, kk = dqk[o:o + 64, 4 * grp + hh // 2, :], dqk[o:o + 64, 12 + 4 * grp + hh // 2, :]
                        pe.matmul(S[:, slot, 0:P], q[:, 0:P], kk[:, 0:P], start=True, stop=True)
                        pe.matmul(S[:, slot, P:384], q[:, P:T], kk, start=True, stop=True).then_inc(s_done, 1)

                def out2(i):
                    if i < 8:
                        parts = [(vm[:, 0, 64 * i:64 * i + 64], vm[:, 1, 64 * i:64 * i + 64], pt2[:, 0, :])]
                        n = i + 1
                    else:
                        cs = [512 * grp + 64 * (i - 8) for grp in range(3)]
                        parts = [(dv[:, 0, c:c + 64], dv[:, 1, c:c + 64], pt2[:, grp, :]) for grp, c in enumerate(cs)]
                        n = 8 + 3 * (i - 7)
                    pv_head2(i % 2, parts, (t_free, t_base + (HYB_T - 32 + n)))

                for i in range(17):
                    if i == 0:
                        g = G_HYB + H_CZ - 1
                        pe.wait_ge(slot_free[g % 4], taken(g) + g4)
                        transposes2(at[:, 3, :], 2)
                        pe.wait_ge(t_free, t_base + (HYB_T - 32))
                        pe.wait_ge(d_norm, l * 24 + 24)
                    if i < 16:
                        scores2(i)
                    if i >= 1:
                        pe.wait_ge(pn_ready, 8 + l * 16 + i)
                        for grp in range(1 if i <= 8 else 3):
                            transposes2(sn[:, (i - 1) % 2, grp, :], 3)
                    for j in BESIDE[i]:
                        block1(j)
                    if i >= 1:
                        out2(i - 1)

                pe.wait_ge(y_lo, l * 12 + 12)
                for mm in range(4):
                    for r in range(3):
                        bb, n = B_HYB + H_MERGE + 9 * mm + 3 * r, G_HYB + H_MERGE + 12 * mm + 4 * r
                        run(bb, n, 2, 8, of_h, b4=b4, g4=g4)
                        run(bb + 2, n + 2, 2, 4, lambda m, k: yh[:, 4 * ((2 * r + m) % 3) + k, :], b4=b4, g4=g4, half=half_done)
                run(B_HYB + H_WO, G_HYB + H_MERGE + 48, 8, 8, lambda m, k: mh[:, k, :], b4=b4, g4=g4,
                    each_k=lambda k: pe.wait_ge(m_lo, l * 8 + k + 1))

        @block.scalar
        def _(act):
            chain = Chain(act, act_own)

            def hi(n, r4=0):
                s = n % 4
                act.wait_ge(w_raw[s], 16 * (n // 4 + 1) + 16 * r4)
                if n >= 4:
                    act.wait_ge(blk_done, n - 3 + 4 * r4)
                act.activation(whi[:, s, :], raw[:, s, :], ACT.Copy).then_inc(w_hi, 1)

            def square_x(k):
                act.activation(sq[:, k, :], x[:, k, :], ACT.Square).then_inc(sq_ready, 1)

            def root(n):
                act.wait_ge(ss_done, n + 1)
                act.activation(rstd[:, :], S[:, 2, 0:T], ACT.Ln, bias=EPS, scale=1.0 / D).then_inc(ln_done, 1)
                act.wait_ge(ln_done, n + 1)
                act.activation(rstd[:, :], rstd[:, :], ACT.Exp, scale=-0.5).then_inc(rstd_ready, 1)

            def norm_hi(base_t, base_h, shift):
                for k in range(KT):
                    act.wait_ge(t_ready, base_t + k + 1)
                    if shift is None:
                        ins = act.activation(h[:, k, 0:T], sq[:, k, :], ACT.Copy)
                    else:
                        ins = act.activation(h[:, k, 0:T], sq[:, k, :], ACT.Identity, bias=mod[:, shift + k:shift + k + 1])
                    ins.then_inc(hi_ready, 1)

            t_ring = Ring(2)

            def evac_t(dst, n=384, scale=1.0):
                slot, _, done = t_ring.next()
                act.wait_ge(t_done, done)
                act.activation(dst, Tp[:, slot, 0:n], ACT.Copy, scale=scale).then_inc(t_free, 1)

            def evac_v(dst):
                slot, _, done = t_ring.next()
                act.wait_ge(t_done, done)
                act.activation(dst, Tp[:, slot, 0:T].rearrange("p (j c) -> p j c", j=2), ACT.Copy).then_inc(t_free, 1)

            act.dma_start(silc[:, 0:8], a["c"]).then_inc(in_cols, 16)
            act.dma_start(cols[:, :], a["cols"]).then_inc(in_cols, 16)
            for dst, name in ((ident, "ident"), (ones, "ones"), (cmask, "cmask"), (slopes, "slopes")):
                act.dma_start(dst[:, :], a[name]).then_inc(in_const, 16)
            for dst, name in ((usum, "usum"), (sbm, "sbm"), (mcos, "mcos"), (msin, "msin")):
                act.dma_start(dst[:, :], a[name]).then_inc(in_att, 16)
            act.wait_ge(in_cols, 32)
            act.preload_act_table_set(LNEXP)
            act.activation(silc[:, 8:16], silc[:, 0:8], ACT.Exp, scale=-1.0).then_inc(exp_c, 1)
            act.wait_ge(in_x, 16)
            for k in range(KT):
                square_x(k)
            root(0)
            for n in range(4):
                hi(n)
            norm_hi(0, 0, 0)

            def softplus_part(g2):
                z4 = zs[:, 4 * g2:4 * g2 + 4, :]
                s4 = sp[:, 4 * g2:4 * g2 + 4, :]
                act.wait_ge(s_free, ATT_S.index(f"z{4 * g2 + 3}") + 1)
                chain.link(act.activation(s4, z4, ACT.Abs))
                chain.link(act.activation(s4, s4, ACT.Exp, scale=-1.0))
                act.activation(s4, s4, ACT.Ln, bias=1.0).then_inc(sb_ln, 1)

            def sb_weights(hh):
                act.wait_ge(s_free, ATT_S.index(f"c{hh}") + 1)
                act.activation(zs[:, hh, :], zs[:, hh, :], ACT.Exp).then_inc(sb_a, 1)

            def o_split(p):
                act.wait_ge(o_done, p + 1)
                act.activation(oh[:, (p + 4) % 8, 0:T], O[:, 0:T], ACT.Copy).then_inc(o_hi, 1)

            def moba_exps(i):
                act.wait_ge(s_free, ATT_S.index(f"m{i}") + 1)
                for qt, r in ((0, slice(0, P)), (1, slice(P, 384))):
                    ins = act.activation(pr[:, i % 2, r], pr[:, i % 2, r], ACT.Exp, scale=-1.0,
                                         bias=mn[:, i % 2, qt:qt + 1], accum_out=rs[:, i % 2, qt:qt + 1])
                ins.then_inc(p_ready, 1)

            def qkv_tile(b):
                act.wait_ge(blk_done, b + 1)
                if b < 8:
                    dst, scale = mqk[:, b, :], -HD ** -0.5 if b < 4 else 1.0
                elif 12 <= b < 20:
                    dst, scale = sqk[:, (b - 12) // 2 + 4 * (b % 2), :], 1.0 if b % 2 else HD ** -0.5
                else:
                    dst, scale = vT[:, b % 4, :], 1.0
                act.activation(dst, gslot(b), ACT.Copy, scale=scale).then_inc(slot_free[b % 4], 1)
                hi(b + 4)

            for b in range(25):
                if b in (15, 17, 19, 21):
                    o_split((b - 15) // 2)
                if 10 <= b <= 13 or b >= 22:
                    c = P * (b - 6 if b <= 13 else b - 22)
                    evac_v(vtok[:, :, c:c + P])
                if 13 <= b <= 20:
                    evac_t(pt[:, (b - 13) % 2, :])
                if b >= 1:
                    qkv_tile(b - 1)
                if 12 <= b < 20:
                    moba_exps(b - 12)
                if b in (18, 22):
                    softplus_part(b // 4 - 4)
                if b == 23:
                    for hh in range(4):
                        sb_weights(hh)
            o_split(4)
            evac_v(vtok[:, :, 3 * P:4 * P])
            for hh in range(4, 8):
                sb_weights(hh)
            for p in range(5, 8):
                o_split(p)

            def x_squares(b, n_blocks, g, ends):
                act.preload_act_table_set(LNEXP)
                for bb in range(n_blocks):
                    hi(b + bb + 4)
                    for m in range(8):
                        if ends[m] == bb:
                            act.wait_ge(slot_free[(g + m) % 4], taken(g + m))
                            square_x(m)

            one_each = list(range(8))
            two_each = [2 * m + 1 for m in range(8)]
            of_down = [-(-FT * (m + 1) // 8) - 1 for m in range(8)]

            x_squares(B_ATT_O, 8, G_ATT_O, one_each)

            def ffn(b, g):
                with act.Fori(0, FT // 2) as i:
                    for q in range(2):
                        gg = g + 2 * q
                        act.wait_ge(blk_done, b + 2 * q + 1 + 4 * i)
                        act.activation(sg[:, q, :], gslot(gg), ACT.Silu).then_inc(slot_free[gg % 4], 1)
                        hi(b + 2 * q + 4, i)
                        hi(b + 2 * q + 5, i)
                        act.wait_ge(slot_free[(gg + 1) % 4], taken(gg + 1) + i)
                        act.activation(ah[:, i * 2 + q, 0:T], af[:, q, :], ACT.Copy).then_inc(ah_hi, 1)

            root(1)
            norm_hi(8, 8, 24)
            ffn(B_FFN0, G_FFN0)
            x_squares(B_DOWN0, FT, G_DOWN0, of_down)

            root(2)
            norm_hi(16, 16, 48)
            act.dma_start(rcos[:, :], a["rcos"]).then_inc(in_ret, 16)
            act.dma_start(rsin[:, :], a["rsin"]).then_inc(in_ret, 16)
            act.dma_start(dec[:, :, :], a["dec"]).then_inc(in_ret, 16)

            def ret_part(hh, part):
                if part == 1:
                    act.wait_ge(r_o, hh + 1)
                    if hh == 0:
                        act.wait_ge(rope_ready, 4)
                    act.activation(sq[:, 0:4, :], S[:, 1:3, :].rearrange("p b (m t) -> p (b m) t", m=2),
                                   ACT.Copy).then_inc(r_of, 1)
                elif part == 2:
                    evac_t(rmu[:, :], T, 1.0 / 512)
                    act.wait_ge(r_c, hh + 1)
                    act.activation(sq[:, 4:8, :], sq[:, 0:4, :], ACT.Square).then_inc(r_sq, 1)
                elif part == 3:
                    slot, _, done = t_ring.next()
                    act.preload_act_table_set(LNEXP)
                    act.wait_ge(t_done, done)
                    act.activation(rstd[:, :], Tp[:, slot, 0:T], ACT.Ln, bias=GN_EPS, scale=1.0 / 512).then_inc(t_free, 1)
                    act.wait_ge(t_free, done)
                    act.activation(rstd[:, :], rstd[:, :], ACT.Exp, scale=-0.5).then_inc(r_norm, 1)
                    act.wait_ge(r_y, hh + 1)
                    act.activation(yr[:, 4 * hh:4 * hh + 4, 0:T], sq[:, 0:4, :], ACT.Copy).then_inc(r_hi, 1)

            for b in range(48):
                g = G_RET + b
                act.wait_ge(blk_done, B_RET + b + 1)
                if b < 16:
                    dst, f, scale = rqk[:, b, :], ACT.Copy, 1.0 if b < 8 else 256 ** -0.5
                elif b < 32:
                    dst, f, scale = rvT[:, b % 2, :], ACT.Copy, 1.0
                else:
                    dst, f, scale = rg[:, b - 32, :], ACT.Silu, 1.0
                act.activation(dst, gslot(g), f, scale=scale).then_inc(slot_free[g % 4], 1)
                hi(B_RET + b + 4)
                if 17 <= b < 33:
                    evac_v(rv[:, :, (b - 17) * P:(b - 16) * P])
                if b >= 33:
                    ret_part((b - 33) // 4, (b - 33) % 4)
            ret_part(3, 3)
            x_squares(B_RET_O, 16, G_RET_O, two_each)
            root(3)
            norm_hi(24, 24, 72)
            ffn(B_FFN1, G_FFN1)

            def x_squares_last(b, n_blocks, g, ends):
                act.preload_act_table_set(LNEXP)
                for bb in range(n_blocks):
                    if bb < n_blocks - 4:
                        hi(b + bb + 4)
                    for m in range(8):
                        if ends[m] == bb:
                            act.wait_ge(slot_free[(g + m) % 4], taken(g + m))
                            square_x(m)

            x_squares_last(B_DOWN1, FT, G_DOWN1, of_down)
            root(4)

            act.dma_start(dist[:, :, :], a["dist"]).then_inc(in_hyb, 16)
            act.dma_start(bones[:, :], a["bones"]).then_inc(in_hyb, 16)
            act.dma_start(lcs[:, :, :, :], a["lcs"]).then_inc(in_hyb, 16)
            act.dma_start(rows[:, :, :, :], a["rows"]).then_inc(in_hyb, 16)
            with act.Fori(0, LAYERS2) as l:
                chain.restart()
                b4, g4 = l * (HYB_BLOCKS // 4), l * (HYB_TILES // 4)
                t_ring = Ring(2, L1_T + l * HYB_T)
                s_base = L1_S + l * HYB_S

                def wait_t():
                    slot, _, done = t_ring.next()
                    act.wait_ge(t_done, done)
                    return slot

                def next_hi(j):
                    if j + 4 < HYB_BLOCKS:
                        hi(B_HYB + j + 4, b4)

                def done(j):
                    act.wait_ge(blk_done, B_HYB + j + 1 + 4 * b4)

                def freed(ins, j):
                    ins.then_inc(slot_free[(G_HYB + j) % 4], 1)

                act.preload_act_table_set(LNEXP)
                for k in range(KT):
                    act.wait_ge(t_ready, 32 + l * 8 + k + 1)
                    last = G_HYB - 8 + k
                    act.wait_ge(slot_free[last % 4], taken(last) + g4)
                    square_x(k)
                    if k in (4, 5):
                        hi(B_HYB + k - 4, b4)
                act.wait_ge(ss_done, l + 6)
                act.activation(rstd[:, :], S[:, 2, 0:T], ACT.Ln, bias=EPS, scale=1.0 / D).then_inc(ln_done, 1)
                act.wait_ge(ln_done, l + 6)
                act.activation(rstd[:, :], rstd[:, :], ACT.Exp, scale=-0.5).then_inc(rstd_ready, 1)
                act.dma_start(wuq, a["uq"][l]).then_inc(in_small, 16)
                act.dma_start(wkv, a["ukv"][l]).then_inc(in_small, 16)
                norm_hi(40 + l * 8, 32 + l * 8, None)
                for j in (2, 3):
                    hi(B_HYB + j, b4)

                for j in range(3):
                    done(j)
                    act.activation(cF[:, j, :], gslot(G_HYB + j), ACT.Copy)
                    freed(act.activation(csq[:, j, :], gslot(G_HYB + j), ACT.Square), j)
                    next_hi(j)
                done(3)
                freed(act.activation(kpT[:, :], gslot(G_HYB + 3)[0:32, :], ACT.Copy), 3)
                next_hi(3)
                for n, width in ((0, 256), (1, 128)):
                    slot = wait_t()
                    act.activation(cr[:, n, :], Tp[:, slot, 0:T], ACT.Ln, bias=EPS, scale=1.0 / width).then_inc(t_free, 1)
                    act.wait_ge(t_free, L1_T + l * HYB_T + n + 1)
                    act.activation(cr[:, n, :], cr[:, n, :], ACT.Exp, scale=-0.5).then_inc(c_ready, 1)
                slot = wait_t()
                act.activation(kpe[:, :, :], Tp[:, slot, 0:64].rearrange("p (j c) -> p j c", j=2),
                               ACT.Copy).then_inc(t_free, 1)
                for j in range(4, 8):
                    done(j)
                    act.activation(bz[:, j - 4, :], gslot(G_HYB + j), ACT.Tanh, scale=0.5).then_inc(tanh_ready, 1)
                    next_hi(j)
                act.preload_act_table_set(LNEXP)

                def d_root(j):
                    slot = wait_t()
                    if j >= 2:
                        act.wait_ge(d_norm, l * 24 + j - 1)
                    act.activation(at[:, j % 2, :], Tp[:, slot, 0:T], ACT.Ln, bias=EPS, scale=1.0 / HD).then_inc(t_free, 1)
                    act.wait_ge(t_free, L1_T + l * HYB_T + t_ring.n)
                    act.activation(at[:, j % 2, :], at[:, j % 2, :], ACT.Exp, scale=-0.5).then_inc(d_rs, 1)

                for j in range(24):
                    done(H_DQ + j)
                    act.activation(sq[:, j % 8, :], gslot(G_HYB + H_DQ + j), ACT.Square).then_inc(d_sq, 1)
                    freed(act.activation(dqk[:, j, :], gslot(G_HYB + H_DQ + j), ACT.Copy), H_DQ + j)
                    next_hi(H_DQ + j)
                    if j >= 1:
                        d_root(j - 1)
                    if j == 3:
                        act.wait_ge(qk_in, l + 1)
                        act.activation(qks[:, :, :, :], qk[:, :, :, :], ACT.Square).then_inc(qk_sq, 1)
                    if j == 6:
                        act.wait_ge(qk_ss, l + 1)
                        chain.link(act.activation(s32[:, :], s32[:, :], ACT.Ln, bias=EPS, scale=1.0 / 96))
                        act.activation(s32[:, :], s32[:, :], ACT.Exp, scale=-0.5).then_inc(qk_rs, 1)
                    if j >= 20:
                        for hh in (2 * (j - 20), 2 * (j - 20) + 1):
                            slot = wait_t()
                            act.activation(qkT[:, hh, :], Tp[0:96, slot, :], ACT.Copy).then_inc(t_free, 1)

                def evac_dv(t):
                    slot = wait_t()
                    act.activation(dv[:, :, t * P:(t + 1) * P], Tp[:, slot, 0:T].rearrange("p (j c) -> p j c", j=2),
                                   ACT.Copy).then_inc(t_free, 1)

                for j in range(12):
                    done(H_DV + j)
                    if j < 2:
                        act.wait_ge(d_norm, l * 24 + 23 + j)
                    freed(act.activation(at[:, j % 4, :], gslot(G_HYB + H_DV + j), ACT.Copy), H_DV + j)
                    next_hi(H_DV + j)
                    if j == 0:
                        d_root(23)
                    else:
                        evac_dv(j - 1)
                evac_dv(11)

                def exps(i):
                    s = i % 2
                    if i < 8:
                        act.wait_ge(s_free, s_base + (8 + i + 1))
                        low = mn2[:, s, :, 0]
                    else:
                        act.wait_ge(mj_ready, l * 8 + (i - 8 + 1))
                        low = mj[:, s, :]
                    for grp in range(1 if i < 8 else 3):
                        for qt, r in ((0, slice(0, P)), (1, slice(P, 384))):
                            ins = act.activation(sn[:, s, grp, r], sn[:, s, grp, r], ACT.Exp, scale=-1.0,
                                                 bias=low[:, qt:qt + 1], accum_out=rs2[:, s, qt, grp:grp + 1])
                    ins.then_inc(p_ready, 1)

                def y_split(idx, ready, src):
                    act.wait_ge(*ready)
                    act.activation(yh[:, idx, 0:T], src, ACT.Copy).then_inc(y_hi, 1)

                def head_block(j):
                    done(j)
                    t, kind = (j - H_A) // 4, (j - H_A) % 4
                    if j < H_A:
                        act.activation(cz[:, j - H_CZ, :], gslot(G_HYB + j), ACT.Tanh, scale=0.5).then_inc(tanh_ready, 1)
                    elif kind == 0:
                        freed(act.activation(at[:, 0, :], gslot(G_HYB + j), ACT.Copy), j)
                    elif kind == 3:
                        act.activation(at[:, 2, :], gslot(G_HYB + j), ACT.Tanh, scale=0.5).then_inc(tanh_ready, 1)
                    next_hi(j)

                for i in range(18):
                    if 1 <= i <= 16:
                        for grp in range(1 if i <= 8 else 3):
                            slot = wait_t()
                            act.activation(pt2[:, grp, :], Tp[:, slot, 0:384], ACT.Copy).then_inc(t_free, 1)
                    if i >= 1:
                        for j in BESIDE[i - 1]:
                            head_block(j)
                    if i < 16:
                        exps(i)
                    if i >= 1:
                        for j in BESIDE[i - 1]:
                            if j >= H_A and (j - H_A) % 4 == 3:
                                t = (j - H_A) // 4
                                y_split(t, (a_ready, l * 4 + t + 1), at[:, 3, :])
                    if i >= 3 and i % 2:
                        p = (i - 3) // 2
                        y_split(4 + p, (o_free, L1_O + l * 8 + p + 1), at[:, 4, :])

                for mm in range(4):
                    for q in range(9):
                        j = H_MERGE + 9 * mm + q
                        done(j)
                        if q % 3 < 2:
                            pair = 2 * (q // 3) + q % 3
                            n = H_MERGE + 12 * mm + 4 * (q // 3) + q % 3
                            col = 8 * (pair % 3) + 2 * mm + pair // 3
                            freed(act.activation(th[:, pair, :], gslot(G_HYB + n), ACT.Tanh, scale=0.5,
                                                 bias=hb[:, col:col + 1]), n)
                        next_hi(j)
                        if q in (6, 8):
                            m = 2 * mm + q // 8
                            act.wait_ge(m_ready, l * 8 + m + 1)
                            act.activation(mh[:, m, 0:T], mg[:, m % 2, :], ACT.Copy, scale=0.5).then_inc(m_hi, 1)
                for j in range(H_WO, HYB_BLOCKS - 4):
                    next_hi(j)
                assert t_ring.n == HYB_T

        @block.vector
        def _(dve):
            chain = Chain(dve, dve_own)

            def lo(n, r4=0):
                s = n % 4
                dve.wait_ge(w_hi, n + 1 + 4 * r4)
                dve.tensor_tensor(wlo[:, s, :], raw[:, s, :], whi[:, s, :], ALU.subtract).then_inc(w_lo, 1)

            def bc(ap, n, axis=1):
                return ap.unsqueeze(axis).broadcast_to([P, n, ap.shape[-1]])

            def add_bias(v, slot):
                return dve.tensor_tensor(mod[:, 8 * v:8 * v + 8], S[:, slot, 0:8],
                                         cols[:, C_ADAB + 8 * v:C_ADAB + 8 * v + 8], ALU.add)

            def mod_vector(v):
                dve.wait_ge(ada_used, v + 1 if v < 2 else v)
                add_bias(v, 0).then_inc(mod_ready, 1)
                dve.wait_ge(mod_ready, v + 1)

            def mod_gain(v, gain):
                chain.link(dve.scalar_tensor_tensor(out=modA[:, :], in0=mod[:, 8 * v:8 * v + 8], scalar=1.0,
                                                    in1=cols[:, gain:gain + 8], op0=ALU.add, op1=ALU.mult))

            def norm(n_rstd, base_t, base_h, gain, shift):
                dve.wait_ge(rstd_ready, n_rstd)
                for k in range(KT + 1):
                    if k < KT:
                        dve.scalar_tensor_tensor(out=sq[:, k, :], in0=x[:, k, :], scalar=gain(k), in1=rstd[:, :],
                                                 op0=ALU.mult, op1=ALU.mult).then_inc(t_ready, 1)
                    if k >= 1:
                        j = k - 1
                        dve.wait_ge(hi_ready, base_h + j + 1)
                        if shift is None:
                            ins = dve.tensor_tensor(h[:, j, T:2 * T], sq[:, j, :], h[:, j, 0:T], ALU.subtract)
                        else:
                            ins = dve.scalar_tensor_tensor(out=h[:, j, T:2 * T], in0=sq[:, j, :], scalar=shift(j),
                                                           in1=h[:, j, 0:T], op0=ALU.add, op1=ALU.subtract)
                        ins.then_inc(h_ready, 1)

            def col(tile_, c):
                return lambda k: tile_[:, c + k:c + k + 1]

            s_ring = Ring(3)

            def wait_s():
                slot, _, done = s_ring.next()
                dve.wait_ge(s_done, done)
                return slot

            dve.wait_ge(exp_c, 1)
            chain.link(dve.tensor_scalar(silc[:, 8:16], silc[:, 8:16], 1.0, None, ALU.add))
            chain.link(dve.reciprocal(silc[:, 8:16], silc[:, 8:16]))
            dve.tensor_tensor(silc[:, 16:24], silc[:, 8:16], silc[:, 0:8], ALU.mult).then_inc(silu_c, 1)
            dve.wait_ge(silu_c, 1)
            for n in range(16):
                dve.wait_ge(ada_first[n // 4], 16)
                half, w = n // 8, adaw[:, n, :]
                if n % 8 == 0:
                    ins = dve.tensor_scalar(acc[:, half, :], w, silc[:, 16:17], None, ALU.mult)
                else:
                    ins = dve.scalar_tensor_tensor(out=acc[:, half, :], in0=w, scalar=silc[:, 16 + n % 8:17 + n % 8],
                                                   in1=acc[:, half, :], op0=ALU.mult, op1=ALU.add)
                if n % 8 < 7:
                    chain.link(ins)
                else:
                    ins.then_inc(ada_acc, 1)
            for n in range(4):
                lo(n)
            mod_vector(0)
            mod_vector(1)
            mod_gain(1, C_G0)
            norm(1, 0, 0, col(modA, 0), col(mod, 0))

            def rope_moba(n):
                A, B = mqk[:, 4 * n:4 * n + 4:2, :], mqk[:, 4 * n + 1:4 * n + 4:2, :]
                RA, RB = mro[:, 4 * n:4 * n + 2, :], mro[:, 4 * n + 2:4 * n + 4, :]
                cos, sin = bc(mcos[:, :], 2), bc(msin[:, :], 2)
                for s in range(4):
                    dve.wait_ge(slot_free[s], 1 + n)
                if n:
                    dve.wait_ge(rope_ready, 1)
                dve.tensor_tensor(RA, A, cos, ALU.mult)
                chain.link(dve.tensor_tensor(rtmp[:, :, :], B, sin, ALU.mult))
                chain.link(dve.tensor_tensor(RA, RA, rtmp[:, :, :], ALU.subtract))
                dve.tensor_tensor(RB, B, cos, ALU.mult)
                chain.link(dve.tensor_tensor(rtmp[:, :, :], A, sin, ALU.mult))
                dve.tensor_tensor(RB, RB, rtmp[:, :, :], ALU.add).then_inc(rope_ready, 1)

            def softplus(g2):
                z4, s4 = zs[:, 4 * g2:4 * g2 + 4, :], sp[:, 4 * g2:4 * g2 + 4, :]
                dve.wait_ge(sb_ln, g2 + 1)
                dve.scalar_tensor_tensor(out=s4, in0=z4, scalar=0.0, in1=s4, op0=ALU.max, op1=ALU.add).then_inc(sb_sp, 1)

            def minus_sums(hh):
                slot = wait_s()
                dve.tensor_tensor(zs[:, hh, :], zs[:, hh, :], S[:, slot, 0:384], ALU.subtract).then_inc(s_free, 1)

            def o_split(p):
                dve.wait_ge(o_hi, p + 1)
                o = (p + 4) % 8
                dve.tensor_tensor(oh[:, o, T:2 * T], O[:, 0:T], oh[:, o, 0:T], ALU.subtract).then_inc(o_free, 1)

            def moba_minima(i):
                slot = wait_s()
                for qt, r in ((0, slice(0, P)), (1, slice(P, 384))):
                    ins = dve.tensor_tensor_reduce(out=pr[:, i % 2, r], in0=S[:, slot, r], in1=cmask[:, r], scale=1.0,
                                                   scalar=3e38, op0=ALU.add, op1=ALU.min,
                                                   accum_out=mn[:, i % 2, qt:qt + 1])
                ins.then_inc(s_free, 1)

            def moba_normalise(i):
                s = i % 2
                dve.wait_ge(p_ready, i + 1)
                chain.link(dve.reciprocal(ri[:, s, :], rs[:, s, :]))
                dve.tensor_scalar(pr[:, s, 0:P], pr[:, s, 0:P], ri[:, s, 0:1], None, ALU.mult)
                dve.tensor_scalar(pr[:, s, P:384], pr[:, s, P:384], ri[:, s, 1:2], None, ALU.mult).then_inc(pn_ready, 1)

            dve.wait_ge(in_att, 64)
            dve.wait_ge(in_const, 64)
            for b in range(25):
                if b in (15, 17, 19, 21):
                    for hh in (b - 15, b - 14):
                        slot = wait_s()
                        dve.tensor_tensor(zs[:, hh, :], S[:, slot, 0:384], sbm[:, :], ALU.add).then_inc(s_free, 1)
                if b == 21:
                    add_bias(2, wait_s()).then_inc(s_free, 1)
                    dve.wait_ge(s_free, ATT_S.index("a") + 1)
                    dve.memset(mark[:, 0:1], 0.0).then_inc(mod_ready, 1)
                if b in (22, 24):
                    for hh in range(2 * b - 44, 2 * b - 40):
                        minus_sums(hh)
                if 12 <= b < 20:
                    moba_minima(b - 12)
                if b >= 1:
                    lo(b + 3)
                if b in (15, 17, 19, 21):
                    o_split((b - 15) // 2)
                if 12 <= b < 20:
                    moba_normalise(b - 12)
                if b in (5, 9):
                    rope_moba(b // 4 - 1)
                if b in (19, 23):
                    softplus(b // 4 - 4)
            for p in range(4, 8):
                o_split(p)

            def x_update(b, n_blocks, g, ends, gate, vectors=(), last=False):
                for bb in range(n_blocks):
                    for m in range(8):
                        if ends[m] == bb:
                            dve.wait_ge(blk_done, b + bb + 1)
                            dve.scalar_tensor_tensor(out=x[:, m, :], in0=gslot(g + m),
                                                     scalar=mod[:, 8 * gate + m:8 * gate + m + 1], in1=x[:, m, :],
                                                     op0=ALU.mult, op1=ALU.add).then_inc(slot_free[(g + m) % 4], 1)
                            if vectors and m in (5, 6):
                                mod_vector(vectors[m - 5])
                    if not (last and bb >= n_blocks - 4):
                        lo(b + bb + 4)

            one_each = list(range(8))
            two_each = [2 * m + 1 for m in range(8)]
            of_down = [-(-FT * (m + 1) // 8) - 1 for m in range(8)]

            x_update(B_ATT_O, 8, G_ATT_O, one_each, 2, (3, 4))

            def ffn(b, g):
                with dve.Fori(0, FT // 2) as i:
                    for q in range(2):
                        gg = g + 2 * q
                        lo(b + 2 * q + 4, i)
                        dve.wait_ge(blk_done, b + 2 * q + 2 + 4 * i)
                        dve.wait_ge(slot_free[gg % 4], taken(gg) + i)
                        dve.tensor_tensor(af[:, q, :], gslot(gg + 1), sg[:, q, :],
                                          ALU.mult).then_inc(slot_free[(gg + 1) % 4], 1)
                        lo(b + 2 * q + 5, i)
                        dve.wait_ge(ah_hi, ah_base[0] + i * 2 + q + 1)
                        dve.tensor_tensor(ah[:, i * 2 + q, T:2 * T], af[:, q, :], ah[:, i * 2 + q, 0:T],
                                          ALU.subtract).then_inc(ah_ready, 1)

            ah_base = [0]
            mod_gain(4, C_G0 + 8)
            norm(2, 8, 8, col(modA, 0), col(mod, 24))
            ffn(B_FFN0, G_FFN0)
            mod_vector(5)
            x_update(B_DOWN0, FT, G_DOWN0, of_down, 5, (6, 7))

            mod_gain(7, C_G0 + 16)
            norm(3, 16, 16, col(modA, 0), col(mod, 48))

            def rope_ret(n):
                A, B = rqk[:, 8 * n:8 * n + 8:2, :], rqk[:, 8 * n + 1:8 * n + 8:2, :]
                cos, sin = bc(rcos[:, :], 4), bc(rsin[:, :], 4)
                for g in range(G_RET + 8 * n + 4, G_RET + 8 * n + 8):
                    dve.wait_ge(slot_free[g % 4], taken(g))
                dve.tensor_tensor(sq[:, 0:4, :], A, sin, ALU.mult)
                chain.link(dve.tensor_tensor(sq[:, 4:8, :], B, sin, ALU.mult))
                dve.tensor_tensor(A, A, cos, ALU.mult)
                chain.link(dve.tensor_tensor(B, B, cos, ALU.mult))
                dve.tensor_tensor(A, A, sq[:, 4:8, :], ALU.subtract)
                dve.tensor_tensor(B, B, sq[:, 0:4, :], ALU.add).then_inc(rope_ready, 1)
                dve.wait_ge(rope_ready, 3 + n)

            def ret_part(hh, part):
                if part == 0:
                    dve.wait_ge(r_sc, hh + 1)
                    dve.tensor_tensor(rp[:, hh % 2, 0:T], S[:, 0, 0:T], dec[:, hh, :], ALU.mult)
                    dve.tensor_tensor(rp[:, hh % 2, T:384], S[:, 0, T:384], dec[:, hh, 0:P], ALU.mult).then_inc(r_pt, 1)
                elif part == 2:
                    dve.wait_ge(t_free, 32 + 2 * hh + 1)
                    dve.tensor_tensor(sq[:, 0:4, :], sq[:, 0:4, :], bc(rmu[:, :], 4), ALU.subtract).then_inc(r_c, 1)
                elif part == 3:
                    dve.wait_ge(r_norm, hh + 1)
                    for m in range(4):
                        c = C_RETGN + 4 * hh + m
                        ins = dve.scalar_tensor_tensor(out=sq[:, m, :], in0=sq[:, m, :], scalar=cols[:, c:c + 1],
                                                       in1=rstd[:, :], op0=ALU.mult, op1=ALU.mult)
                    chain.link(ins)
                    dve.tensor_tensor(sq[:, 0:4, :], sq[:, 0:4, :], rg[:, 4 * hh:4 * hh + 4, :], ALU.mult).then_inc(r_y, 1)
                    dve.wait_ge(r_hi, hh + 1)
                    dve.tensor_tensor(yr[:, 4 * hh:4 * hh + 4, T:2 * T], sq[:, 0:4, :], yr[:, 4 * hh:4 * hh + 4, 0:T],
                                      ALU.subtract).then_inc(r_lo, 1)

            dve.wait_ge(in_ret, 48)
            for b in range(48):
                lo(B_RET + b + 4)
                if b in (8, 16):
                    rope_ret(b // 8 - 1)
                if b >= 33:
                    ret_part((b - 33) // 4, (b - 33) % 4)
            ret_part(3, 3)
            mod_vector(8)
            x_update(B_RET_O, 16, G_RET_O, two_each, 8, (9, 10))
            ah_base[0] = FT
            mod_gain(10, C_G0 + 24)
            norm(4, 24, 24, col(modA, 0), col(mod, 72))
            ffn(B_FFN1, G_FFN1)
            mod_vector(11)
            x_update(B_DOWN1, FT, G_DOWN1, of_down, 11, last=True)
            dve.wait_ge(rstd_ready, 5)
            for k in range(KT):
                dve.scalar_tensor_tensor(out=x[:, k, :], in0=x[:, k, :], scalar=cols[:, C_FINAL + k:C_FINAL + k + 1],
                                         in1=rstd[:, :], op0=ALU.mult, op1=ALU.mult).then_inc(t_ready, 1)

            chain.link(dve.memset(ua[:, 0:2], 0.0))
            dve.wait_ge(in_hyb, 64)
            with dve.Fori(0, LAYERS2) as l:
                chain.restart()
                b4, g4 = l * (HYB_BLOCKS // 4), l * (HYB_TILES // 4)
                s_ring = Ring(3, L1_S + l * HYB_S)

                def next_lo(j):
                    if j + 4 < HYB_BLOCKS:
                        lo(B_HYB + j + 4, b4)

                def done(j):
                    dve.wait_ge(blk_done, B_HYB + j + 1 + 4 * b4)

                def freed(ins, n):
                    ins.then_inc(slot_free[(G_HYB + n) % 4], 1)

                def wait_s():
                    slot, _, d_ = s_ring.next()
                    dve.wait_ge(s_done, d_)
                    return slot

                dve.tensor_copy(lcol[:, :], cols[:, C_HYB:].rearrange("p (l c) -> p l c", l=LAYERS2)[:, l, :])\
                   .then_inc(lcol_ready, 1)
                dve.wait_ge(lcol_ready, l * 3 + 1)
                dve.tensor_scalar(hb[:, :], lcol[:, L_BGATE:L_BGATE + 24], 0.5, None, ALU.mult).then_inc(lcol_ready, 1)
                dve.tensor_scalar(nq[:, :], lcol[:, L_DQ:L_DQ + 3], -HD ** -0.5, None, ALU.mult).then_inc(lcol_ready, 1)
                dve.wait_ge(lcol_ready, l * 3 + 3)
                for j in (0, 1):
                    lo(B_HYB + j, b4)
                norm(l + 6, 40 + l * 8, 32 + l * 8, col(lcol, L_NORM), None)
                for j in (2, 3):
                    lo(B_HYB + j, b4)

                for j in range(4):
                    next_lo(j)
                dve.wait_ge(c_ready, l * 2 + 2)
                for k in range(3):
                    ins = dve.scalar_tensor_tensor(out=cF[:, k, :], in0=cF[:, k, :], scalar=lcol[:, L_QA + k:L_QA + k + 1],
                                                   in1=cr[:, k // 2, :], op0=ALU.mult, op1=ALU.mult)
                ins.then_inc(cn_ready, 1)
                for j in range(4, 8):
                    dve.wait_ge(tanh_ready, l * 12 + (j - 3))
                    freed(dve.scalar_tensor_tensor(out=bz[:, j - 4, :], in0=bz[:, j - 4, :], scalar=1.0,
                                                   in1=gslot(G_HYB + j), op0=ALU.add, op1=ALU.mult), j)
                    next_lo(j)

                def mla_in():
                    for tt in range(2):
                        for half in range(2):
                            slot = wait_s()
                            dve.tensor_copy(qk[:, 0, tt, 384 * half:384 * half + 384], S[:, slot, 0:384])\
                               .then_inc(s_free, 1)
                    for tt in range(2):
                        slot = wait_s()
                        dve.tensor_copy(qk[:, 1, tt, :].rearrange("p (h c) -> p h c", c=96)[:, :, 0:64],
                                        S[:, slot, :].rearrange("p (h c) -> p h c", c=64)).then_inc(s_free, 1)
                    for tt in range(2):
                        slot = wait_s()
                        dve.tensor_copy(vm[:, tt, :], S[:, slot, :]).then_inc(s_free, 1)
                    dve.wait_ge(t_free, L1_T + l * HYB_T + 3)
                    for tt in range(2):
                        ins = dve.tensor_copy(qk[:, 1, tt, :].rearrange("p (h c) -> p h c", c=96)[:, :, 64:96],
                                              bc(kpe[:, tt, :], 8))
                    ins.then_inc(qk_in, 1)

                qk_rows = qk[:, :, :, :].rearrange("p n t (h c) -> p (n t h) c", c=96)
                s_rows = qks[:, :, :, :].rearrange("p n t (h c) -> p (n t h) c", c=96)

                def mla_sums():
                    dve.wait_ge(qk_sq, l + 1)
                    dve.tensor_reduce(out=s32[:, :], in_=s_rows, op=ALU.add, axis=AX).then_inc(qk_ss, 1)

                def mla_scale():
                    dve.wait_ge(qk_rs, l + 1)
                    chain.link(dve.tensor_scalar(s32[:, 0:16], s32[:, 0:16], -96.0 ** -0.5, None, ALU.mult))
                    chain.link(dve.tensor_tensor(qk_rows, qk_rows, s32[:, :].unsqueeze(2).broadcast_to([P, 32, 96]),
                                                 ALU.mult))

                def mla_gain():
                    for n in range(2):
                        v = qk[:, n, :, :].rearrange("p t (h c) -> p (t h) c", c=96)
                        ins = dve.tensor_tensor(v, v, rows[:, l, n, :].unsqueeze(1).broadcast_to([P, 16, 96]), ALU.mult)
                    chain.link(ins)

                def mla_rope(n):
                    v = qk[:, n, :, :].rearrange("p t (h c) -> p t h c", c=96)
                    x1, x2 = v[:, :, :, 64:80], v[:, :, :, 80:96]
                    w = qks[:, n, :, :].rearrange("p t (h c) -> p t h c", c=96)
                    t1, t2 = w[:, :, :, 0:16], w[:, :, :, 16:32]
                    cos = lcs[:, 0, :, :].unsqueeze(2).broadcast_to([P, 2, 8, 16])
                    sin = lcs[:, 1, :, :].unsqueeze(2).broadcast_to([P, 2, 8, 16])
                    dve.tensor_tensor(t1, x1, sin, ALU.mult)
                    chain.link(dve.tensor_tensor(t2, x2, sin, ALU.mult))
                    dve.tensor_tensor(x1, x1, cos, ALU.mult)
                    chain.link(dve.tensor_tensor(x2, x2, cos, ALU.mult))
                    dve.tensor_tensor(x1, x1, t2, ALU.subtract)
                    ins = dve.tensor_tensor(x2, x2, t1, ALU.add)
                    if n:
                        ins.then_inc(qk_ready, 1)
                    else:
                        chain.link(ins)

                def d_norm_tile(j):
                    dve.wait_ge(d_rs, l * 24 + j + 1)
                    grp = (j % 12) // 4
                    gain = nq[:, grp:grp + 1] if j < 12 else lcol[:, L_DK + grp:L_DK + grp + 1]
                    dve.scalar_tensor_tensor(out=dqk[:, j, :], in0=dqk[:, j, :], scalar=gain, in1=at[:, j % 2, :],
                                             op0=ALU.mult, op1=ALU.mult).then_inc(d_norm, 1)

                for j in range(24):
                    next_lo(H_DQ + j)
                    if j >= 2:
                        d_norm_tile(j - 2)
                    if j == 2:
                        mla_in()
                    if j == 5:
                        mla_sums()
                    if j == 8:
                        mla_scale()
                    if j == 10:
                        mla_gain()
                    if j in (12, 14):
                        mla_rope(j // 2 - 6)
                for j in range(12):
                    if j < 2:
                        d_norm_tile(22 + j)
                    next_lo(H_DV + j)

                def minima(i):
                    s = i % 2
                    for grp in range(1 if i < 8 else 3):
                        slot = wait_s()
                        if i >= 8:
                            j = 3 * (i - 8) + grp
                            dve.wait_ge(bias_ready, l * 24 + j + 1)
                            add = bias[:, j % 2, :]
                        else:
                            add = cmask[:, :]
                        dve.memset(mark[:, s_ring.n - 1:s_ring.n], 0.0)
                        for qt, r in ((0, slice(0, P)), (1, slice(P, 384))):
                            ins = dve.tensor_tensor_reduce(out=sn[:, s, grp, r], in0=S[:, slot, r], in1=add[:, r], scale=1.0,
                                                           scalar=3e38, op0=ALU.add, op1=ALU.min,
                                                           accum_out=mn2[:, s, qt, grp:grp + 1])
                        ins.then_inc(s_free, 1)
                    if i >= 8:
                        dve.wait_ge(s_free, L1_S + l * HYB_S + (16 + 3 * (i - 7)))
                        dve.tensor_reduce(out=mj[:, s, :], in_=mn2[:, s, :, :], op=ALU.min, axis=AX).then_inc(mj_ready, 1)

                def normalise(i):
                    s = i % 2
                    dve.wait_ge(p_ready, 8 + l * 16 + i + 1)
                    n = 1 if i < 8 else 3
                    if i < 8:
                        chain.link(dve.reciprocal(rj[:, s, :], rs2[:, s, :, 0]))
                    else:
                        chain.link(dve.tensor_reduce(out=rj[:, s, :], in_=rs2[:, s, :, :], op=ALU.add, axis=AX))
                        chain.link(dve.reciprocal(rj[:, s, :], rj[:, s, :]))
                    dve.tensor_scalar(sn[:, s, 0:n, 0:P], sn[:, s, 0:n, 0:P], rj[:, s, 0:1], None, ALU.mult)
                    dve.tensor_scalar(sn[:, s, 0:n, P:384], sn[:, s, 0:n, P:384], rj[:, s, 1:2], None,
                                      ALU.mult).then_inc(pn_ready, 1)

                y_n = [0]

                def y_split(idx, src):
                    y_n[0] += 1
                    dve.wait_ge(y_hi, l * 12 + y_n[0])
                    dve.tensor_tensor(yh[:, idx, T:2 * T], src, yh[:, idx, 0:T], ALU.subtract).then_inc(y_lo, 1)

                def head_block(j):
                    n = G_HYB + j
                    if j < H_A:
                        dve.wait_ge(tanh_ready, l * 12 + (4 + j - H_CZ + 1))
                        freed(dve.scalar_tensor_tensor(out=cz[:, j - H_CZ, :], in0=cz[:, j - H_CZ, :], scalar=1.0,
                                                       in1=gslot(n), op0=ALU.add, op1=ALU.mult), j)
                        next_lo(j)
                        return
                    t, kind = (j - H_A) // 4, (j - H_A) % 4
                    if kind == 1:
                        done(j)
                        dve.wait_ge(slot_free[(n - 1) % 4], taken(n - 1) + g4)
                        freed(dve.tensor_tensor(ua[:, 2:2 + T], gslot(n), at[:, 0, :], ALU.mult), j)
                        dve.wait_ge(slot_free[n % 4], taken(n) + g4)
                        w = [lcol[:, L_CONVW + 4 * tap + t:L_CONVW + 4 * tap + t + 1] for tap in range(3)]
                        chain.link(dve.tensor_scalar(at[:, 1, :], ua[:, 0:T], w[0], lcol[:, L_CONVB + t:L_CONVB + t + 1],
                                                     ALU.mult, ALU.add))
                        for tap in (1, 2):
                            chain.link(dve.scalar_tensor_tensor(out=at[:, 1, :], in0=ua[:, tap:tap + T], scalar=w[tap],
                                                                in1=at[:, 1, :], op0=ALU.mult, op1=ALU.add))
                    if kind == 2:
                        done(j)
                        freed(dve.tensor_tensor(at[:, 1, :], gslot(n), at[:, 1, :], ALU.mult), j)
                    if kind == 3:
                        dve.wait_ge(tanh_ready, l * 12 + (8 + t + 1))
                        freed(dve.scalar_tensor_tensor(out=at[:, 2, :], in0=at[:, 2, :], scalar=1.0, in1=gslot(n),
                                                       op0=ALU.add, op1=ALU.mult), j)
                        dve.wait_ge(slot_free[n % 4], taken(n) + g4)
                        dve.scalar_tensor_tensor(out=at[:, 3, :], in0=at[:, 1, :], scalar=0.5, in1=at[:, 2, :],
                                                 op0=ALU.mult, op1=ALU.mult).then_inc(a_ready, 1)
                    next_lo(j)

                def pair_out(p):
                    z = bz[:, p, :] if p < 4 else cz[:, p - 4, :]
                    dve.wait_ge(o_done, L1_O + l * 8 + p + 1)
                    dve.scalar_tensor_tensor(out=at[:, 4, :], in0=O[:, 0:T], scalar=0.5, in1=z, op0=ALU.mult,
                                             op1=ALU.mult).then_inc(o_free, 1)

                for i in range(18):
                    if i >= 3 and i % 2 and i < 17:
                        pair_out((i - 3) // 2)
                    if i < 16:
                        minima(i)
                    if i >= 1:
                        for j in BESIDE[i - 1]:
                            head_block(j)
                    if i == 17:
                        pair_out(7)
                    if i < 16:
                        normalise(i)
                    if i >= 1:
                        for j in BESIDE[i - 1]:
                            if j >= H_A and (j - H_A) % 4 == 3:
                                y_split((j - H_A) // 4, at[:, 3, :])
                    if i >= 3 and i % 2:
                        y_split(4 + (i - 3) // 2, at[:, 4, :])

                for mm in range(4):
                    for q in range(6):
                        r = q // 2
                        bb = H_MERGE + 9 * mm + 3 * r
                        gate = G_HYB + H_MERGE + 12 * mm + 4 * r + q % 2
                        n = gate + 2
                        m = 2 * mm + q // 3
                        if q % 2 == 0:
                            next_lo(bb)
                            next_lo(bb + 1)
                        if q % 2:
                            done(bb + 2)
                        else:
                            dve.wait_ge(half_done, l * 12 + 3 * mm + r + 1)
                        dve.wait_ge(slot_free[gate % 4], taken(gate) + g4)
                        if q % 3 == 0:
                            freed(dve.scalar_tensor_tensor(out=mg[:, m % 2, :], in0=th[:, q, :], scalar=1.0, in1=gslot(n),
                                                           op0=ALU.add, op1=ALU.mult), n - G_HYB)
                        else:
                            freed(dve.scalar_tensor_tensor(out=th[:, q, :], in0=th[:, q, :], scalar=1.0, in1=gslot(n),
                                                           op0=ALU.add, op1=ALU.mult), n - G_HYB)
                            dve.wait_ge(slot_free[n % 4], taken(n) + g4)
                            ins = dve.tensor_tensor(mg[:, m % 2, :], mg[:, m % 2, :], th[:, q, :], ALU.add)
                            if q % 3 == 1:
                                chain.link(ins)
                            else:
                                ins.then_inc(m_ready, 1)
                        if q % 2:
                            next_lo(bb + 2)
                        if q in (3, 5):
                            m = 2 * mm + q // 4
                            dve.wait_ge(m_hi, l * 8 + m + 1)
                            dve.scalar_tensor_tensor(out=mh[:, m, T:2 * T], in0=mg[:, m % 2, :], scalar=0.5,
                                                     in1=mh[:, m, 0:T], op0=ALU.mult, op1=ALU.subtract).then_inc(m_lo, 1)
                for m in range(8):
                    done(H_WO + m)
                    n = H_MERGE + 48 + m
                    freed(dve.tensor_tensor(x[:, m, :], gslot(G_HYB + n), x[:, m, :], ALU.add), n)
                    next_lo(H_WO + m)
                assert s_ring.n == HYB_S


def tables():
    f = np.float32
    r = np.arange(P)
    qpos = np.concatenate([np.zeros(P, int), np.full(T, P)])
    kpos = np.concatenate([np.arange(P), np.arange(T)])
    dist = (qpos[None, :] + r[:, None]) - kpos[None, :]
    t = {"ident": np.eye(P, dtype=f), "ones": np.ones((P, P), f)}
    t["cmask"] = np.where(dist >= 0, 0, MASKED).astype(f)
    t["usum"] = (r[:, None] >= r[None, :]).astype(f)
    q2 = np.concatenate([np.arange(T), np.arange(P, T)])
    k2 = np.concatenate([np.zeros(T, int), np.full(P, P)])
    t["sbm"] = np.where(k2[None, :] + r[:, None] < q2[None, :], 0, -MASKED).astype(f)
    t["dist"] = np.stack([np.where((dist >= 0) & (dist % d == 0) & (dist // d <= back), dist, MASKED)
                          for d, back in zip(DIL, N_BACK)], axis=1).astype(f)
    t["slopes"] = np.tile(np.array(SLOPES, f)[None, :], (P, 1))
    t["bones"] = np.kron(np.eye(2), np.ones((64, 64))).astype(f)

    def angles(d):
        inv = f(10000.0) ** (-np.arange(0, d, 2, dtype=f) / f(d))
        return (np.arange(T, dtype=f)[:, None] * inv[None, :]).astype(f)

    m = angles(64)
    t["mcos"], t["msin"] = (np.tile(g(m).T, (4, 1)).astype(f) for g in (np.cos, np.sin))
    m = angles(256)
    t["rcos"], t["rsin"] = (np.ascontiguousarray(g(m).T).astype(f) for g in (np.cos, np.sin))
    m = angles(32).reshape(2, P, 16)
    t["lcs"] = np.ascontiguousarray(np.stack([np.cos(m), np.sin(m)]).transpose(2, 0, 1, 3)).astype(f)
    log_g = np.log(1.0 - 2.0 ** (-5.0 - np.arange(4, dtype=np.float64)))
    diff = np.arange(T)[None, :] - r[:, None]
    t["dec"] = np.ascontiguousarray(np.where(diff[None] >= 0, np.exp(log_g[:, None, None] * np.maximum(diff, 0)[None]), 0)
                                    .transpose(1, 0, 2)).astype(f)
    return t


def blocks(w, cols=None, tiles=None):
    if cols is not None:
        w = w[:, cols]
    k, n = w.shape
    v = w.reshape(k // P, P, n // P, P).transpose(2, 0, 1, 3)
    return v if tiles else v.reshape(-1, 8, P, P)


def columns(v):
    return np.ascontiguousarray(np.asarray(v).reshape(-1, P).T)


def lay_out(i):
    halves = lambda base: np.concatenate([base + 64 * hh + 32 * half + np.arange(32)
                                          for g in range(2) for half in range(2) for hh in range(4 * g, 4 * g + 4)])
    s, m = np.arange(512), 512
    pairs = np.stack([s.reshape(4, P), 1024 + s.reshape(4, P)], axis=1).reshape(-1)
    qkv_cols = np.concatenate([halves(m), halves(1024 + m), 2048 + m + s, pairs, 2048 + s])
    parts = [blocks(i["att_w_qkv"][0], qkv_cols), blocks(i["att_w_o"][0])]

    def gate_up(w):
        v = w.reshape(D, 2, FT, P).transpose(0, 2, 1, 3).reshape(D, 2 * D_FF)
        return blocks(v)

    parts += [gate_up(i["ffn_w_gate_up"][0]), blocks(i["ffn_w_down"][0])]
    parts += [blocks(i["ret_w_in"][0]), blocks(i["ret_w_o"][0])]
    parts += [gate_up(i["ffn_w_gate_up"][1]), blocks(i["ffn_w_down"][1])]
    for l in range(LAYERS2):
        w = i["w_in_2"][l]
        at = np.cumsum([0] + [512] * 4 + [256, 128, 32, 512] + [1536] * 3 + [512, 3072])
        a_b, a_c, a_x, a_z, c_q, c_kv, k_pe, b_z, dq, dk, dv, c_z, gate = (w[:, p:q] for p, q in zip(at[:-1], at[1:]))
        parts += [blocks(c_q), blocks(c_kv), blocks(np.pad(k_pe, ((0, 0), (0, 96))))]
        parts += [blocks(v) for v in (b_z, dq, dk, dv, c_z)]
        conv = np.stack([v.reshape(D, 4, P) for v in (a_c, a_x, a_b, a_z)], axis=2).reshape(D, 2048)
        parts += [blocks(conv)]
        g = blocks(gate, tiles=True).reshape(3, 8, 8, P, P)
        o = np.stack([blocks(i[f"w_out_{b}_2"][l], tiles=True) for b in "abc"])
        for mm in range(4):
            for r in range(3):
                pairs = [(q % 3, 2 * mm + q // 3) for q in (2 * r, 2 * r + 1)]
                parts += [np.stack([g[b, m] for b, m in pairs]),
                          np.concatenate([o[b, m] for b, m in pairs])[None]]
        parts += [blocks(i["w_o_2"][l])]
    w = np.concatenate(parts).transpose(0, 2, 1, 3).reshape(-1, P, 1024)
    assert w.shape[0] == N_BLOCKS, w.shape
    ada = i["ada_w"].reshape(2, 8, P, 6, D).transpose(0, 3, 1, 2, 4).reshape(96, P, D)
    cols = [columns(i["norm_gains"]), columns(i["final_norm"]), columns(i["ret_gn"]), columns(i["ada_b"])]
    for l in range(LAYERS2):
        cols += [columns(i["norm_g_2"][l]), columns(i["b_gate_2"][l]), columns(i["conv_w_2"][l]),
                 columns(i["conv_b_2"][l]), columns(i["q_a_norm_g_2"][l]), columns(i["kv_a_norm_g_2"][l]),
                 columns(np.tile(i["dil_q_norm_g_2"][l], (1, 2))), columns(np.tile(i["dil_k_norm_g_2"][l], (1, 2)))]
    rows = np.stack([i["mla_q_norm_g_2"], i["mla_k_norm_g_2"]], axis=1)
    kv = i["w_ukv_2"].reshape(LAYERS2, P, 8, 2, 64).transpose(0, 1, 3, 2, 4).reshape(LAYERS2, P, 1024)
    return {
        "w": w, "ada": ada, "cols": np.concatenate(cols, axis=1), "c": columns(i["c"]),
        "x": i["x"][0].T.reshape(KT, P, T).transpose(1, 0, 2),
        "rows": np.broadcast_to(rows[None], (P, LAYERS2, 2, 96)),
        "uq": i["w_uq_2"].reshape(LAYERS2, 2, P, 768).transpose(0, 2, 1, 3), "ukv": kv,
    }


def kernel(**inputs):
    import concourse.bacc as bacc
    from concourse.bass_utils import run_bass_kernel_spmd

    arrays = lay_out({k: np.asarray(v) for k, v in inputs.items()})
    arrays.update(tables())
    arrays = {f"in_{k}": np.ascontiguousarray(v) for k, v in arrays.items()}
    nc = bacc.Bacc("TRN2", target_bir_lowering=False, num_devices=1)
    aps = {k[3:]: nc.dram_tensor(k, v.shape, mybir.dt.from_np(v.dtype), kind="ExternalInput").ap()
           for k, v in arrays.items()}
    out = nc.dram_tensor("out", (P, KT, T), mybir.dt.float32, kind="ExternalOutput").ap()
    build(nc, aps, out)
    r = run_bass_kernel_spmd(nc, [arrays], core_ids=[0])
    got = np.asarray(r.results[0]["out"])
    return np.ascontiguousarray(got.transpose(1, 0, 2).reshape(D, T).T)[None]
```

```python
from contextlib import ExitStack

import numpy as np

import concourse.bass as bass
from concourse import mybir

D = 1024
T = 256
P = 128
KT = D // P
HD = 64
D_FF = 2816
FT = D_FF // P
EPS = 1e-6
GN_EPS = 1e-5
MASKED = 1e30
LAYERS2 = 2

B_QKV = 0
B_ATT_O = B_QKV + 24
B_FFN0 = B_ATT_O + 8
B_DOWN0 = B_FFN0 + 2 * FT
B_RET = B_DOWN0 + FT
B_RET_O = B_RET + 48
B_FFN1 = B_RET_O + 16
B_DOWN1 = B_FFN1 + 2 * FT
B_HYB = B_DOWN1 + FT
HYB_BLOCKS = 88 + 12 + 8
N_BLOCKS = B_HYB + LAYERS2 * HYB_BLOCKS
G_QKV = 0
G_ATT_O = 24
G_FFN0 = G_ATT_O + 8
G_DOWN0 = G_FFN0 + 2 * FT
G_RET = G_DOWN0 + 8
G_RET_O = G_RET + 48
G_FFN1 = G_RET_O + 8
G_DOWN1 = G_FFN1 + 2 * FT
G_HYB = G_DOWN1 + 8
HYB_TILES = 88 + 24 + 8
G_END = G_HYB + LAYERS2 * HYB_TILES
assert B_HYB % 4 == 0 and HYB_BLOCKS % 4 == 0 and G_HYB % 4 == 0 and HYB_TILES % 4 == 0

C_G0 = 0
C_FINAL = C_G0 + 32
C_RETGN = C_FINAL + 8
C_ADAB = C_RETGN + 16
C_HYB = C_ADAB + 96
L_NORM = 0
L_BGATE = 8
L_CONVW = L_BGATE + 24
L_CONVB = L_CONVW + 12
L_QA = L_CONVB + 4
L_KVA = L_QA + 2
L_DQ = L_KVA + 1
L_DK = L_DQ + 3
LC = L_DK + 3
N_COLS = C_HYB + LAYERS2 * LC

H_BZ, H_DQ, H_DV, H_CZ, H_A = 4, 8, 32, 44, 48
H_MERGE = 64
H_WO = 100
DIL = (1, 4, 16)
N_BACK = (128, 128, 128)
SLOPES = [2.0 ** (-8.0 * (n + 1) / 24) for n in range(24)]
HYB_S = 4 + 4 + 8 + 24 + 8
HYB_T = 2 + 1 + 24 + 12 + 8 + 8 + 24
HYB_O = 8
ATT_S = ["m0", "m1", "m2", "m3", "z0", "z1", "m4", "m5", "z2", "z3", "m6", "m7", "z4", "z5", "a", "z6", "z7",
         "c0", "c1", "c2", "c3", "c4", "c5", "c6", "c7"]
L1_S = len(ATT_S)
L1_T = 8 + 8 + 16 + 8
L1_O = 8


BESIDE = [[] for _ in range(18)]
for _n in range(H_MERGE - H_CZ):
    BESIDE[0 if _n < 3 else _n - 2 if _n < 18 else 16].append(H_CZ + _n)


TAKEN = [BESIDE[0][:1], BESIDE[0][1:]] + BESIDE[1:17]

FIRST = [(0, 4), (4, 8), (8, 12), (12, 14), (14, 15), (15, 16)]

RET_PARTS = {}
for _n in range(4):
    for _part, _b in enumerate((32, 33, 34, 36)):
        if _b + 4 * _n < 48:
            RET_PARTS.setdefault(_b + 4 * _n, []).insert(0 if _part == 0 else 1, (_n, _part))


def pairs_before(i):
    return max(0, (i - 2) // 2)


def score_uses(i):
    return 8 + min(i + 1, 8) + 3 * max(0, i - 7) + pairs_before(i)


def pair_use(p):
    return score_uses(min(2 * p + 3, 15)) + (p == 7) + 1


class Ring:

    def __init__(self, slots, base=0):
        self.slots, self.base, self.n = slots, base, 0

    def next(self):
        n = self.n
        self.n += 1
        freed = self.base + (n - self.slots + 1 if n >= self.slots else 0)
        return n % self.slots, freed, self.base + n + 1


class Chain:

    def __init__(self, eng, sem):
        self.eng, self.sem, self.n = eng, sem, 0

    def add(self, ins):
        ins.then_inc(self.sem, 1)
        self.n += 1
        return self.n

    def wait(self, n=None):
        self.eng.wait_ge(self.sem, self.n if n is None else n)

    def link(self, ins):
        self.add(ins)
        self.wait()

    def restart(self):
        self.eng.sem_clear(self.sem)
        self.n = 0


def build(nc, a, out):
    fp32 = mybir.dt.float32
    f32r = mybir.dt.float32r
    ALU = mybir.AluOpType
    ACT = mybir.ActivationFunctionType
    AX = mybir.AxisListType.X
    LNEXP = "natural_log_exp_and_others"

    ctx = ExitStack()
    with ctx:
        def sb(name, shape, dt=fp32, stack=ctx):
            return stack.enter_context(nc.sbuf_tensor(name, shape, dt))

        def sem(name):
            return ctx.enter_context(nc.semaphore(name))

        x = sb("x", [P, KT, T])
        sq = sb("sq", [P, KT, T])
        h = sb("h", [P, KT, 2 * T], f32r)
        raw = sb("raw", [P, 4, 1024])
        whi = sb("whi", [P, 4, 1024], f32r)
        wlo = sb("wlo", [P, 4, 1024], f32r)
        rstd = sb("rstd", [P, T])
        cols = sb("cols", [P, N_COLS])
        lcol = sb("lcol", [P, LC])
        hb = sb("hb", [P, 24])
        nq = sb("nq", [P, 3])
        mod = sb("mod", [P, 96])
        modA = sb("modA", [P, 8])
        silc = sb("silc", [P, 3 * 8])
        ident = sb("ident", [P, P])
        ones = sb("ones", [P, P])
        slopes = sb("slopes", [P, 24])
        mark = sb("mark", [P, HYB_S])
        cmask = sb("cmask", [P, 384])

        G = ctx.enter_context(nc.psum_tensor("G", [P, 2, 512], fp32))
        S = ctx.enter_context(nc.psum_tensor("S", [P, 3, 512], fp32))
        Tp = ctx.enter_context(nc.psum_tensor("Tp", [P, 2, 512], fp32))
        O = ctx.enter_context(nc.psum_tensor("O", [P, 512], fp32))

        first = ExitStack()
        araw = sb("araw", [P, 4, 1024], stack=first)
        acc = sb("acc", [P, 2, 1024], stack=first)
        att = ExitStack()
        sqk = sb("sqk", [P, 8, T], stack=att)
        mqk = sb("mqk", [P, 8, T], stack=att)
        mro = sb("mro", [P, 8, T], stack=att)
        rtmp = sb("rtmp", [P, 2, T], stack=att)
        vT = sb("vT", [P, 4, T], stack=att)
        vtok = sb("vtok", [P, 2, 1024], stack=att)
        zs = sb("zs", [P, 8, 384], stack=att)
        sp = sb("sp", [P, 8, 384], stack=att)
        pr = sb("pr", [P, 2, 384], stack=att)
        pt = sb("pt", [P, 2, 384], stack=att)
        mn = sb("mn", [P, 2, 2], stack=att)
        rs = sb("rs", [P, 2, 2], stack=att)
        ri = sb("ri", [P, 2, 2], stack=att)
        usum = sb("usum", [P, P], stack=att)
        sbm = sb("sbm", [P, 384], stack=att)
        mcos = sb("mcos", [P, T], stack=att)
        msin = sb("msin", [P, T], stack=att)
        oh = sb("oh", [P, KT, 2 * T], f32r, stack=att)
        att.close()
        start = ExitStack()
        adaw = sb("adaw", [P, 16, 1024], stack=start)
        start.close()
        ffn = ExitStack()
        ah = sb("ah", [P, FT, 2 * T], f32r, stack=ffn)
        sg = sb("sg", [P, 2, T], stack=ffn)
        af = sb("af", [P, 2, T], stack=ffn)
        ffn.close()
        ret = ExitStack()
        rqk = sb("rqk", [P, 16, T], stack=ret)
        rv = sb("rv", [P, 2, 2048], stack=ret)
        rvT = sb("rvT", [P, 2, T], stack=ret)
        rg = sb("rg", [P, 16, T], stack=ret)
        rp = sb("rp", [P, 2, 384], stack=ret)
        rcos = sb("rcos", [P, T], stack=ret)
        rsin = sb("rsin", [P, T], stack=ret)
        dec = sb("dec", [P, 4, T], stack=ret)
        rmu = sb("rmu", [P, T], stack=ret)
        yr = sb("yr", [P, 16, 2 * T], f32r, stack=ret)
        ret.close()
        first.close()
        second = ExitStack()
        dist = sb("dist", [P, 3, 384], stack=second)
        bones = sb("bones", [P, P], stack=second)
        lcs = sb("lcs", [P, 2, 2, 16], stack=second)
        rows = sb("rows", [P, LAYERS2, 2, 96], stack=second)
        dqk = sb("dqk", [P, 24, T], stack=second)
        dv = sb("dv", [P, 2, 1536], stack=second)
        qkT = sb("qkT", [96, 8, 2 * T], stack=second)
        vm = sb("vm", [P, 2, 512], stack=second)
        bz = sb("bz", [P, 4, T], stack=second)
        cz = sb("cz", [P, 4, T], stack=second)
        sn = sb("sn", [P, 2, 3, 384], stack=second)
        bias = sb("bias", [P, 2, 384], stack=second)
        pt2 = sb("pt2", [P, 3, 384], stack=second)
        mn2 = sb("mn2", [P, 2, 2, 3], stack=second)
        mj = sb("mj", [P, 2, 2], stack=second)
        rs2 = sb("rs2", [P, 2, 2, 3], stack=second)
        rj = sb("rj", [P, 4, 2], stack=second)
        hpair = sb("hpair", [P, T], stack=second)
        s32 = sb("s32", [P, 32], stack=second)
        ua = sb("ua", [P, 2 + T], stack=second)
        at = sb("at", [P, 5, T], stack=second)
        over = ExitStack()
        cF = sb("cF", [P, 3, T], stack=over)
        csq = sb("csq", [P, 3, T], stack=over)
        cr = sb("cr", [P, 2, T], stack=over)
        kpT = sb("kpT", [32, T], stack=over)
        kpe = sb("kpe", [P, 2, 32], stack=over)
        qk = sb("qk", [P, 2, 2, 8 * 96], stack=over)
        over.close()
        yh = sb("yh", [P, 12, 2 * T], f32r, stack=second)
        second.close()
        wuq = sn[:, :, :, :].rearrange("p a b c -> p (a b c)")[:, 0:1536].rearrange("p (k n) -> p k n", k=2)
        wkv = pt2[:, :, :].rearrange("p a b -> p (a b)")[:, 0:1024]
        mh_stack = ExitStack()
        for n, t in (("o_dist", [P, 3, 384]), ("o_bones", [P, P]), ("o_lcs", [P, 2, 2, 16]),
                     ("o_rows", [P, LAYERS2, 2, 96])):
            sb(n, t, stack=mh_stack)
        mh = sb("mh", [P, KT, 2 * T], f32r, stack=mh_stack)
        th = sb("th", [P, 6, T], stack=mh_stack)
        mg = sb("mg", [P, 2, T], stack=mh_stack)
        mh_stack.close()
        sq2 = ExitStack()
        for n, t in (("o2_dist", [P, 3, 384]), ("o2_bones", [P, P]), ("o2_lcs", [P, 2, 2, 16]),
                     ("o2_rows", [P, LAYERS2, 2, 96]), ("o2_dqk", [P, 24, T]), ("o2_dv", [P, 2, 1536])):
            sb(n, t, stack=sq2)
        qks = sb("qks", [P, 2, 2, 8 * 96], stack=sq2)
        sq2.close()

        w_raw = [sem(f"w_raw{i}") for i in range(4)]
        w_hi, w_lo = sem("w_hi"), sem("w_lo")
        blk_done = sem("blk_done")
        slot_free = [sem(f"slot_free{i}") for i in range(4)]
        sq_ready = sem("sq_ready")
        sq_summed = sem("sq_summed")
        ss_done = sem("ss_done")
        ln_done = sem("ln_done")
        rstd_ready = sem("rstd_ready")
        t_ready = sem("t_ready")
        hi_ready = sem("hi_ready")
        h_ready = sem("h_ready")
        s_done, s_free = sem("s_done"), sem("s_free")
        t_done, t_free = sem("t_done"), sem("t_free")
        o_done, o_free = sem("o_done"), sem("o_free")
        o_hi = sem("o_hi")
        in_c, in_ones = sem("in_c"), sem("in_ones")
        in_x, in_cols, in_const, in_att = sem("in_x"), sem("in_cols"), sem("in_const"), sem("in_att")
        in_ret, in_hyb, in_small = sem("in_ret"), sem("in_hyb"), sem("in_small")
        ada_raw = [sem(f"ada_raw{i}") for i in range(4)]
        ada_first = [sem(f"ada_first{i}") for i in range(len(FIRST))]
        ada_acc = sem("ada_acc")
        ada_used = sem("ada_used")
        mod_ready = sem("mod_ready")
        exp_c, silu_c = sem("exp_c"), sem("silu_c")
        rope_ready = sem("rope_ready")
        sb_ln, sb_sp, sb_a = sem("sb_ln"), sem("sb_sp"), sem("sb_a")
        p_ready, pn_ready = sem("p_ready"), sem("pn_ready")
        ah_hi, ah_ready = sem("ah_hi"), sem("ah_ready")
        r_sc, r_pt, r_o, r_of = sem("r_sc"), sem("r_pt"), sem("r_o"), sem("r_of")
        r_c, r_sq, r_norm, r_y, r_hi, r_lo = (sem(n) for n in ("r_c", "r_sq", "r_norm", "r_y", "r_hi", "r_lo"))
        c_ready, cn_ready = sem("c_ready"), sem("cn_ready")
        qk_in, qk_sq, qk_ss, qk_rs, qk_ready = (sem(n) for n in ("qk_in", "qk_sq", "qk_ss", "qk_rs", "qk_ready"))
        d_sq, d_rs, d_norm = sem("d_sq"), sem("d_rs"), sem("d_norm")
        mj_ready = sem("mj_ready")
        bias_ready = sem("bias_ready")
        tanh_ready = sem("tanh_ready")
        a_ready = sem("a_ready")
        y_hi, y_lo = sem("y_hi"), sem("y_lo")
        half_done = sem("half_done")
        m_ready, m_hi, m_lo = sem("m_ready"), sem("m_hi"), sem("m_lo")
        lcol_ready = sem("lcol_ready")
        dve_own, act_own, pool_own = sem("dve_own"), sem("act_own"), sem("pool_own")
        stored = sem("stored")

        def gslot(g):
            return G[:, g % 2, 0:T]

        def att_out(p):
            return O[:, 0:T] if p < 5 else S[:, p - 5, 0:T]

        def taken(g, r4=0):
            return g // 4 + 1 + r4

        block = ctx.enter_context(nc.Block())

        @block.sync
        def _(sp_):
            sp_.dma_start(silc[:, 0:8], a["c"]).then_inc(in_c, 16)
            for q, (n0, n1) in enumerate(FIRST):
                sp_.dma_start(adaw[:, n0:n1, :], a["ada"][n0:n1].rearrange("n p c -> p n c")).then_inc(ada_first[q], 16)
                if q == 0:
                    sp_.dma_start(ones[:, :], a["ones"]).then_inc(in_ones, 16)
                    sp_.dma_start(cols[:, :], a["cols"]).then_inc(in_cols, 16)
                    sp_.dma_start(x[:, :, :], a["x"]).then_inc(in_x, 16)
            for s in range(4):
                sp_.dma_start(raw[:, s, :], a["w"][s]).then_inc(w_raw[s], 16)
            with sp_.Fori(1, N_BLOCKS // 4) as t:
                for s in range(4):
                    sp_.wait_ge(w_lo, t * 4 - 3 + s)
                    sp_.dma_start(raw[:, s, :], a["w"][t * 4 + s]).then_inc(w_raw[s], 16)
            for m in range(1, KT, 2):
                for g in (G_END - KT + m - 1, G_END - KT + m):
                    sp_.wait_ge(slot_free[g % 4], taken(g))
                sp_.dma_start(out[:, m - 1:m + 1, :], x[:, m - 1:m + 1, :]).then_inc(stored, 16)
            sp_.wait_ge(stored, 16 * KT // 2)

        @block.gpsimd
        def _(pool):
            chain = Chain(pool, pool_own)
            pool.wait_ge(ada_acc, 2)
            for s in range(4):
                pool.dma_start(araw[:, s, :], a["ada"][16 + s]).then_inc(ada_raw[s], 16)

            def times_c(dst, w, k):
                return pool.tensor_tensor(dst, w, silc[:, 16 + k:17 + k].broadcast_to([P, 1024]), ALU.mult)

            def pair(v2, last):
                chain.restart()
                for half in range(2):
                    for k in range(8):
                        n = 8 * half + k
                        s = n % 4
                        pool.wait_ge(ada_raw[s], v2 * 64 - 48 + 16 * (n // 4))
                        if k == 0:
                            pool.wait_ge(mod_ready, v2 * 2 + half - 1)
                            ins = times_c(acc[:, half, :], araw[:, s, :], 0)
                        else:
                            chain.link(times_c(araw[:, s, :], araw[:, s, :], k))
                            ins = pool.tensor_tensor(acc[:, half, :], acc[:, half, :], araw[:, s, :], ALU.add)
                        if k < 7:
                            chain.link(ins)
                        else:
                            ins.then_inc(ada_acc, 1)
                            pool.wait_ge(ada_acc, v2 * 2 + half + 1)
                        if not (last and n >= 12):
                            pool.dma_start(araw[:, s, :], a["ada"][v2 * 16 + (n + 4)]).then_inc(ada_raw[s], 16)

            with pool.Fori(1, 5) as v2:
                pair(v2, False)
            pair(5, True)
            pool.wait_ge(t_ready, 33)
            pool.dma_start(bones[:, :], a["bones"]).then_inc(in_hyb, 16)
            pool.dma_start(dist[:, :, :], a["dist"]).then_inc(in_hyb, 16)
            pool.dma_start(lcs[:, :, :, :], a["lcs"]).then_inc(in_hyb, 16)
            pool.dma_start(rows[:, :, :, :], a["rows"]).then_inc(in_hyb, 16)
            pool.wait_ge(in_hyb, 64)
            with pool.Fori(0, LAYERS2) as l:
                for j in range(24):
                    head, grp = j // 3, j % 3
                    k = j - 2
                    pool.wait_ge(s_free, L1_S + l * HYB_S + (score_uses(8 + k // 3) - 2 + k % 3 if j >= 2 else 0))
                    c = 8 * grp + head
                    pool.tensor_tensor(bias[:, j % 2, :], dist[:, grp, :], slopes[:, c:c + 1].broadcast_to([P, 384]),
                                       ALU.mult).then_inc(bias_ready, 1)

        @block.tensor
        def _(pe):
            def run(b, g, n_out, k_of, moving, b4=0, g4=0, each_k=None, each_out=None, half=None):
                t = 0
                for m in range(n_out):
                    if g + m >= 2:
                        pe.wait_ge(slot_free[(g + m - 2) % 4], taken(g + m - 2) + g4)
                    o = gslot(g + m)
                    for k in range(k_of):
                        c = t % 8
                        slot = (b + t // 8) % 4
                        if c == 0:
                            pe.wait_ge(w_lo, b + t // 8 + 1 + 4 * b4)
                        if each_k is not None and m == 0:
                            each_k(k)
                        mv = moving(m, k)
                        wh, wl = whi[:, slot, c * P:(c + 1) * P], wlo[:, slot, c * P:(c + 1) * P]
                        pe.matmul(o, wh, mv[:, 0:T], start=(k == 0), stop=False)
                        pe.matmul(o, wh, mv[:, T:2 * T], start=False, stop=False)
                        ins = pe.matmul(o, wl, mv[:, 0:T], start=False, stop=(k == k_of - 1))
                        t += 1
                        if t % 8 == 0:
                            ins.then_inc(blk_done, 1)
                        elif half is not None and k == k_of - 1:
                            ins.then_inc(half, 1)
                    if each_out is not None:
                        each_out(m)
                assert t % 8 == 0

            def run_two(b, g, base, b4=0, g4=0):
                o = [gslot(g), gslot(g + 1)]
                for n in range(2):
                    if g + n >= 2:
                        pe.wait_ge(slot_free[(g + n - 2) % 4], taken(g + n - 2) + g4)
                pe.wait_ge(w_lo, b + 2 + 4 * b4)
                for k in range(KT):
                    pe.wait_ge(hi_ready, base + k + 1)
                    for n in range(2):
                        slot = (b + n) % 4
                        for w in (whi, wlo):
                            pe.matmul(o[n], w[:, slot, k * P:(k + 1) * P], h[:, k, 0:T], start=(k == 0 and w is whi),
                                      stop=False)
                for n in range(2):
                    for k in range(KT):
                        if n == 0:
                            pe.wait_ge(h_ready, base + k + 1)
                        ins = pe.matmul(o[n], whi[:, (b + n) % 4, k * P:(k + 1) * P], h[:, k, T:2 * T], start=False,
                                        stop=(k == KT - 1))
                    ins.then_inc(blk_done, 1)

            def sum_squares(base, k):
                pe.wait_ge(sq_ready, base + k + 1)
                ins = pe.matmul(S[:, 2, 0:T], ones[:, :], sq[:, k, :], start=(k == 0), stop=(k == KT - 1))
                if k == KT - 1:
                    ins.then_inc(ss_done, 1)

            def vectors_at(vectors):
                def hook(m):
                    if m in (5, 6):
                        ada(vectors[m - 5])
                return hook

            def sum_of_squares(n):
                pe.wait_ge(sq_summed, n)
                pe.matmul(S[:, 2, 0:T], ones[:, :], sq[:, 0, :], start=True, stop=False)
                pe.wait_ge(sq_ready, 8 * n + KT)
                pe.matmul(S[:, 2, 0:T], ones[:, :], sq[:, KT - 1, :], start=False, stop=True).then_inc(ss_done, 1)

            def ada(v, slot=None):
                pe.wait_ge(ada_acc, v + 1)
                if slot is None and v:
                    pe.wait_ge(mod_ready, v)
                for m in range(8):
                    ins = pe.matmul(S[:, slot or 0, m:m + 1], acc[:, v % 2, m * P:(m + 1) * P], ones[:, 0:1],
                                    start=True, stop=True)
                ins.then_inc(ada_used if slot is None else s_done, 1)

            def of_h(m, k):
                return h[:, k, :]

            s_ring, t_ring, o_ring = Ring(3), Ring(2), Ring(1)

            def use_s():
                slot, freed, _ = s_ring.next()
                if not (isinstance(freed, int) and freed == 0):
                    pe.wait_ge(s_free, freed)
                return slot

            def use_t():
                slot, freed, _ = t_ring.next()
                if not (isinstance(freed, int) and freed == 0):
                    pe.wait_ge(t_free, freed)
                return slot

            def pv_head(odd, parts, ready, bank=None):
                to = O if bank is None else bank
                if not odd and bank is None:
                    _, freed, _ = o_ring.next()
                    if not (isinstance(freed, int) and freed == 0):
                        pe.wait_ge(o_free, freed)
                pe.wait_ge(*ready)
                o = 64 * odd
                for n, (v0, v1, p_) in enumerate(parts):
                    pe.matmul(to[o:o + 64, 0:T], v0, p_[:, 0:T], start=(n == 0), stop=False)
                    ins = pe.matmul(to[o:o + 64, P:T], v1, p_[:, T:384], start=False,
                                    stop=(n == len(parts) - 1))
                if odd:
                    ins.then_inc(o_done, 1)

            def transposes_v(src):
                slot = use_t()
                for j in range(2):
                    ins = pe.transpose(Tp[:, slot, j * P:(j + 1) * P], src[:, j * P:(j + 1) * P], ident[:, :])
                ins.then_inc(t_done, 1)

            def transposes_p(src):
                slot = use_t()
                for j in range(3):
                    ins = pe.transpose(Tp[:, slot, j * P:(j + 1) * P], src[:, j * P:(j + 1) * P], ident[:, :])
                ins.then_inc(t_done, 1)

            pe.wait_ge(in_ones, 16)
            for k in range(KT):
                sum_squares(0, k)
            ada(0)
            ada(1)

            def sb_scores(hh):
                g = 13 + 2 * (hh // 2)
                pe.wait_ge(slot_free[g % 4], taken(g))
                slot = use_s()
                t, o = hh // 2, 64 * (hh % 2)
                kk, qq = sqk[o:o + 64, 4 + t, :], sqk[o:o + 64, t, :]
                pe.matmul(S[:, slot, 0:T], kk[:, 0:P], qq, start=True, stop=True)
                pe.matmul(S[:, slot, T:384], kk[:, P:T], qq[:, P:T], start=True, stop=True).then_inc(s_done, 1)

            def sb_sums(hh):
                slot = use_s()
                pe.wait_ge(sb_sp, hh // 4 + 1)
                pe.matmul(S[:, slot, T:384], usum[:, :], sp[:, hh, T:384], start=True, stop=True)
                pe.matmul(S[:, slot, 0:T], usum[:, :], sp[:, hh, 0:T], start=True, stop=False)
                pe.matmul(S[:, slot, P:T], ones[:, :], sp[:, hh, T:384], start=False, stop=True).then_inc(s_done, 1)

            def v_of_att(t):
                g = 8 + t if t < 4 else 16 + t
                pe.wait_ge(slot_free[g % 4], taken(g))
                transposes_v(vT[:, t % 4, :])

            def sb_pair(p):
                pe.wait_ge(t_free, 12 + p + 1)
                if p:
                    pe.wait_ge(s_free, L1_S)
                for hh in (2 * p, 2 * p + 1):
                    c = 64 * hh
                    pv_head(hh % 2, [(vtok[:, 0, c:c + 64], vtok[:, 1, c:c + 64], zs[:, hh, :])], (sb_a, hh + 1),
                            S[:, p - 1, :] if p else None)

            def moba_scores(i):
                slot = use_s()
                g, o = i // 4, 32 * (i % 4)
                q = [mro[o:o + 32, 2 * half + g, :] for half in range(2)]
                kk = [mro[o:o + 32, 4 + 2 * half + g, :] for half in range(2)]
                for half in range(2):
                    pe.matmul(S[:, slot, 0:P], q[half][:, 0:P], kk[half][:, 0:P], start=(half == 0), stop=(half == 1))
                for half in range(2):
                    ins = pe.matmul(S[:, slot, P:384], q[half][:, P:T], kk[half], start=(half == 0), stop=(half == 1))
                ins.then_inc(s_done, 1)

            for b in range(24):
                i = b - 12
                if i == 0:
                    pe.wait_ge(rope_ready, 2)
                if 0 <= i < 8:
                    moba_scores(i)
                if 1 <= i <= 8:
                    pe.wait_ge(pn_ready, i)
                    transposes_p(pr[:, (i - 1) % 2, :])
                if b in (15, 17, 19, 21):
                    sb_scores(b - 15)
                    sb_scores(b - 14)
                if b == 0:
                    run_two(B_QKV, G_QKV, 0)
                elif b > 1:
                    run(B_QKV + b, G_QKV + b, 1, 8, of_h)
                if 1 <= i <= 8:
                    j, col = i - 1, 512 + 64 * (i - 1)
                    pv_head(j % 2, [(vtok[:, 0, col:col + 64], vtok[:, 1, col:col + 64], pt[:, j % 2, :])],
                            (t_free, 4 + j + 1))
                if 9 <= b <= 12:
                    v_of_att(b - 9)
                if 21 <= b:
                    v_of_att(b - 17)
                if b == 14:
                    pe.wait_ge(in_att, 64)
                if b == 20:
                    ada(2, use_s())
                if b == 23:
                    sb_pair(0)
                if b in (21, 23):
                    for hh in range(2 * b - 42, 2 * b - 38):
                        sb_sums(hh)
            v_of_att(7)
            for p in range(1, 4):
                sb_pair(p)

            run(B_ATT_O, G_ATT_O, 8, 8, lambda m, k: oh[:, k, :],
                each_k=lambda k: pe.wait_ge(o_free, 5 + k % 4), each_out=vectors_at((3, 4)))
            sum_of_squares(1)

            def ffn(b, g, n):
                run_two(b, g, 8 * n)
                run(b + 2, g + 2, 2, 8, of_h)
                with pe.Fori(1, FT // 2) as i:
                    run(b, g, 4, 8, of_h, b4=i, g4=i)

            def down(b, g, f, n, vectors):
                run(b, g, 8, FT, lambda m, k: ah[:, k, :], each_k=lambda k: pe.wait_ge(ah_ready, FT * f + k + 1),
                    each_out=vectors_at(vectors) if vectors else None)
                sum_of_squares(n)

            ffn(B_FFN0, G_FFN0, 1)
            ada(5)
            down(B_DOWN0, G_DOWN0, 0, 2, (6, 7))

            def ret_scores(hh):
                if hh == 0:
                    pe.wait_ge(rope_ready, 4)
                else:
                    pe.wait_ge(r_pt, hh)
                for o, r in ((0, slice(0, T)), (T, slice(P, T))):
                    for half in range(2):
                        kk = rqk[:, 8 + 2 * hh + half, P if o else 0:T if o else P]
                        q = rqk[:, 2 * hh + half, r]
                        ins = pe.matmul(S[:, 0, o:o + r.stop - r.start], kk, q, start=(half == 0), stop=(half == 1))
                ins.then_inc(r_sc, 1)

            def ret_out(hh):
                pe.wait_ge(r_pt, hh + 1)
                if hh == 0:
                    pe.wait_ge(t_free, 32)
                else:
                    pe.wait_ge(r_of, hh)
                for m in range(4):
                    o = S[:, 1 + m // 2, (m % 2) * T:(m % 2 + 1) * T]
                    c = 512 * hh + P * m
                    pe.matmul(o, rv[:, 0, c:c + P], rp[:, hh % 2, 0:T], start=True, stop=False)
                    ins = pe.matmul(o[:, P:T], rv[:, 1, c:c + P], rp[:, hh % 2, T:384], start=False, stop=True)
                ins.then_inc(r_o, 1)

            def ret_sum(src, sem_, n):
                slot = use_t()
                pe.wait_ge(sem_, n)
                for m in range(4):
                    ins = pe.matmul(Tp[:, slot, 0:T], ones[:, :], sq[:, src + m, :], start=(m == 0), stop=(m == 3))
                ins.then_inc(t_done, 1)

            for b in range(48):
                if b == 0:
                    run_two(B_RET, G_RET, 16)
                elif b > 1:
                    run(B_RET + b, G_RET + b, 1, 8, of_h)
                if b == 24:
                    ada(8)
                if 17 <= b < 33:
                    g = G_RET + b - 1
                    pe.wait_ge(slot_free[g % 4], taken(g))
                    transposes_v(rvT[:, (b - 17) % 2, :])
                if b in RET_PARTS:
                    for hh, part in RET_PARTS[b]:
                        if part == 0:
                            ret_scores(hh)
                        elif part == 1:
                            ret_out(hh)
                        elif part == 2:
                            ret_sum(0, r_of, hh + 1)
                        else:
                            ret_sum(4, r_sq, hh + 1)
            ret_sum(4, r_sq, 4)
            run(B_RET_O, G_RET_O, 8, 16, lambda m, k: yr[:, k, :],
                each_k=lambda k: pe.wait_ge(r_lo, k // 4 + 1), each_out=vectors_at((9, 10)))
            sum_of_squares(3)
            ffn(B_FFN1, G_FFN1, 3)
            ada(11)
            down(B_DOWN1, G_DOWN1, 1, 4, None)

            with pe.Fori(0, LAYERS2) as l:
                b4, g4 = l * (HYB_BLOCKS // 4), l * (HYB_TILES // 4)
                s_ring = Ring(3, L1_S + l * HYB_S)
                t_ring = Ring(2, L1_T + l * HYB_T)
                o_ring = Ring(1, L1_O + l * HYB_O)
                t_base = L1_T + l * HYB_T

                def use_s():
                    slot, freed, _ = s_ring.next()
                    pe.wait_ge(s_free, freed)
                    return slot

                def use_t():
                    slot, freed, _ = t_ring.next()
                    pe.wait_ge(t_free, freed)
                    return slot

                def head_out(odd, parts, ready):
                    if not odd:
                        _, freed, _ = o_ring.next()
                        pe.wait_ge(o_free, freed)
                    pe.wait_ge(*ready)
                    for qt in range(2):
                        o = O[:, P * odd + HD * qt:P * odd + HD * qt + HD]
                        terms = [(p_[:, P * (qt + kt):P * (qt + kt + 1)], v[kt]) for *v, p_ in parts for kt in range(qt + 1)]
                        for n, (w, v) in enumerate(terms):
                            ins = pe.matmul(o, w, v, start=(n == 0), stop=(n == len(terms) - 1))
                    if odd:
                        ins.then_inc(o_done, 1)

                def pair_back(p):
                    slot = use_s()
                    pe.wait_ge(o_free, L1_O + l * 8 + p + 1)
                    for qt in range(2):
                        ins = pe.transpose(S[:, slot, qt * P:(qt + 1) * P], at[:, 4, qt * P:(qt + 1) * P], ident[:, :])
                    ins.then_inc(s_done, 1)

                def to_keys(src, n):
                    slot = use_t()
                    for j in range(n):
                        ins = pe.transpose(Tp[:, slot, j * P:(j + 1) * P], src[:, j * P:(j + 1) * P], ident[:, :])
                    ins.then_inc(t_done, 1)

                def block1(j):
                    run(B_HYB + j, G_HYB + j, 1, 8, of_h, b4=b4, g4=g4)

                for k in range(KT):
                    sum_squares(40 + l * 8, k)
                run_two(B_HYB, G_HYB, 32 + l * 8, b4, g4)
                for j in (2, 3):
                    block1(j)
                for tiles in ((0, 1), (2,)):
                    slot = use_t()
                    j = tiles[-1]
                    pe.wait_ge(slot_free[(G_HYB + j) % 4], taken(G_HYB + j) + g4)
                    for k in tiles:
                        ins = pe.matmul(Tp[:, slot, 0:T], ones[:, :], csq[:, k, :], start=(k == tiles[0]),
                                        stop=(k == tiles[-1]))
                    ins.then_inc(t_done, 1)
                slot = use_t()
                pe.wait_ge(slot_free[(G_HYB + 3) % 4], taken(G_HYB + 3) + g4)
                for j in range(2):
                    ins = pe.matmul(Tp[:, slot, 32 * j:32 * j + 32], kpT[:, j * P:(j + 1) * P], ident[0:32, 0:32],
                                    start=True, stop=True)
                ins.then_inc(t_done, 1)
                for j in range(4, 8):
                    block1(j)

                def mla_projections():
                    pe.wait_ge(cn_ready, l + 1)
                    pe.wait_ge(in_small, l * 32 + 32)
                    for tt in range(2):
                        for half in range(2):
                            slot = use_s()
                            for k in range(2):
                                ins = pe.matmul(S[:, slot, 0:384], cF[:, k, tt * P:(tt + 1) * P],
                                                wuq[:, k, 384 * half:384 * half + 384], start=(k == 0), stop=(k == 1))
                            ins.then_inc(s_done, 1)
                    for half in range(2):
                        for tt in range(2):
                            slot = use_s()
                            pe.matmul(S[:, slot, :], cF[:, 2, tt * P:(tt + 1) * P], wkv[:, 512 * half:512 * half + 512],
                                      start=True, stop=True).then_inc(s_done, 1)

                def mla_transposes(hh):
                    slot = use_t()
                    pe.wait_ge(qk_ready, l + 1)
                    for n in range(2):
                        for tt in range(2):
                            ins = pe.transpose(Tp[0:96, slot, (2 * n + tt) * P:(2 * n + tt + 1) * P],
                                               qk[:, n, tt, 96 * hh:96 * hh + 96], ident[:, :])
                    ins.then_inc(t_done, 1)

                def d_sums(j):
                    slot = use_t()
                    pe.wait_ge(d_sq, l * 24 + j + 1)
                    pe.matmul(Tp[:, slot, 0:T], bones[:, :], sq[:, j % 8, :], start=True, stop=True).then_inc(t_done, 1)

                pe.wait_ge(in_hyb, 64)
                for j in range(24):
                    block1(H_DQ + j)
                    if j >= 1:
                        d_sums(j - 1)
                    if j == 2:
                        mla_projections()
                    if j >= 16:
                        mla_transposes(j - 16)
                for j in range(12):
                    block1(H_DV + j)
                    if j == 0:
                        d_sums(23)
                    else:
                        g = G_HYB + H_DV + j - 1
                        pe.wait_ge(slot_free[g % 4], taken(g) + g4)
                        to_keys(at[:, (j - 1) % 4, :], 2)

                def scores2(i, grp):
                    slot = use_s()
                    if i < 8:
                        q, kk = qkT[:, i, 0:T], qkT[:, i, T:2 * T]
                    else:
                        o, t = 64 * (i % 2), (i - 8) // 2
                        q, kk = dqk[o:o + 64, 4 * grp + t, :], dqk[o:o + 64, 12 + 4 * grp + t, :]
                    pe.matmul(S[:, slot, 0:P], q[:, 0:P], kk[:, 0:P], start=True, stop=True)
                    pe.matmul(S[:, slot, P:384], q[:, P:T], kk, start=True, stop=True).then_inc(s_done, 1)

                def out2(i):
                    if i < 8:
                        parts = [(vm[:, 0, 64 * i:64 * i + 64], vm[:, 1, 64 * i:64 * i + 64], pt2[:, 0, :])]
                        n = i + 1
                    else:
                        cs = [512 * grp + 64 * (i - 8) for grp in range(3)]
                        parts = [(dv[:, 0, c:c + 64], dv[:, 1, c:c + 64], pt2[:, grp, :]) for grp, c in enumerate(cs)]
                        n = 8 + 3 * (i - 7)
                    head_out(i % 2, parts, (t_free, t_base + (HYB_T - 32 + n)))

                for i in range(17):
                    if i == 0:
                        g = G_HYB + H_CZ - 1
                        pe.wait_ge(slot_free[g % 4], taken(g) + g4)
                        to_keys(at[:, 3, :], 2)
                        block1(BESIDE[0][0])
                        pe.wait_ge(t_free, t_base + (HYB_T - 32))
                        pe.wait_ge(d_norm, l * 24 + 24)
                    n_scores = 0 if i == 16 else 1 if i < 8 else 3
                    n_back = 0 if i == 0 else 1 if i <= 8 else 3
                    for grp in range(3):
                        if grp < n_scores:
                            scores2(i, grp)
                        if grp < n_back:
                            if grp == 0:
                                pe.wait_ge(p_ready, 8 + l * 16 + i)
                            to_keys(sn[:, (i - 1) % 2, grp, :], 3)
                    for j in BESIDE[i][1 if i == 0 else 0:]:
                        block1(j)
                    if i >= 3 and i % 2:
                        pair_back((i - 3) // 2)
                    if i >= 1:
                        out2(i - 1)

                for mm in range(4):
                    for r in range(3):
                        bb, n = B_HYB + H_MERGE + 9 * mm + 3 * r, G_HYB + H_MERGE + 12 * mm + 4 * r
                        run(bb, n, 1, 8, of_h, b4=b4, g4=g4)
                        if mm == 0 and r == 0:
                            pair_back(7)
                        run(bb + 1, n + 1, 1, 8, of_h, b4=b4, g4=g4)
                        if mm == 0 and r == 0:
                            pe.wait_ge(y_lo, l * 12 + 12)
                        run(bb + 2, n + 2, 2, 4, lambda m, k: yh[:, 4 * ((2 * r + m) % 3) + k, :], b4=b4, g4=g4,
                            half=half_done)
                run(B_HYB + H_WO, G_HYB + H_MERGE + 48, 8, 8, lambda m, k: mh[:, k, :], b4=b4, g4=g4,
                    each_k=lambda k: pe.wait_ge(m_lo, l * 8 + k + 1))

        @block.scalar
        def _(act):
            chain = Chain(act, act_own)

            def hi(n, r4=0):
                s = n % 4
                act.wait_ge(w_raw[s], 16 * (n // 4 + 1) + 16 * r4)
                if n >= 4:
                    act.wait_ge(blk_done, n - 3 + 4 * r4)
                act.activation(whi[:, s, :], raw[:, s, :], ACT.Copy).then_inc(w_hi, 1)

            def square_x(k):
                act.activation(sq[:, k, :], x[:, k, :], ACT.Square).then_inc(sq_ready, 1)

            def root(n):
                act.wait_ge(ss_done, n + 1)
                act.activation(rstd[:, :], S[:, 2, 0:T], ACT.Ln, bias=EPS, scale=1.0 / D).then_inc(ln_done, 1)
                act.wait_ge(ln_done, n + 1)
                act.activation(rstd[:, :], rstd[:, :], ACT.Exp, scale=-0.5).then_inc(rstd_ready, 1)

            def norm_hi(base_t, base_h, shift):
                for k in range(KT):
                    act.wait_ge(t_ready, base_t + k + 1)
                    if shift is None:
                        ins = act.activation(h[:, k, 0:T], sq[:, k, :], ACT.Copy)
                    else:
                        ins = act.activation(h[:, k, 0:T], sq[:, k, :], ACT.Identity, bias=mod[:, shift + k:shift + k + 1])
                    ins.then_inc(hi_ready, 1)

            t_ring = Ring(2)

            def evac_t(dst, n=384, scale=1.0):
                slot, _, done = t_ring.next()
                act.wait_ge(t_done, done)
                act.activation(dst, Tp[:, slot, 0:n], ACT.Copy, scale=scale).then_inc(t_free, 1)

            def evac_v(dst):
                slot, _, done = t_ring.next()
                act.wait_ge(t_done, done)
                act.activation(dst, Tp[:, slot, 0:T].rearrange("p (j c) -> p j c", j=2), ACT.Copy).then_inc(t_free, 1)

            act.preload_act_table_set(LNEXP)
            act.wait_ge(in_c, 16)
            act.activation(silc[:, 8:16], silc[:, 0:8], ACT.Exp, scale=-1.0).then_inc(exp_c, 1)
            act.wait_ge(in_x, 16)
            for dst, name in ((ident, "ident"), (cmask, "cmask"), (slopes, "slopes")):
                act.dma_start(dst[:, :], a[name]).then_inc(in_const, 16)
            for dst, name in ((usum, "usum"), (sbm, "sbm"), (mcos, "mcos"), (msin, "msin")):
                act.dma_start(dst[:, :], a[name]).then_inc(in_att, 16)
            for k in range(KT):
                square_x(k)
            root(0)
            for n in range(2):
                hi(n)
            norm_hi(0, 0, 0)
            for n in range(2, 4):
                hi(n)

            def softplus_part(g2):
                z4 = zs[:, 4 * g2:4 * g2 + 4, :]
                s4 = sp[:, 4 * g2:4 * g2 + 4, :]
                act.wait_ge(s_free, ATT_S.index(f"z{4 * g2 + 3}") + 1)
                chain.link(act.activation(s4, z4, ACT.Abs))
                chain.link(act.activation(s4, s4, ACT.Exp, scale=-1.0))
                act.activation(s4, s4, ACT.Ln, bias=1.0).then_inc(sb_ln, 1)

            def sb_weights(hh):
                act.wait_ge(s_free, ATT_S.index(f"c{hh}") + 1)
                act.activation(zs[:, hh, :], zs[:, hh, :], ACT.Exp).then_inc(sb_a, 1)

            def o_split(p):
                act.wait_ge(o_done, p + 1)
                act.activation(oh[:, (p + 4) % 8, 0:T], att_out(p), ACT.Copy).then_inc(o_hi, 1)

            def moba_exps(i):
                act.wait_ge(s_free, ATT_S.index(f"m{i}") + 1)
                for qt, r in ((0, slice(0, P)), (1, slice(P, 384))):
                    ins = act.activation(pr[:, i % 2, r], pr[:, i % 2, r], ACT.Exp, scale=-1.0,
                                         bias=mn[:, i % 2, qt:qt + 1], accum_out=rs[:, i % 2, qt:qt + 1])
                ins.then_inc(p_ready, 1)

            def qkv_tile(b):
                act.wait_ge(blk_done, b + 1)
                if b < 8:
                    dst, scale = mqk[:, b, :], -HD ** -0.5 if b < 4 else 1.0
                elif 12 <= b < 20:
                    dst, scale = sqk[:, (b - 12) // 2 + 4 * (b % 2), :], 1.0 if b % 2 else HD ** -0.5
                else:
                    dst, scale = vT[:, b % 4, :], 1.0
                act.activation(dst, gslot(b), ACT.Copy, scale=scale).then_inc(slot_free[b % 4], 1)
                hi(b + 4)

            for b in range(25):
                if b in (15, 17, 19, 21):
                    o_split((b - 15) // 2)
                if 10 <= b <= 13 or b >= 22:
                    c = P * (b - 6 if b <= 13 else b - 22)
                    evac_v(vtok[:, :, c:c + P])
                if 13 <= b <= 20:
                    evac_t(pt[:, (b - 13) % 2, :])
                if b >= 1:
                    qkv_tile(b - 1)
                if 12 <= b < 20:
                    moba_exps(b - 12)
                if b in (18, 22):
                    softplus_part(b // 4 - 4)
                if b == 23:
                    for hh in range(4):
                        sb_weights(hh)
            o_split(4)
            evac_v(vtok[:, :, 3 * P:4 * P])
            for hh in range(4, 8):
                sb_weights(hh)
            for p in range(5, 8):
                o_split(p)

            def x_squares(b, n_blocks, g, ends, last=False):
                for bb in range(n_blocks):
                    if bb == 2:
                        act.preload_act_table_set(LNEXP)
                    for m in range(8):
                        if ends[m] == bb:
                            if m < 7 and not last:
                                hi(b + bb + 4)
                            act.wait_ge(slot_free[(g + m) % 4], taken(g + m))
                            square_x(m)
                    if bb not in ends or last:
                        if not (last and bb >= n_blocks - 4):
                            hi(b + bb + 4)

            one_each = list(range(8))
            two_each = [2 * m + 1 for m in range(8)]
            of_down = [-(-FT * (m + 1) // 8) - 1 for m in range(8)]

            x_squares(B_ATT_O, 8, G_ATT_O, one_each)

            def ffn(b, g):
                with act.Fori(0, FT // 2) as i:
                    for q in range(2):
                        gg = g + 2 * q
                        act.wait_ge(blk_done, b + 2 * q + 1 + 4 * i)
                        act.activation(sg[:, q, :], gslot(gg), ACT.Silu).then_inc(slot_free[gg % 4], 1)
                        hi(b + 2 * q + 4, i)
                        hi(b + 2 * q + 5, i)
                        act.wait_ge(slot_free[(gg + 1) % 4], taken(gg + 1) + i)
                        act.activation(ah[:, i * 2 + q, 0:T], af[:, q, :], ACT.Copy).then_inc(ah_hi, 1)

            root(1)
            norm_hi(8, 8, 24)
            hi(B_FFN0 + 3)
            ffn(B_FFN0, G_FFN0)
            x_squares(B_DOWN0, FT, G_DOWN0, of_down)

            root(2)
            norm_hi(16, 16, 48)
            hi(B_RET + 3)
            act.dma_start(rcos[:, :], a["rcos"]).then_inc(in_ret, 16)
            act.dma_start(rsin[:, :], a["rsin"]).then_inc(in_ret, 16)
            act.dma_start(dec[:, :, :], a["dec"]).then_inc(in_ret, 16)

            def ret_part(hh, part):
                if part == 1:
                    act.wait_ge(r_o, hh + 1)
                    if hh == 0:
                        act.wait_ge(rope_ready, 4)
                    else:
                        act.wait_ge(r_lo, hh)
                    act.activation(sq[:, 0:4, :], S[:, 1:3, :].rearrange("p b (m t) -> p (b m) t", m=2),
                                   ACT.Copy).then_inc(r_of, 1)
                elif part == 2:
                    evac_t(rmu[:, :], T, 1.0 / 512)
                    act.wait_ge(r_c, hh + 1)
                    act.activation(sq[:, 4:8, :], sq[:, 0:4, :], ACT.Square).then_inc(r_sq, 1)
                elif part == 3:
                    slot, _, done = t_ring.next()
                    act.preload_act_table_set(LNEXP)
                    act.wait_ge(t_done, done)
                    act.activation(rstd[:, :], Tp[:, slot, 0:T], ACT.Ln, bias=GN_EPS, scale=1.0 / 512).then_inc(t_free, 1)
                    act.wait_ge(t_free, done)
                    act.activation(rstd[:, :], rstd[:, :], ACT.Exp, scale=-0.5).then_inc(r_norm, 1)
                    act.wait_ge(r_y, hh + 1)
                    act.activation(yr[:, 4 * hh:4 * hh + 4, 0:T], sq[:, 0:4, :], ACT.Copy).then_inc(r_hi, 1)

            for b in range(48):
                g = G_RET + b
                act.wait_ge(blk_done, B_RET + b + 1)
                if b < 16:
                    dst, f, scale = rqk[:, b, :], ACT.Copy, 1.0 if b < 8 else 256 ** -0.5
                elif b < 32:
                    dst, f, scale = rvT[:, b % 2, :], ACT.Copy, 1.0
                else:
                    dst, f, scale = rg[:, b - 32, :], ACT.Silu, 1.0
                act.activation(dst, gslot(g), f, scale=scale).then_inc(slot_free[g % 4], 1)
                hi(B_RET + b + 4)
                if 17 <= b < 33:
                    evac_v(rv[:, :, (b - 17) * P:(b - 16) * P])
                for hh, part in RET_PARTS.get(b, ()):
                    ret_part(hh, part)
            ret_part(3, 3)
            x_squares(B_RET_O, 16, G_RET_O, two_each)
            root(3)
            norm_hi(24, 24, 72)
            hi(B_FFN1 + 3)
            ffn(B_FFN1, G_FFN1)

            x_squares(B_DOWN1, FT, G_DOWN1, of_down, last=True)
            root(4)

            with act.Fori(0, LAYERS2) as l:
                chain.restart()
                b4, g4 = l * (HYB_BLOCKS // 4), l * (HYB_TILES // 4)
                t_ring = Ring(2, L1_T + l * HYB_T)
                s_base = L1_S + l * HYB_S

                def wait_t():
                    slot, _, done = t_ring.next()
                    act.wait_ge(t_done, done)
                    return slot

                def next_hi(j):
                    if j + 4 < HYB_BLOCKS:
                        hi(B_HYB + j + 4, b4)

                def done(j):
                    act.wait_ge(blk_done, B_HYB + j + 1 + 4 * b4)

                def freed(ins, j):
                    ins.then_inc(slot_free[(G_HYB + j) % 4], 1)

                for k in range(KT):
                    act.wait_ge(t_ready, 32 + l * 8 + k + 1)
                    last = G_HYB - 8 + k
                    act.wait_ge(slot_free[last % 4], taken(last) + g4)
                    square_x(k)
                    if k in (4, 5):
                        hi(B_HYB + k - 4, b4)
                act.wait_ge(ss_done, l + 6)
                act.activation(rstd[:, :], S[:, 2, 0:T], ACT.Ln, bias=EPS, scale=1.0 / D).then_inc(ln_done, 1)
                act.wait_ge(ln_done, l + 6)
                act.activation(rstd[:, :], rstd[:, :], ACT.Exp, scale=-0.5).then_inc(rstd_ready, 1)
                act.dma_start(wuq, a["uq"][l]).then_inc(in_small, 16)
                act.dma_start(wkv, a["ukv"][l]).then_inc(in_small, 16)
                norm_hi(40 + l * 8, 32 + l * 8, None)
                for j in (2, 3):
                    hi(B_HYB + j, b4)

                for j in range(3):
                    done(j)
                    act.activation(cF[:, j, :], gslot(G_HYB + j), ACT.Copy)
                    freed(act.activation(csq[:, j, :], gslot(G_HYB + j), ACT.Square), j)
                    next_hi(j)
                done(3)
                freed(act.activation(kpT[:, :], gslot(G_HYB + 3)[0:32, :], ACT.Copy), 3)
                next_hi(3)
                for n, width in ((0, 256), (1, 128)):
                    slot = wait_t()
                    act.activation(cr[:, n, :], Tp[:, slot, 0:T], ACT.Ln, bias=EPS, scale=1.0 / width).then_inc(t_free, 1)
                    act.wait_ge(t_free, L1_T + l * HYB_T + n + 1)
                    act.activation(cr[:, n, :], cr[:, n, :], ACT.Exp, scale=-0.5).then_inc(c_ready, 1)
                slot = wait_t()
                act.activation(kpe[:, :, :], Tp[:, slot, 0:64].rearrange("p (j c) -> p j c", j=2),
                               ACT.Copy).then_inc(t_free, 1)
                for j in range(4, 8):
                    done(j)
                    act.activation(bz[:, j - 4, :], gslot(G_HYB + j), ACT.Tanh, scale=0.5).then_inc(tanh_ready, 1)
                    next_hi(j)
                act.preload_act_table_set(LNEXP)

                def d_root(j):
                    slot = wait_t()
                    if j >= 2:
                        act.wait_ge(d_norm, l * 24 + j - 1)
                    act.activation(at[:, j % 2, :], Tp[:, slot, 0:T], ACT.Ln, bias=EPS, scale=1.0 / HD).then_inc(t_free, 1)
                    act.wait_ge(t_free, L1_T + l * HYB_T + t_ring.n)
                    act.activation(at[:, j % 2, :], at[:, j % 2, :], ACT.Exp, scale=-0.5).then_inc(d_rs, 1)

                for j in range(24):
                    done(H_DQ + j)
                    act.activation(sq[:, j % 8, :], gslot(G_HYB + H_DQ + j), ACT.Square).then_inc(d_sq, 1)
                    freed(act.activation(dqk[:, j, :], gslot(G_HYB + H_DQ + j), ACT.Copy), H_DQ + j)
                    next_hi(H_DQ + j)
                    if j >= 1:
                        d_root(j - 1)
                    if j == 3:
                        act.wait_ge(qk_in, l + 1)
                        act.activation(qks[:, :, :, :], qk[:, :, :, :], ACT.Square).then_inc(qk_sq, 1)
                    if j == 6:
                        act.wait_ge(qk_ss, l + 1)
                        chain.link(act.activation(s32[:, :], s32[:, :], ACT.Ln, bias=EPS, scale=1.0 / 96))
                        act.activation(s32[:, :], s32[:, :], ACT.Exp, scale=-0.5).then_inc(qk_rs, 1)
                    if j >= 16:
                        slot = wait_t()
                        act.activation(qkT[:, j - 16, :], Tp[0:96, slot, :], ACT.Copy).then_inc(t_free, 1)

                def evac_dv(t):
                    slot = wait_t()
                    act.activation(dv[:, :, t * P:(t + 1) * P], Tp[:, slot, 0:T].rearrange("p (j c) -> p j c", j=2),
                                   ACT.Copy).then_inc(t_free, 1)

                for j in range(12):
                    done(H_DV + j)
                    if j < 2:
                        act.wait_ge(d_norm, l * 24 + 23 + j)
                    freed(act.activation(at[:, j % 4, :], gslot(G_HYB + H_DV + j), ACT.Copy), H_DV + j)
                    next_hi(H_DV + j)
                    if j == 0:
                        d_root(23)
                    else:
                        evac_dv(j - 1)
                evac_dv(11)

                act.preload_act_table_set("exp_and_others")
                def exps(i):
                    s = i % 2
                    if i < 8:
                        act.wait_ge(s_free, s_base + score_uses(i))
                        low = mn2[:, s, :, 0]
                    else:
                        act.wait_ge(mj_ready, l * 8 + (i - 8 + 1))
                        low = mj[:, s, :]
                    for grp in range(1 if i < 8 else 3):
                        for qt, r in ((0, slice(0, P)), (1, slice(P, 384))):
                            ins = act.activation(sn[:, s, grp, r], sn[:, s, grp, r], ACT.Exp, scale=-1.0,
                                                 bias=low[:, qt:qt + 1], accum_out=rs2[:, s, qt, grp:grp + 1])
                    ins.then_inc(p_ready, 1)

                def y_split(idx, ready, src):
                    act.wait_ge(*ready)
                    act.activation(yh[:, idx, 0:T], src, ACT.Copy).then_inc(y_hi, 1)

                def head_block(j):
                    done(j)
                    t, kind = (j - H_A) // 4, (j - H_A) % 4
                    if j < H_A:
                        act.activation(cz[:, j - H_CZ, :], gslot(G_HYB + j), ACT.Tanh, scale=0.5).then_inc(tanh_ready, 1)
                    elif kind == 0:
                        freed(act.activation(at[:, 0, :], gslot(G_HYB + j), ACT.Copy), j)
                    elif kind == 3:
                        act.activation(at[:, 2, :], gslot(G_HYB + j), ACT.Tanh, scale=0.5).then_inc(tanh_ready, 1)
                    next_hi(j)

                for i in range(18):
                    if 1 <= i <= 16:
                        for grp in range(1 if i <= 8 else 3):
                            slot = wait_t()
                            act.activation(pt2[:, grp, :], Tp[:, slot, 0:384], ACT.Copy).then_inc(t_free, 1)
                    for j in TAKEN[i]:
                        head_block(j)
                    if i < 16:
                        exps(i)
                    if i >= 1:
                        for j in TAKEN[i]:
                            if j >= H_A and (j - H_A) % 4 == 3:
                                t = (j - H_A) // 4
                                y_split(t, (a_ready, l * 4 + t + 1), at[:, 3, :])
                    if i >= 3 and i % 2:
                        p = (i - 3) // 2
                        y_split(4 + p, (s_free, s_base + pair_use(p)), hpair[:, :])

                for mm in range(4):
                    for q in range(9):
                        j = H_MERGE + 9 * mm + q
                        done(j)
                        if q % 3 < 2:
                            pair = 2 * (q // 3) + q % 3
                            n = H_MERGE + 12 * mm + 4 * (q // 3) + q % 3
                            col = 8 * (pair % 3) + 2 * mm + pair // 3
                            freed(act.activation(th[:, pair, :], gslot(G_HYB + n), ACT.Tanh, scale=0.5,
                                                 bias=hb[:, col:col + 1]), n)
                        next_hi(j)
                        if q in (6, 8):
                            m = 2 * mm + q // 8
                            act.wait_ge(m_ready, l * 8 + m + 1)
                            act.activation(mh[:, m, 0:T], mg[:, m % 2, :], ACT.Copy, scale=0.5).then_inc(m_hi, 1)
                for j in range(H_WO, HYB_BLOCKS - 4):
                    next_hi(j)
                act.preload_act_table_set(LNEXP)
                assert t_ring.n == HYB_T

        @block.vector
        def _(dve):
            chain = Chain(dve, dve_own)

            def lo(n, r4=0):
                s = n % 4
                dve.wait_ge(w_hi, n + 1 + 4 * r4)
                dve.tensor_tensor(wlo[:, s, :], raw[:, s, :], whi[:, s, :], ALU.subtract).then_inc(w_lo, 1)

            def bc(ap, n, axis=1):
                return ap.unsqueeze(axis).broadcast_to([P, n, ap.shape[-1]])

            def add_bias(v, slot):
                return dve.tensor_tensor(mod[:, 8 * v:8 * v + 8], S[:, slot, 0:8],
                                         cols[:, C_ADAB + 8 * v:C_ADAB + 8 * v + 8], ALU.add)

            def mod_vector(v):
                dve.wait_ge(ada_used, v + 1 if v < 2 else v)
                add_bias(v, 0).then_inc(mod_ready, 1)
                dve.wait_ge(mod_ready, v + 1)

            def mod_gain(v, gain):
                chain.link(dve.scalar_tensor_tensor(out=modA[:, :], in0=mod[:, 8 * v:8 * v + 8], scalar=1.0,
                                                    in1=cols[:, gain:gain + 8], op0=ALU.add, op1=ALU.mult))

            def norm(n_rstd, base_t, base_h, gain, shift, then_lo=()):
                dve.wait_ge(rstd_ready, n_rstd)
                for k in range(KT):
                    dve.scalar_tensor_tensor(out=sq[:, k, :], in0=x[:, k, :], scalar=gain(k), in1=rstd[:, :],
                                             op0=ALU.mult, op1=ALU.mult).then_inc(t_ready, 1)
                for k in range(KT):
                    dve.wait_ge(hi_ready, base_h + k + 1)
                    if shift is None:
                        ins = dve.tensor_tensor(h[:, k, T:2 * T], sq[:, k, :], h[:, k, 0:T], ALU.subtract)
                    else:
                        ins = dve.scalar_tensor_tensor(out=h[:, k, T:2 * T], in0=sq[:, k, :], scalar=shift(k),
                                                       in1=h[:, k, 0:T], op0=ALU.add, op1=ALU.subtract)
                    ins.then_inc(h_ready, 1)
                for n in then_lo:
                    lo(n)

            def col(tile_, c):
                return lambda k: tile_[:, c + k:c + k + 1]

            s_ring = Ring(3)

            def wait_s():
                slot, _, done = s_ring.next()
                dve.wait_ge(s_done, done)
                return slot

            dve.wait_ge(exp_c, 1)
            chain.link(dve.tensor_scalar(silc[:, 8:16], silc[:, 8:16], 1.0, None, ALU.add))
            chain.link(dve.reciprocal(silc[:, 8:16], silc[:, 8:16]))
            dve.tensor_tensor(silc[:, 16:24], silc[:, 8:16], silc[:, 0:8], ALU.mult).then_inc(silu_c, 1)
            dve.wait_ge(silu_c, 1)
            for n in range(16):
                if n in dict(FIRST):
                    dve.wait_ge(ada_first[[n0 for n0, _ in FIRST].index(n)], 16)
                half, w = n // 8, adaw[:, n, :]
                if n % 8 == 0:
                    ins = dve.tensor_scalar(acc[:, half, :], w, silc[:, 16:17], None, ALU.mult)
                else:
                    ins = dve.scalar_tensor_tensor(out=acc[:, half, :], in0=w, scalar=silc[:, 16 + n % 8:17 + n % 8],
                                                   in1=acc[:, half, :], op0=ALU.mult, op1=ALU.add)
                if n % 8 < 7:
                    chain.link(ins)
                else:
                    ins.then_inc(ada_acc, 1)
            dve.wait_ge(in_cols, 16)
            mod_vector(0)
            for n in range(2):
                lo(n)
            mod_vector(1)
            mod_gain(1, C_G0)
            norm(1, 0, 0, col(modA, 0), col(mod, 0))
            for n in range(2, 4):
                lo(n)

            def rope_moba(n):
                A, B = mqk[:, 4 * n:4 * n + 4:2, :], mqk[:, 4 * n + 1:4 * n + 4:2, :]
                RA, RB = mro[:, 4 * n:4 * n + 2, :], mro[:, 4 * n + 2:4 * n + 4, :]
                cos, sin = bc(mcos[:, :], 2), bc(msin[:, :], 2)
                for s in range(4):
                    dve.wait_ge(slot_free[s], 1 + n)
                if n:
                    dve.wait_ge(rope_ready, 1)
                dve.tensor_tensor(RA, A, cos, ALU.mult)
                chain.link(dve.tensor_tensor(rtmp[:, :, :], B, sin, ALU.mult))
                chain.link(dve.tensor_tensor(RA, RA, rtmp[:, :, :], ALU.subtract))
                dve.tensor_tensor(RB, B, cos, ALU.mult)
                chain.link(dve.tensor_tensor(rtmp[:, :, :], A, sin, ALU.mult))
                dve.tensor_tensor(RB, RB, rtmp[:, :, :], ALU.add).then_inc(rope_ready, 1)

            def softplus(g2):
                z4, s4 = zs[:, 4 * g2:4 * g2 + 4, :], sp[:, 4 * g2:4 * g2 + 4, :]
                dve.wait_ge(sb_ln, g2 + 1)
                dve.scalar_tensor_tensor(out=s4, in0=z4, scalar=0.0, in1=s4, op0=ALU.max, op1=ALU.add).then_inc(sb_sp, 1)

            def minus_sums(hh):
                slot = wait_s()
                dve.tensor_tensor(zs[:, hh, :], zs[:, hh, :], S[:, slot, 0:384], ALU.subtract).then_inc(s_free, 1)

            def o_split(p):
                dve.wait_ge(o_hi, p + 1)
                o = (p + 4) % 8
                dve.tensor_tensor(oh[:, o, T:2 * T], att_out(p), oh[:, o, 0:T], ALU.subtract).then_inc(o_free, 1)

            def moba_minima(i):
                slot = wait_s()
                for qt, r in ((0, slice(0, P)), (1, slice(P, 384))):
                    ins = dve.tensor_tensor_reduce(out=pr[:, i % 2, r], in0=S[:, slot, r], in1=cmask[:, r], scale=1.0,
                                                   scalar=3e38, op0=ALU.add, op1=ALU.min,
                                                   accum_out=mn[:, i % 2, qt:qt + 1])
                ins.then_inc(s_free, 1)

            def moba_normalise(i):
                s = i % 2
                dve.wait_ge(p_ready, i + 1)
                chain.link(dve.reciprocal(ri[:, s, :], rs[:, s, :]))
                dve.tensor_scalar(pr[:, s, 0:P], pr[:, s, 0:P], ri[:, s, 0:1], None, ALU.mult)
                dve.tensor_scalar(pr[:, s, P:384], pr[:, s, P:384], ri[:, s, 1:2], None, ALU.mult).then_inc(pn_ready, 1)

            dve.wait_ge(in_att, 64)
            dve.wait_ge(in_const, 48)
            for b in range(25):
                if b == 21:
                    add_bias(2, wait_s()).then_inc(s_free, 1)
                    dve.wait_ge(s_free, ATT_S.index("a") + 1)
                    dve.memset(mark[:, 0:1], 0.0).then_inc(mod_ready, 1)
                if b in (22, 24):
                    for hh in range(2 * b - 44, 2 * b - 40):
                        minus_sums(hh)
                if 12 <= b < 20:
                    moba_minima(b - 12)
                if b in (15, 17, 19, 21):
                    o_split((b - 15) // 2)
                if b >= 1:
                    lo(b + 3)
                if 12 <= b < 20:
                    moba_normalise(b - 12)
                if b in (15, 17, 19, 21):
                    for hh in (b - 15, b - 14):
                        slot = wait_s()
                        dve.tensor_tensor(zs[:, hh, :], S[:, slot, 0:384], sbm[:, :], ALU.add).then_inc(s_free, 1)
                if b in (5, 9):
                    rope_moba(b // 4 - 1)
                if b in (19, 23):
                    softplus(b // 4 - 4)
            for p in range(4, 8):
                o_split(p)

            norms = [0]

            def x_update(b, n_blocks, g, ends, gate, vectors=(), last=False):
                norms[0] += 1

                def add_squares(m):
                    dve.wait_ge(sq_ready, 8 * norms[0] + m + 1)
                    if m > 1:
                        chain.wait()
                    ins = dve.tensor_tensor(sq[:, 0, :], sq[:, 0, :], sq[:, m, :], ALU.add)
                    if m < KT - 2:
                        chain.add(ins)
                    else:
                        ins.then_inc(sq_summed, 1)

                for bb in range(n_blocks):
                    for m in range(8):
                        if ends[m] == bb:
                            if m >= 2:
                                add_squares(m - 1)
                            dve.wait_ge(blk_done, b + bb + 1)
                            dve.scalar_tensor_tensor(out=x[:, m, :], in0=gslot(g + m),
                                                     scalar=mod[:, 8 * gate + m:8 * gate + m + 1], in1=x[:, m, :],
                                                     op0=ALU.mult, op1=ALU.add).then_inc(slot_free[(g + m) % 4], 1)
                            if vectors and m in (5, 6):
                                mod_vector(vectors[m - 5])
                            if vectors and m == 6:
                                mod_gain(vectors[1], C_G0 + 8 * norms[0])
                    if bb < n_blocks - (4 if last else 1):
                        lo(b + bb + 4)

            one_each = list(range(8))
            two_each = [2 * m + 1 for m in range(8)]
            of_down = [-(-FT * (m + 1) // 8) - 1 for m in range(8)]

            x_update(B_ATT_O, 8, G_ATT_O, one_each, 2, (3, 4))

            def ffn(b, g):
                with dve.Fori(0, FT // 2) as i:
                    for q in range(2):
                        gg = g + 2 * q
                        lo(b + 2 * q + 4, i)
                        dve.wait_ge(blk_done, b + 2 * q + 2 + 4 * i)
                        dve.wait_ge(slot_free[gg % 4], taken(gg) + i)
                        dve.tensor_tensor(af[:, q, :], gslot(gg + 1), sg[:, q, :],
                                          ALU.mult).then_inc(slot_free[(gg + 1) % 4], 1)
                        lo(b + 2 * q + 5, i)
                        dve.wait_ge(ah_hi, ah_base[0] + i * 2 + q + 1)
                        dve.tensor_tensor(ah[:, i * 2 + q, T:2 * T], af[:, q, :], ah[:, i * 2 + q, 0:T],
                                          ALU.subtract).then_inc(ah_ready, 1)

            ah_base = [0]
            norm(2, 8, 8, col(modA, 0), col(mod, 24), [B_FFN0 + 3])
            ffn(B_FFN0, G_FFN0)
            mod_vector(5)
            x_update(B_DOWN0, FT, G_DOWN0, of_down, 5, (6, 7))

            norm(3, 16, 16, col(modA, 0), col(mod, 48), [B_RET + 3])

            def rope_ret(n):
                A, B = rqk[:, 8 * n:8 * n + 8:2, :], rqk[:, 8 * n + 1:8 * n + 8:2, :]
                cos, sin = bc(rcos[:, :], 4), bc(rsin[:, :], 4)
                for g in range(G_RET + 8 * n + 4, G_RET + 8 * n + 8):
                    dve.wait_ge(slot_free[g % 4], taken(g))
                dve.tensor_tensor(sq[:, 0:4, :], A, sin, ALU.mult)
                chain.link(dve.tensor_tensor(sq[:, 4:8, :], B, sin, ALU.mult))
                dve.tensor_tensor(A, A, cos, ALU.mult)
                chain.link(dve.tensor_tensor(B, B, cos, ALU.mult))
                dve.tensor_tensor(A, A, sq[:, 4:8, :], ALU.subtract)
                dve.tensor_tensor(B, B, sq[:, 0:4, :], ALU.add).then_inc(rope_ready, 1)
                dve.wait_ge(rope_ready, 3 + n)

            def ret_part(hh, part):
                if part == 0:
                    dve.wait_ge(r_sc, hh + 1)
                    dve.tensor_tensor(rp[:, hh % 2, 0:T], S[:, 0, 0:T], dec[:, hh, :], ALU.mult)
                    dve.tensor_tensor(rp[:, hh % 2, T:384], S[:, 0, T:384], dec[:, hh, 0:P], ALU.mult).then_inc(r_pt, 1)
                elif part == 2:
                    dve.wait_ge(t_free, 32 + 2 * hh + 1)
                    dve.tensor_tensor(sq[:, 0:4, :], sq[:, 0:4, :], bc(rmu[:, :], 4), ALU.subtract).then_inc(r_c, 1)
                elif part == 3:
                    dve.wait_ge(r_norm, hh + 1)
                    for m in range(4):
                        c = C_RETGN + 4 * hh + m
                        ins = dve.scalar_tensor_tensor(out=sq[:, m, :], in0=sq[:, m, :], scalar=cols[:, c:c + 1],
                                                       in1=rstd[:, :], op0=ALU.mult, op1=ALU.mult)
                    chain.link(ins)
                    dve.tensor_tensor(sq[:, 0:4, :], sq[:, 0:4, :], rg[:, 4 * hh:4 * hh + 4, :], ALU.mult).then_inc(r_y, 1)
                    dve.wait_ge(r_hi, hh + 1)
                    dve.tensor_tensor(yr[:, 4 * hh:4 * hh + 4, T:2 * T], sq[:, 0:4, :], yr[:, 4 * hh:4 * hh + 4, 0:T],
                                      ALU.subtract).then_inc(r_lo, 1)

            dve.wait_ge(in_ret, 48)
            for b in range(48):
                lo(B_RET + b + 4)
                if b == 24:
                    mod_vector(8)
                if b in (8, 16):
                    rope_ret(b // 8 - 1)
                for hh, part in RET_PARTS.get(b, ()):
                    ret_part(hh, part)
            ret_part(3, 3)
            x_update(B_RET_O, 16, G_RET_O, two_each, 8, (9, 10))
            ah_base[0] = FT
            norm(4, 24, 24, col(modA, 0), col(mod, 72), [B_FFN1 + 3])
            ffn(B_FFN1, G_FFN1)
            mod_vector(11)
            x_update(B_DOWN1, FT, G_DOWN1, of_down, 11, last=True)
            dve.wait_ge(rstd_ready, 5)
            for k in range(KT):
                dve.scalar_tensor_tensor(out=x[:, k, :], in0=x[:, k, :], scalar=cols[:, C_FINAL + k:C_FINAL + k + 1],
                                         in1=rstd[:, :], op0=ALU.mult, op1=ALU.mult).then_inc(t_ready, 1)

            chain.link(dve.memset(ua[:, 0:2], 0.0))
            with dve.Fori(0, LAYERS2) as l:
                chain.restart()
                b4, g4 = l * (HYB_BLOCKS // 4), l * (HYB_TILES // 4)
                s_ring = Ring(3, L1_S + l * HYB_S)

                def next_lo(j):
                    if j + 4 < HYB_BLOCKS:
                        lo(B_HYB + j + 4, b4)

                def done(j):
                    dve.wait_ge(blk_done, B_HYB + j + 1 + 4 * b4)

                def freed(ins, n):
                    ins.then_inc(slot_free[(G_HYB + n) % 4], 1)

                def wait_s():
                    slot, _, d_ = s_ring.next()
                    dve.wait_ge(s_done, d_)
                    return slot

                dve.tensor_copy(lcol[:, :], cols[:, C_HYB:].rearrange("p (l c) -> p l c", l=LAYERS2)[:, l, :])\
                   .then_inc(lcol_ready, 1)
                dve.wait_ge(lcol_ready, l * 3 + 1)
                dve.tensor_scalar(hb[:, :], lcol[:, L_BGATE:L_BGATE + 24], 0.5, None, ALU.mult).then_inc(lcol_ready, 1)
                dve.tensor_scalar(nq[:, :], lcol[:, L_DQ:L_DQ + 3], -HD ** -0.5, None, ALU.mult).then_inc(lcol_ready, 1)
                dve.wait_ge(lcol_ready, l * 3 + 3)
                for j in (0, 1):
                    lo(B_HYB + j, b4)
                norm(l + 6, 40 + l * 8, 32 + l * 8, col(lcol, L_NORM), None)
                for j in (2, 3):
                    lo(B_HYB + j, b4)

                for j in range(4):
                    next_lo(j)
                dve.wait_ge(c_ready, l * 2 + 2)
                for k in range(3):
                    ins = dve.scalar_tensor_tensor(out=cF[:, k, :], in0=cF[:, k, :], scalar=lcol[:, L_QA + k:L_QA + k + 1],
                                                   in1=cr[:, k // 2, :], op0=ALU.mult, op1=ALU.mult)
                ins.then_inc(cn_ready, 1)
                for j in range(4, 8):
                    dve.wait_ge(tanh_ready, l * 12 + (j - 3))
                    freed(dve.scalar_tensor_tensor(out=bz[:, j - 4, :], in0=bz[:, j - 4, :], scalar=1.0,
                                                   in1=gslot(G_HYB + j), op0=ALU.add, op1=ALU.mult), j)
                    next_lo(j)

                def mla_in():
                    for tt in range(2):
                        for half in range(2):
                            slot = wait_s()
                            dve.tensor_copy(qk[:, 0, tt, 384 * half:384 * half + 384], S[:, slot, 0:384])\
                               .then_inc(s_free, 1)
                    for tt in range(2):
                        slot = wait_s()
                        dve.tensor_copy(qk[:, 1, tt, :].rearrange("p (h c) -> p h c", c=96)[:, :, 0:64],
                                        S[:, slot, :].rearrange("p (h c) -> p h c", c=64)).then_inc(s_free, 1)
                    for tt in range(2):
                        slot = wait_s()
                        dve.tensor_copy(vm[:, tt, :], S[:, slot, :]).then_inc(s_free, 1)
                    dve.wait_ge(t_free, L1_T + l * HYB_T + 3)
                    for tt in range(2):
                        ins = dve.tensor_copy(qk[:, 1, tt, :].rearrange("p (h c) -> p h c", c=96)[:, :, 64:96],
                                              bc(kpe[:, tt, :], 8))
                    ins.then_inc(qk_in, 1)

                qk_rows = qk[:, :, :, :].rearrange("p n t (h c) -> p (n t h) c", c=96)
                s_rows = qks[:, :, :, :].rearrange("p n t (h c) -> p (n t h) c", c=96)

                def mla_sums():
                    dve.wait_ge(qk_sq, l + 1)
                    dve.tensor_reduce(out=s32[:, :], in_=s_rows, op=ALU.add, axis=AX).then_inc(qk_ss, 1)

                def mla_scale():
                    dve.wait_ge(qk_rs, l + 1)
                    chain.link(dve.tensor_scalar(s32[:, 0:16], s32[:, 0:16], -96.0 ** -0.5, None, ALU.mult))
                    chain.link(dve.tensor_tensor(qk_rows, qk_rows, s32[:, :].unsqueeze(2).broadcast_to([P, 32, 96]),
                                                 ALU.mult))

                def mla_gain():
                    for n in range(2):
                        v = qk[:, n, :, :].rearrange("p t (h c) -> p (t h) c", c=96)
                        ins = dve.tensor_tensor(v, v, rows[:, l, n, :].unsqueeze(1).broadcast_to([P, 16, 96]), ALU.mult)
                    chain.link(ins)

                def mla_rope(n):
                    v = qk[:, n, :, :].rearrange("p t (h c) -> p t h c", c=96)
                    x1, x2 = v[:, :, :, 64:80], v[:, :, :, 80:96]
                    w = qks[:, n, :, :].rearrange("p t (h c) -> p t h c", c=96)
                    t1, t2 = w[:, :, :, 0:16], w[:, :, :, 16:32]
                    cos = lcs[:, 0, :, :].unsqueeze(2).broadcast_to([P, 2, 8, 16])
                    sin = lcs[:, 1, :, :].unsqueeze(2).broadcast_to([P, 2, 8, 16])
                    dve.tensor_tensor(t1, x1, sin, ALU.mult)
                    chain.link(dve.tensor_tensor(t2, x2, sin, ALU.mult))
                    dve.tensor_tensor(x1, x1, cos, ALU.mult)
                    chain.link(dve.tensor_tensor(x2, x2, cos, ALU.mult))
                    dve.tensor_tensor(x1, x1, t2, ALU.subtract)
                    ins = dve.tensor_tensor(x2, x2, t1, ALU.add)
                    if n:
                        ins.then_inc(qk_ready, 1)
                    else:
                        chain.link(ins)

                def d_norm_tile(j):
                    dve.wait_ge(d_rs, l * 24 + j + 1)
                    grp = (j % 12) // 4
                    gain = nq[:, grp:grp + 1] if j < 12 else lcol[:, L_DK + grp:L_DK + grp + 1]
                    dve.scalar_tensor_tensor(out=dqk[:, j, :], in0=dqk[:, j, :], scalar=gain, in1=at[:, j % 2, :],
                                             op0=ALU.mult, op1=ALU.mult).then_inc(d_norm, 1)

                for j in range(24):
                    next_lo(H_DQ + j)
                    if j >= 2:
                        d_norm_tile(j - 2)
                    if j == 2:
                        mla_in()
                    if j == 5:
                        mla_sums()
                    if j == 8:
                        mla_scale()
                    if j == 10:
                        dve.wait_ge(in_hyb, 64)
                        mla_gain()
                    if j in (12, 14):
                        mla_rope(j // 2 - 6)
                for j in range(12):
                    if j < 2:
                        d_norm_tile(22 + j)
                    next_lo(H_DV + j)

                def minima(i):
                    s = i % 2
                    for grp in range(1 if i < 8 else 3):
                        slot = wait_s()
                        if i >= 8:
                            j = 3 * (i - 8) + grp
                            dve.wait_ge(bias_ready, l * 24 + j + 1)
                            add = bias[:, j % 2, :]
                        else:
                            add = cmask[:, :]
                        dve.memset(mark[:, s_ring.n - 1:s_ring.n], 0.0)
                        for qt, r in ((0, slice(0, P)), (1, slice(P, 384))):
                            ins = dve.tensor_tensor_reduce(out=sn[:, s, grp, r], in0=S[:, slot, r], in1=add[:, r], scale=1.0,
                                                           scalar=3e38, op0=ALU.add, op1=ALU.min,
                                                           accum_out=mn2[:, s, qt, grp:grp + 1])
                        ins.then_inc(s_free, 1)
                    if i >= 8:
                        dve.wait_ge(s_free, L1_S + l * HYB_S + s_ring.n)
                        dve.tensor_reduce(out=mj[:, s, :], in_=mn2[:, s, :, :], op=ALU.min, axis=AX).then_inc(mj_ready, 1)

                def over_sums(i):
                    dve.wait_ge(p_ready, 8 + l * 16 + i + 1)
                    total = rs2[:, i % 2, :, 0]
                    if i >= 8:
                        chain.link(dve.tensor_reduce(out=rj[:, i % 4, :], in_=rs2[:, i % 2, :, :], op=ALU.add, axis=AX))
                        total = rj[:, i % 4, :]
                    chain.add(dve.reciprocal(rj[:, i % 4, :], total))

                y_n = [0]

                def y_split(idx, src):
                    y_n[0] += 1
                    dve.wait_ge(y_hi, l * 12 + y_n[0])
                    dve.tensor_tensor(yh[:, idx, T:2 * T], src, yh[:, idx, 0:T], ALU.subtract).then_inc(y_lo, 1)

                def head_block(j):
                    n = G_HYB + j
                    if j < H_A:
                        dve.wait_ge(tanh_ready, l * 12 + (4 + j - H_CZ + 1))
                        freed(dve.scalar_tensor_tensor(out=cz[:, j - H_CZ, :], in0=cz[:, j - H_CZ, :], scalar=1.0,
                                                       in1=gslot(n), op0=ALU.add, op1=ALU.mult), j)
                        next_lo(j)
                        return
                    t, kind = (j - H_A) // 4, (j - H_A) % 4
                    if kind == 1:
                        done(j)
                        dve.wait_ge(slot_free[(n - 1) % 4], taken(n - 1) + g4)
                        freed(dve.tensor_tensor(ua[:, 2:2 + T], gslot(n), at[:, 0, :], ALU.mult), j)
                        dve.wait_ge(slot_free[n % 4], taken(n) + g4)
                        w = [lcol[:, L_CONVW + 4 * tap + t:L_CONVW + 4 * tap + t + 1] for tap in range(3)]
                        chain.link(dve.tensor_scalar(at[:, 1, :], ua[:, 0:T], w[0], lcol[:, L_CONVB + t:L_CONVB + t + 1],
                                                     ALU.mult, ALU.add))
                        for tap in (1, 2):
                            chain.link(dve.scalar_tensor_tensor(out=at[:, 1, :], in0=ua[:, tap:tap + T], scalar=w[tap],
                                                                in1=at[:, 1, :], op0=ALU.mult, op1=ALU.add))
                    if kind == 2:
                        done(j)
                        freed(dve.tensor_tensor(at[:, 1, :], gslot(n), at[:, 1, :], ALU.mult), j)
                    if kind == 3:
                        dve.wait_ge(tanh_ready, l * 12 + (8 + t + 1))
                        freed(dve.scalar_tensor_tensor(out=at[:, 2, :], in0=at[:, 2, :], scalar=1.0, in1=gslot(n),
                                                       op0=ALU.add, op1=ALU.mult), j)
                        dve.wait_ge(slot_free[n % 4], taken(n) + g4)
                        dve.scalar_tensor_tensor(out=at[:, 3, :], in0=at[:, 1, :], scalar=0.5, in1=at[:, 2, :],
                                                 op0=ALU.mult, op1=ALU.mult).then_inc(a_ready, 1)
                    next_lo(j)

                def pair_out(p):
                    dve.wait_ge(o_done, L1_O + l * 8 + p + 1)
                    s = 2 * (p % 2)
                    chain.wait()
                    dve.tensor_tensor(at[:, 4, :].rearrange("p (q e d) -> p e q d", q=2, e=2),
                                      O[:, 0:T].rearrange("p (e q d) -> p e q d", e=2, q=2),
                                      rj[:, s:s + 2, :].unsqueeze(3).broadcast_to([P, 2, 2, HD]),
                                      ALU.mult).then_inc(o_free, 1)

                def pair_gate(p):
                    z = bz[:, p, :] if p < 4 else cz[:, p - 4, :]
                    slot = wait_s()
                    dve.scalar_tensor_tensor(out=hpair[:, :], in0=S[:, slot, 0:T], scalar=0.5, in1=z, op0=ALU.mult,
                                             op1=ALU.mult).then_inc(s_free, 1)

                for i in range(18):
                    if i >= 3 and i % 2 and i < 17:
                        pair_out((i - 3) // 2)
                    if i < 16:
                        minima(i)
                    for j in TAKEN[i]:
                        head_block(j)
                    if i == 17:
                        pair_out(7)
                    if i < 16:
                        over_sums(i)
                    if i >= 3 and i % 2:
                        pair_gate((i - 3) // 2)
                    if i >= 1:
                        for j in TAKEN[i]:
                            if j >= H_A and (j - H_A) % 4 == 3:
                                y_split((j - H_A) // 4, at[:, 3, :])
                    if i >= 3 and i % 2:
                        y_split(4 + (i - 3) // 2, hpair[:, :])

                for mm in range(4):
                    for q in range(6):
                        r = q // 2
                        bb = H_MERGE + 9 * mm + 3 * r
                        gate = G_HYB + H_MERGE + 12 * mm + 4 * r + q % 2
                        n = gate + 2
                        m = 2 * mm + q // 3
                        next_lo(bb + q % 2)
                        if q % 2:
                            done(bb + 2)
                        else:
                            dve.wait_ge(half_done, l * 12 + 3 * mm + r + 1)
                        dve.wait_ge(slot_free[gate % 4], taken(gate) + g4)
                        if q % 3 == 0:
                            freed(dve.scalar_tensor_tensor(out=mg[:, m % 2, :], in0=th[:, q, :], scalar=1.0, in1=gslot(n),
                                                           op0=ALU.add, op1=ALU.mult), n - G_HYB)
                        else:
                            freed(dve.scalar_tensor_tensor(out=th[:, q, :], in0=th[:, q, :], scalar=1.0, in1=gslot(n),
                                                           op0=ALU.add, op1=ALU.mult), n - G_HYB)
                            dve.wait_ge(slot_free[n % 4], taken(n) + g4)
                            ins = dve.tensor_tensor(mg[:, m % 2, :], mg[:, m % 2, :], th[:, q, :], ALU.add)
                            if q % 3 == 1:
                                chain.link(ins)
                            else:
                                ins.then_inc(m_ready, 1)
                        if q % 2:
                            next_lo(bb + 2)
                        if q in (3, 5):
                            m = 2 * mm + q // 4
                            dve.wait_ge(m_hi, l * 8 + m + 1)
                            dve.scalar_tensor_tensor(out=mh[:, m, T:2 * T], in0=mg[:, m % 2, :], scalar=0.5,
                                                     in1=mh[:, m, 0:T], op0=ALU.mult, op1=ALU.subtract).then_inc(m_lo, 1)
                for m in range(8):
                    done(H_WO + m)
                    n = H_MERGE + 48 + m
                    freed(dve.tensor_tensor(x[:, m, :], gslot(G_HYB + n), x[:, m, :], ALU.add), n)
                    next_lo(H_WO + m)
                assert s_ring.n == HYB_S


def tables():
    f = np.float32
    r = np.arange(P)
    qpos = np.concatenate([np.zeros(P, int), np.full(T, P)])
    kpos = np.concatenate([np.arange(P), np.arange(T)])
    dist = (qpos[None, :] + r[:, None]) - kpos[None, :]
    t = {"ident": np.eye(P, dtype=f), "ones": np.ones((P, P), f)}
    t["cmask"] = np.where(dist >= 0, 0, MASKED).astype(f)
    t["usum"] = (r[:, None] >= r[None, :]).astype(f)
    q2 = np.concatenate([np.arange(T), np.arange(P, T)])
    k2 = np.concatenate([np.zeros(T, int), np.full(P, P)])
    t["sbm"] = np.where(k2[None, :] + r[:, None] < q2[None, :], 0, -MASKED).astype(f)
    t["dist"] = np.stack([np.where((dist >= 0) & (dist % d == 0) & (dist // d <= back), dist, MASKED)
                          for d, back in zip(DIL, N_BACK)], axis=1).astype(f)
    t["slopes"] = np.tile(np.array(SLOPES, f)[None, :], (P, 1))
    t["bones"] = np.kron(np.eye(2), np.ones((64, 64))).astype(f)

    def angles(d):
        inv = f(10000.0) ** (-np.arange(0, d, 2, dtype=f) / f(d))
        return (np.arange(T, dtype=f)[:, None] * inv[None, :]).astype(f)

    m = angles(64)
    t["mcos"], t["msin"] = (np.tile(g(m).T, (4, 1)).astype(f) for g in (np.cos, np.sin))
    m = angles(256)
    t["rcos"], t["rsin"] = (np.ascontiguousarray(g(m).T).astype(f) for g in (np.cos, np.sin))
    m = angles(32).reshape(2, P, 16)
    t["lcs"] = np.ascontiguousarray(np.stack([np.cos(m), np.sin(m)]).transpose(2, 0, 1, 3)).astype(f)
    log_g = np.log(1.0 - 2.0 ** (-5.0 - np.arange(4, dtype=np.float64)))
    diff = np.arange(T)[None, :] - r[:, None]
    t["dec"] = np.ascontiguousarray(np.where(diff[None] >= 0, np.exp(log_g[:, None, None] * np.maximum(diff, 0)[None]), 0)
                                    .transpose(1, 0, 2)).astype(f)
    return t


def blocks(w, cols=None, tiles=None):
    if cols is not None:
        w = w[:, cols]
    k, n = w.shape
    v = w.reshape(k // P, P, n // P, P).transpose(2, 0, 1, 3)
    return v if tiles else v.reshape(-1, 8, P, P)


def columns(v):
    return np.ascontiguousarray(np.asarray(v).reshape(-1, P).T)


def lay_out(i):
    halves = lambda base: np.concatenate([base + 64 * hh + 32 * half + np.arange(32)
                                          for g in range(2) for half in range(2) for hh in range(4 * g, 4 * g + 4)])
    s, m = np.arange(512), 512
    pairs = np.stack([s.reshape(4, P), 1024 + s.reshape(4, P)], axis=1).reshape(-1)
    qkv_cols = np.concatenate([halves(m), halves(1024 + m), 2048 + m + s, pairs, 2048 + s])
    parts = [blocks(i["att_w_qkv"][0], qkv_cols), blocks(i["att_w_o"][0])]

    def gate_up(w):
        v = w.reshape(D, 2, FT, P).transpose(0, 2, 1, 3).reshape(D, 2 * D_FF)
        return blocks(v)

    parts += [gate_up(i["ffn_w_gate_up"][0]), blocks(i["ffn_w_down"][0])]
    parts += [blocks(i["ret_w_in"][0]), blocks(i["ret_w_o"][0])]
    parts += [gate_up(i["ffn_w_gate_up"][1]), blocks(i["ffn_w_down"][1])]
    for l in range(LAYERS2):
        w = i["w_in_2"][l]
        at = np.cumsum([0] + [512] * 4 + [256, 128, 32, 512] + [1536] * 3 + [512, 3072])
        a_b, a_c, a_x, a_z, c_q, c_kv, k_pe, b_z, dq, dk, dv, c_z, gate = (w[:, p:q] for p, q in zip(at[:-1], at[1:]))
        parts += [blocks(c_q), blocks(c_kv), blocks(np.pad(k_pe, ((0, 0), (0, 96))))]
        parts += [blocks(v) for v in (b_z, dq, dk, dv, c_z)]
        conv = np.stack([v.reshape(D, 4, P) for v in (a_c, a_x, a_b, a_z)], axis=2).reshape(D, 2048)
        parts += [blocks(conv)]
        g = blocks(gate, tiles=True).reshape(3, 8, 8, P, P)
        o = np.stack([blocks(i[f"w_out_{b}_2"][l], tiles=True) for b in "abc"])
        for mm in range(4):
            for r in range(3):
                pairs = [(q % 3, 2 * mm + q // 3) for q in (2 * r, 2 * r + 1)]
                parts += [np.stack([g[b, m] for b, m in pairs]),
                          np.concatenate([o[b, m] for b, m in pairs])[None]]
        parts += [blocks(i["w_o_2"][l])]
    w = np.concatenate(parts).transpose(0, 2, 1, 3).reshape(-1, P, 1024)
    assert w.shape[0] == N_BLOCKS, w.shape
    ada = i["ada_w"].reshape(2, 8, P, 6, D).transpose(0, 3, 1, 2, 4).reshape(96, P, D)
    cols = [columns(i["norm_gains"]), columns(i["final_norm"]), columns(i["ret_gn"]), columns(i["ada_b"])]
    for l in range(LAYERS2):
        cols += [columns(i["norm_g_2"][l]), columns(i["b_gate_2"][l]), columns(i["conv_w_2"][l]),
                 columns(i["conv_b_2"][l]), columns(i["q_a_norm_g_2"][l]), columns(i["kv_a_norm_g_2"][l]),
                 columns(np.tile(i["dil_q_norm_g_2"][l], (1, 2))), columns(np.tile(i["dil_k_norm_g_2"][l], (1, 2)))]
    rows = np.stack([i["mla_q_norm_g_2"], i["mla_k_norm_g_2"]], axis=1)
    kv = i["w_ukv_2"].reshape(LAYERS2, P, 8, 2, 64).transpose(0, 1, 3, 2, 4).reshape(LAYERS2, P, 1024)
    return {
        "w": w, "ada": ada, "cols": np.concatenate(cols, axis=1), "c": columns(i["c"]),
        "x": i["x"][0].T.reshape(KT, P, T).transpose(1, 0, 2),
        "rows": np.broadcast_to(rows[None], (P, LAYERS2, 2, 96)),
        "uq": i["w_uq_2"].reshape(LAYERS2, 2, P, 768).transpose(0, 2, 1, 3), "ukv": kv,
    }


def kernel(**inputs):
    import concourse.bacc as bacc
    from concourse.bass_utils import run_bass_kernel_spmd

    arrays = lay_out({k: np.asarray(v) for k, v in inputs.items()})
    arrays.update(tables())
    arrays = {f"in_{k}": np.ascontiguousarray(v) for k, v in arrays.items()}
    nc = bacc.Bacc("TRN2", target_bir_lowering=False, num_devices=1)
    aps = {k[3:]: nc.dram_tensor(k, v.shape, mybir.dt.from_np(v.dtype), kind="ExternalInput").ap()
           for k, v in arrays.items()}
    out = nc.dram_tensor("out", (P, KT, T), mybir.dt.float32, kind="ExternalOutput").ap()
    build(nc, aps, out)
    r = run_bass_kernel_spmd(nc, [arrays], core_ids=[0])
    got = np.asarray(r.results[0]["out"])
    return np.ascontiguousarray(got.transpose(1, 0, 2).reshape(D, T).T)[None]
```
